# Optimizing a Trainium2 kernel written in Bass

```python
import math
import jax, jax.numpy as jnp
from jax import lax
import numpy as np

D_MODEL = 1024
BATCH = 1
SEQ = 256
DEPTH = 2

f32 = jnp.float32

N_A_LAYERS = DEPTH // 2
N_B_LAYERS = DEPTH - N_A_LAYERS
ALPHA = (2.0 * DEPTH) ** 0.25
BETA = (8.0 * DEPTH) ** -0.25
LN_EPS = 1e-5

DN_HEADS = 8
DN_HEAD_DIM = 128
DN_WIDTH = DN_HEADS * DN_HEAD_DIM
CONV_K = 4
DN_CHUNK = 64

ATTN_GROUPS = ((128, 1), (512, 4), (2048, 16))
N_GROUPS = len(ATTN_GROUPS)
B_HEADS = 8
B_HEAD_DIM = 128
B_WIDTH = B_HEADS * B_HEAD_DIM
ATTN_BLOCK = 128
ROT_DIM = B_HEAD_DIM // 4
ROPE_THETA = 500000.0

PEER_HEADS = 8
PEER_NKEYS = 128
PEER_EXPERTS = PEER_NKEYS * PEER_NKEYS
PEER_TOPK = 16
PEER_QDIM = 256
PEER_TOK_BLOCK = 128

kernel_name = 'yoco_deltanet_dilated_peer'

def layer_norm(x, g, b):
    xf = x.astype(f32)
    mu = jnp.mean(xf, -1, keepdims=True)
    var = jnp.mean(jnp.square(xf - mu), -1, keepdims=True)
    return ((xf - mu) * lax.rsqrt(var + LN_EPS) * g.astype(f32) + b.astype(f32)).astype(x.dtype)

def l2norm(t):
    return t * lax.rsqrt(jnp.sum(t * t, -1, keepdims=True) + 1e-6)

def causal_short_conv(x, w):
    s = x.shape[1]
    xp = jnp.pad(x, ((0, 0), (CONV_K - 1, 0), (0, 0)))
    y = xp[:, 0:s] * w[0]
    for j in range(1, CONV_K):
        y = y + xp[:, j:j + s] * w[j]
    return y

def gated_delta_rule(q, k, v, g, beta):
    b, s, h, dk = q.shape
    dv = v.shape[-1]
    n = s // DN_CHUNK

    def chunked(t):
        return jnp.moveaxis(t.reshape(b, n, DN_CHUNK, h, -1), 3, 1)

    q = chunked(q) * (dk ** -0.5)
    k = chunked(k)
    v = chunked(v)
    g = jnp.cumsum(jnp.moveaxis(g.reshape(b, n, DN_CHUNK, h), 3, 1), axis=-1)
    beta = jnp.moveaxis(beta.reshape(b, n, DN_CHUNK, h), 3, 1)
    idx = jnp.arange(DN_CHUNK)
    causal = idx[:, None] >= idx[None, :]
    strict = idx[:, None] > idx[None, :]
    decay = jnp.exp(jnp.where(causal, g[..., :, None] - g[..., None, :], -jnp.inf))
    k_beta = k * beta[..., None]
    m = jnp.where(strict, jnp.einsum('bhnid,bhnjd->bhnij', k_beta, k) * decay, 0.0)
    tri = m + jnp.eye(DN_CHUNK, dtype=m.dtype)
    rhs = jnp.concatenate([v * beta[..., None], k_beta * jnp.exp(g)[..., None]], axis=-1)
    sol = lax.linalg.triangular_solve(tri, rhs, left_side=True, lower=True, unit_diagonal=True)
    u, w = sol[..., :dv], sol[..., dv:]
    a_qk = jnp.einsum('bhnid,bhnjd->bhnij', q, k) * decay

    def step(state, xs):
        q_c, k_c, u_c, w_c, g_c, a_c = xs
        v_new = u_c - jnp.einsum('bhck,bhkv->bhcv', w_c, state)
        o_c = (jnp.einsum('bhck,bhkv->bhcv', q_c * jnp.exp(g_c)[..., None], state)
               + jnp.einsum('bhij,bhjv->bhiv', a_c, v_new))
        g_last = g_c[..., -1]
        state = (state * jnp.exp(g_last)[..., None, None]
                 + jnp.einsum('bhck,bhcv->bhkv', k_c * jnp.exp(g_last[..., None] - g_c)[..., None], v_new))
        return state, o_c

    xs = tuple(jnp.moveaxis(t, 2, 0) for t in (q, k, u, w, g, a_qk))
    s0 = jnp.zeros((b, h, dk, dv), f32)
    _, o = lax.scan(step, s0, xs)
    return jnp.transpose(o, (1, 0, 3, 2, 4)).reshape(b, s, h, dv)

def deltanet_mixer(x, w_in, conv_w, a_log, dt_bias, norm_w, w_out):
    b, s, _ = x.shape
    proj = x @ w_in
    qkv = jax.nn.silu(causal_short_conv(proj[..., :3 * DN_WIDTH], conv_w))
    z = proj[..., 3 * DN_WIDTH:4 * DN_WIDTH].reshape(b, s, DN_HEADS, DN_HEAD_DIM).astype(f32)
    a = proj[..., 4 * DN_WIDTH:4 * DN_WIDTH + DN_HEADS].astype(f32)
    bl = proj[..., 4 * DN_WIDTH + DN_HEADS:].astype(f32)
    q, k, v = (qkv[..., i * DN_WIDTH:(i + 1) * DN_WIDTH].reshape(b, s, DN_HEADS, DN_HEAD_DIM).astype(f32)
               for i in range(3))
    q = l2norm(q)
    k = l2norm(k)
    beta = jax.nn.sigmoid(bl)
    g = -jnp.exp(a_log.astype(f32)) * jax.nn.softplus(a + dt_bias.astype(f32))
    o = gated_delta_rule(q, k, v, g, beta)
    o = o * lax.rsqrt(jnp.mean(o * o, -1, keepdims=True) + 1e-6) * norm_w.astype(f32)
    o = o * jax.nn.silu(z)
    return o.reshape(b, s, DN_WIDTH).astype(x.dtype) @ w_out

def rope_tables(s):
    half = ROT_DIM // 2
    inv_freq = ROPE_THETA ** (-jnp.arange(half, dtype=f32) * 2.0 / ROT_DIM)
    ang = jnp.arange(s, dtype=f32)[:, None] * inv_freq[None, :]
    return jnp.cos(ang), jnp.sin(ang)

def partial_rope(t, cos, sin):
    half = ROT_DIM // 2
    c = cos[:, None, None, :]
    sn = sin[:, None, None, :]
    tf = t.astype(f32)
    x1 = tf[..., :half]
    x2 = tf[..., half:ROT_DIM]
    out = jnp.concatenate([x1 * c - x2 * sn, x2 * c + x1 * sn, tf[..., ROT_DIM:]], axis=-1)
    return out.astype(t.dtype)

def dilated_window_attention(q, k, v, dilation, window):
    b, s, h, dh = q.shape
    steps = window // dilation
    n = s // dilation
    nb = -(-n // ATTN_BLOCK)
    pad = nb * ATTN_BLOCK - n

    def to_sub(t):
        return jnp.transpose(t.reshape(b, n, dilation, h, dh), (0, 2, 1, 3, 4)).reshape(b * dilation, n, h, dh)

    qs = jnp.pad(to_sub(q), ((0, 0), (0, pad), (0, 0), (0, 0))).reshape(b * dilation, nb, ATTN_BLOCK, h, dh)

    def kv_blocks(t):
        tp = jnp.pad(to_sub(t), ((0, 0), (ATTN_BLOCK, pad), (0, 0), (0, 0)))
        tp = tp.reshape(b * dilation, nb + 1, ATTN_BLOCK, h, dh)
        return jnp.concatenate([tp[:, :-1], tp[:, 1:]], axis=2)

    kw = kv_blocks(k)
    vw = kv_blocks(v)
    sc = jnp.einsum('znqhd,znkhd->znhqk', qs, kw, preferred_element_type=f32) * (dh ** -0.5)
    qi = jnp.arange(ATTN_BLOCK)[:, None]
    kj = jnp.arange(2 * ATTN_BLOCK)[None, :]
    dist = qi + ATTN_BLOCK - kj
    key_pos = jnp.arange(nb)[:, None, None] * ATTN_BLOCK + kj[None] - ATTN_BLOCK
    mask = (dist >= 0)[None] & (dist <= steps)[None] & (key_pos >= 0)
    sc = jnp.where(mask[None, :, None], sc, -jnp.inf)
    mx = jnp.max(sc, -1, keepdims=True)
    p = jnp.exp(sc - mx)
    den = jnp.sum(p, -1)
    o = jnp.einsum('znhqk,znkhd->znqhd', p, vw.astype(f32)) / jnp.moveaxis(den, 2, 3)[..., None]
    lse = jnp.moveaxis(mx[..., 0] + jnp.log(den), 2, 3)

    def from_sub(t):
        t = t.reshape(b, dilation, nb * ATTN_BLOCK, *t.shape[3:])[:, :, :n]
        return jnp.swapaxes(t, 1, 2).reshape(b, s, *t.shape[3:])

    return from_sub(o), from_sub(lse)

def dilated_mixer(x, w_q, k_sh, v_sh, w_out, cos, sin):
    b, s, _ = x.shape
    q = partial_rope((x @ w_q).reshape(b, s, N_GROUPS, B_HEADS, B_HEAD_DIM), cos, sin)
    outs, lses = [], []
    for gi, (window, dilation) in enumerate(ATTN_GROUPS):
        o, l = dilated_window_attention(q[:, :, gi], k_sh[:, :, gi], v_sh[:, :, gi], dilation, window)
        outs.append(o)
        lses.append(l)
    wts = jax.nn.softmax(jnp.stack(lses, 0), axis=0)
    o = jnp.sum(wts[..., None] * jnp.stack(outs, 0), axis=0)
    return o.reshape(b, s, B_WIDTH).astype(x.dtype) @ w_out

def peer_ffn(x, w_query, sub_keys, u_tab, v_tab):
    b, s, d = x.shape
    t_blk = PEER_TOK_BLOCK
    xt = x.reshape(b * s // t_blk, t_blk, d)

    def block(xb):
        qh = (xb @ w_query).reshape(t_blk, PEER_HEADS, 2, PEER_QDIM // 2)
        sc = jnp.einsum('thcd,hckd->thck', qh, sub_keys, preferred_element_type=f32)
        top_s, top_i = lax.top_k(sc, PEER_TOPK)
        cand_s = (top_s[:, :, 0, :, None] + top_s[:, :, 1, None, :]).reshape(t_blk, PEER_HEADS, PEER_TOPK * PEER_TOPK)
        cand_i = (top_i[:, :, 0, :, None] * PEER_NKEYS + top_i[:, :, 1, None, :]).reshape(t_blk, PEER_HEADS, PEER_TOPK * PEER_TOPK)
        best_s, pos = lax.top_k(cand_s, PEER_TOPK)
        idx = jnp.take_along_axis(cand_i, pos, axis=-1)
        gate = jax.nn.softmax(best_s, axis=-1)
        u = jnp.take(u_tab, idx, axis=0)
        act = jax.nn.gelu(jnp.einsum('thkd,td->thk', u, xb, preferred_element_type=f32), approximate=False)
        vsel = jnp.take(v_tab, idx, axis=0)
        return jnp.einsum('thk,thkd->td', (gate * act).astype(xb.dtype), vsel)

    return lax.map(block, xt).reshape(b, s, d)

def setup_inputs(seed: int = 0) -> dict:
    key = jax.random.key(seed)
    ks = jax.random.split(key, 20)

    def nrm(k, shape, std):
        return jax.random.normal(k, shape, f32) * std

    dt = jnp.exp(jax.random.uniform(ks[4], (N_A_LAYERS, DN_HEADS), f32, math.log(1e-3), math.log(1e-1)))
    return {
        'x': nrm(ks[0], (BATCH, SEQ, D_MODEL), 1.0),
        'dn_w_in': nrm(ks[1], (N_A_LAYERS, D_MODEL, 4 * DN_WIDTH + 2 * DN_HEADS), D_MODEL ** -0.5),
        'dn_conv': nrm(ks[2], (N_A_LAYERS, CONV_K, 3 * DN_WIDTH), CONV_K ** -0.5),
        'dn_a_log': jnp.log(jax.random.uniform(ks[3], (N_A_LAYERS, DN_HEADS), f32, 1.0, 16.0)),
        'dn_dt_bias': dt + jnp.log(-jnp.expm1(-dt)),
        'dn_norm_w': 1.0 + nrm(ks[5], (N_A_LAYERS, DN_HEAD_DIM), 0.02),
        'dn_w_out': nrm(ks[6], (N_A_LAYERS, DN_WIDTH, D_MODEL), BETA * DN_WIDTH ** -0.5),
        'shared_w_kv': nrm(ks[7], (D_MODEL, 2 * N_GROUPS * B_WIDTH), D_MODEL ** -0.5),
        'attn_w_q': nrm(ks[8], (N_B_LAYERS, D_MODEL, N_GROUPS * B_WIDTH), D_MODEL ** -0.5),
        'attn_w_out': nrm(ks[9], (N_B_LAYERS, B_WIDTH, D_MODEL), BETA * B_WIDTH ** -0.5),
        'peer_w_query': nrm(ks[10], (DEPTH, D_MODEL, PEER_HEADS * PEER_QDIM), D_MODEL ** -0.5),
        'peer_sub_keys': nrm(ks[11], (DEPTH, PEER_HEADS, 2, PEER_NKEYS, PEER_QDIM // 2), (PEER_QDIM // 2) ** -0.5),
        'peer_u': nrm(ks[12], (DEPTH, PEER_EXPERTS, D_MODEL), D_MODEL ** -0.5),
        'peer_v': nrm(ks[13], (DEPTH, PEER_EXPERTS, D_MODEL), BETA),
        'ln_mix_g': 1.0 + nrm(ks[14], (DEPTH, D_MODEL), 0.02),
        'ln_mix_b': nrm(ks[15], (DEPTH, D_MODEL), 0.02),
        'ln_ffn_g': 1.0 + nrm(ks[16], (DEPTH, D_MODEL), 0.02),
        'ln_ffn_b': nrm(ks[17], (DEPTH, D_MODEL), 0.02),
    }

def reference(x, dn_w_in, dn_conv, dn_a_log, dn_dt_bias, dn_norm_w, dn_w_out, shared_w_kv, attn_w_q, attn_w_out,
              peer_w_query, peer_sub_keys, peer_u, peer_v, ln_mix_g, ln_mix_b, ln_ffn_g, ln_ffn_b):
    b, s, _ = x.shape
    cos, sin = rope_tables(s)
    k_sh = None
    v_sh = None
    for layer in range(DEPTH):
        if layer < N_A_LAYERS:
            i = layer
            h = deltanet_mixer(x, dn_w_in[i], dn_conv[i], dn_a_log[i], dn_dt_bias[i], dn_norm_w[i], dn_w_out[i])
        else:
            j = layer - N_A_LAYERS
            if j == 0:
                kv = (x @ shared_w_kv).reshape(b, s, 2, N_GROUPS, B_HEADS, B_HEAD_DIM)
                k_sh = partial_rope(kv[:, :, 0], cos, sin)
                v_sh = kv[:, :, 1]
            h = dilated_mixer(x, attn_w_q[j], k_sh, v_sh, attn_w_out[j], cos, sin)
        x = layer_norm(ALPHA * x + h, ln_mix_g[layer], ln_mix_b[layer])
        f = peer_ffn(x, peer_w_query[layer], peer_sub_keys[layer], peer_u[layer], peer_v[layer])
        x = layer_norm(ALPHA * x + f, ln_ffn_g[layer], ln_ffn_b[layer])
    return x


_drawn_inputs = setup_inputs


def setup_inputs(seed=0):
    import zlib

    import numpy as np

    out = dict(_drawn_inputs(seed))
    spreads = {}
    factors = {}
    for name, (base, spread) in spreads.items():
        noise = np.random.default_rng([zlib.crc32(name.encode()), seed]).standard_normal(out[name].shape)
        drawn = base * np.exp(spread * noise) if base else spread * noise
        out[name] = __import__('jax').numpy.asarray(drawn.astype(out[name].dtype))
    for name, factor in factors.items():
        out[name] = (out[name] * factor).astype(out[name].dtype)
    return out
```

```python
from contextlib import ExitStack

import concourse.bass as bass
from concourse import mybir

F32 = mybir.dt.float32
U32 = mybir.dt.uint32
ALU = mybir.AluOpType
ACT = mybir.ActivationFunctionType
AX_X = mybir.AxisListType.X

P = 128
SEQ, D = 256, 1024
TILES = SEQ // P
KB = D // P
HEADS = 8
HALF = HEADS // 2
GROUPS = 3
TOPK = 16
CONV = 4
ALPHA = 4.0 ** 0.25
LN_EPS = 1e-5
NORM_EPS = 1e-6
SCALE = float(P) ** -0.5
NEG = -1e30
LEVELS = 7
RING = 8
BLOCKS = 4 * HEADS
WSLOTS = 2
SLICE = 512

C_ID = 0
C_TRI = C_ID + P
C_NEG = C_TRI + P
C_LVL = C_NEG + P
C_ATT = C_LVL + LEVELS * P
C_ROPE = C_ATT + GROUPS * SEQ
C_IOTA = C_ROPE + TILES * 2 * 16
C_ALL = C_IOTA + 16

INITIAL_LOADS = 8


def psum_plan():
    plan = []
    for t in range(TILES):
        plan += [(("x0T", t, i), 2 * t + i, 1) for i in range(2)]
    plan += [(("convw",), 4, 1)]
    plan += [(("qkv", n), n % 2, 1) for n in range(12)]
    plan += [(("z", n), n % 2, 1) for n in range(4)]
    plan += [(("ab",), 2, 1), (("gcum",), 3, 1)]

    def delta(t):
        out = []
        for f in range(2):
            out += [(("kt", t, f), 2 + f, 2), (("vt", t, f), 4 + f, 1),
                    (("qt", t, f), 6 + f, 1), (("gB", t, f), f, 1)]
        for f in range(2):
            out += [(("kbT", t, f), 4 + f, 1), (("A", t, f), 6 + f, 1)]
        out += [(("M", t, f), f, 1) for f in range(2)]
        for s in range(LEVELS):
            out += [(("Y", t, s, f), 2 + f, 1) for f in range(2)]
            for f in range(2):
                if s < LEVELS - 1:
                    out += [(("Z", t, s, f), 4 + f, 1)]
                out += [(("ZT", t, s, f), 6 + f, 1)]
        if t:
            out += [(("kS", t, f), 2 + f, 1) for f in range(2)]
            out += [(("qS", t, f), 4 + f, 1) for f in range(2)]
        out += [(("vn", t, f), f, 1) for f in range(2)]
        out += [(("o", t, f), 6 + f, 1) for f in range(2)]
        if not t:
            out += [(("S", t, f), 2 + f, 1) for f in range(2)]
        out += [(("oT", t, f), 4 + f, 1) for f in range(2)]
        out += mixed_out(0, t)
        return out

    def mixed_out(layer, t):
        return ([(("mix", layer, t, n), n, 1) for n in range(2)]
                + [(("x1T", layer, t, n), 2 + n, 1) for n in range(2)])

    def head(g):
        out = []
        if g % 2 == 0:
            out += [(("skT", g // 2, i), 4 + i, 1) for i in range(4)]
        out += [(("query", g, n), n % 2, 1) for n in range(4)]
        out += [(("sc", g, n), 2 + n % 4, 1) for n in range(4)]
        return out

    def attend(t):
        out = [(("x2T", t, n), 2 + n, 1) for n in range(2)]
        for f in range(2):
            for n in range(9):
                out += [(("kvq", t, f, n), n % 2, 1)]
                if n // 3 != 1:
                    out += [(("kqT", t, f, n), 7, 1)]
            for h in range(HALF):
                out += [(("score", t, f, h), 2, 1), (("pT", t, f, h), 4, 1), (("pv", t, f, h), 6, 1)]
            out += [(("aoT", t, f), 7, 1)]
        return out + mixed_out(1, t)

    plan += delta(0) + head(0) + delta(1) + head(1)
    plan += attend(0) + head(2) + attend(1) + head(3)
    return plan


class Psum:

    def __init__(self, banks, full, taken):
        self.banks, self.full_sem, self.taken_sem = banks, full, taken
        self.at = {}
        fills, taken_count = [0] * 8, [0] * 8
        for key, bank, releases in psum_plan():
            before = taken_count[bank]
            fills[bank] += 1
            taken_count[bank] += releases
            self.at[key] = (bank, fills[bank], before, taken_count[bank])

    def bank(self, *key):
        b = self.at[key][0]
        return self.banks[:, b * SLICE:(b + 1) * SLICE]

    def full(self, *key):
        b, n, _, _ = self.at[key]
        return self.full_sem[b], n

    def taken(self, *key):
        b, _, _, n = self.at[key]
        return self.taken_sem[b], n

    def sem_full(self, *key):
        return self.full_sem[self.at[key][0]]

    def sem_taken(self, *key):
        return self.taken_sem[self.at[key][0]]

    def free(self, eng, *key):
        b, _, before, _ = self.at[key]
        if before:
            eng.wait_ge(self.taken_sem[b], before)


def weight_slices(w_in, w_out, w_kv, w_q, a_out, w_query, sub_keys):
    def cols(w, c, n=SLICE):
        return w.rearrange("(k p) n -> p k n", p=P)[:, :, c:c + n]

    out = []
    for s in range(6):
        out.append((("qkv", s), cols(w_in, s * SLICE), ("qkv", 2 * s + 1)))
    for s in range(2):
        out.append((("z", s), cols(w_in, 3 * D + s * SLICE), ("z", 2 * s + 1)))

    def mixed_out(layer, t, w):
        return [(("mix", layer, t, s), cols(w, s * SLICE), ("mix", layer, t, s)) for s in range(2)]

    def head(g):
        keys = [(("sk", g // 2), sub_keys[g // 2], ("skT", g // 2, 3))] if g % 2 == 0 else []
        return keys + [(("query", g, s), cols(w_query[g // 2], s * SLICE), ("query", g, s))
                       for s in range(4)]

    def attend(t):
        got = []
        for f in range(2):
            for n in range(9):
                what, grp = divmod(n, 3)
                w, base = (w_kv, what * GROUPS * D) if what < 2 else (w_q, 0)
                got.append((("kvq", t, f, n), cols(w, base + grp * D + f * SLICE), ("kvq", t, f, n)))
        return got

    out += mixed_out(0, 0, w_out) + head(0) + mixed_out(0, 1, w_out) + head(1)
    out += attend(0) + mixed_out(1, 0, a_out) + head(2)
    out += attend(1) + mixed_out(1, 1, a_out) + head(3)
    return out


def norm_order():
    return [("mix", 0, 0), ("mix", 0, 1), ("ffn", 0, 0), ("mix", 1, 0), ("ffn", 0, 1), ("mix", 1, 1),
            ("ffn", 1, 0), ("ffn", 1, 1)]


class Steps:

    def __init__(self, eng, sem):
        self.eng, self.sem, self.n = eng, sem, 0

    def __call__(self, ins):
        self.n += 1
        return ins.then_inc(self.sem, 1)

    def wait(self):
        self.eng.wait_ge(self.sem, self.n)


def yoco_deltanet_dilated_peer(nc, x_d, w_in, conv_d, alog_d, dtb_d, normw_d, w_out, w_kv, w_q, a_out,
                               w_query, sub_keys, u_tab, v_tab, gmix, bmix, gffn, bffn, const_d, out_d):
    with ExitStack() as ctx:
        def sb(name, cols, dt=F32):
            return ctx.enter_context(nc.sbuf_tensor(name, [P, cols], dt))

        def sem(name):
            return ctx.enter_context(nc.semaphore(name))

        ring = sb("ring", RING * D)
        wbuf = sb("wbuf", WSLOTS * KB * SLICE)
        x = sb("x_rows", TILES * D)
        xT = sb("xT", KB * SEQ)
        skT = sb("skT", 16 * P)
        consts = sb("consts", C_ALL)
        gb = sb("gb", 2 * D)
        acc = sb("acc", 2 * D)
        qhT = sb("qhT", 16 * P)
        sc = sb("sc", 16 * P)
        topv = sb("topv", 16 * TOPK)
        topi = sb("topi", 16 * TOPK, U32)
        topf = sb("topf", 16 * TOPK)
        best = sb("best", P)
        pos = sb("pos", P, U32)
        posf = sb("posf", 2 * P)
        expert = sb("expert", 2 * P)
        posc = expert[:, :].bitcast(U32)
        idx = sb("idx", 2 * P, U32)
        stage = sb("stage", 2 * TOPK, U32)
        gate = sb("gate", 2 * P)
        gden = sb("gden", 2 * HEADS)
        dots = sb("dots", TOPK)
        gel = sb("gel", TOPK)
        wts = sb("wts", TOPK)
        ab = sb("ab", TILES * 16)
        alog = sb("alog", HEADS)
        dtb = sb("dtb", HEADS)
        normw = sb("normw", P)
        cw = sb("cw", 24 * CONV)
        glog = sb("glog", TILES * HEADS)
        gtmp = sb("gtmp", 3 * TILES * HEADS)
        beta = sb("beta", TILES * HEADS)
        gcum = sb("gcum", TILES * HEADS)
        egc = sb("egc", TILES * HEADS)
        decl = sb("decl", HEADS)
        ss = sb("ss", 16)
        c_state = sb("c_state", HEADS)
        c_query = sb("c_query", HEADS)
        c_carry = sb("c_carry", HEADS)
        coef = sb("coef", HEADS)
        rs_in = sb("rs_in", 16)
        rs_y = sb("rs_y", 16)
        rs_t = sb("rs_t", 16)
        rqk = sb("rqk", 16)
        bn = sb("bn", 2 * 6)
        mv = sb("mv", 2)
        mxs = sb("mxs", 4)
        arena = sb("arena", 17 * D)

        def part(first, cols):
            return arena[:, first:first + cols]

        qkvT = part(0, 24 * SEQ)
        zs = part(6 * D, 2 * D)
        dec = part(8 * D, D)
        Ybuf = dec
        MT = part(9 * D, D)
        AT = part(10 * D, D)
        Tm = part(11 * D, D)
        oT = Tm
        TT = part(12 * D, D)
        vb = part(13 * D, D)
        kb = part(14 * D, D)
        vn = kb
        kbT = part(15 * D, D)
        od = kbT
        S1 = part(16 * D, D)
        raw = part(8 * D, 2 * 2 * (SEQ + CONV - 1))
        kS = acc[:, 0:D]
        cw_in = acc[:, D:D + P]
        wab = acc[:, D + P:D + 2 * P]
        kT0 = part(0, 24 * P)
        v0 = part(3 * D, 24 * P)
        kT1 = part(6 * D, 12 * P)
        v1 = part(7 * D + 512, 12 * P)
        qT = part(9 * D, 12 * P)
        kq = part(10 * D + 512, 2 * SLICE)
        rope = part(11 * D + 512, 2 * P)
        prob = part(12 * D, GROUPS * SEQ)
        probT = part(13 * D, GROUPS * SEQ)
        oh = part(14 * D, HALF * P)
        oaT = part(15 * D, D)

        banks = ctx.enter_context(nc.psum_tensor("banks", [P, 8 * SLICE], F32))
        full = [sem(f"bank{b}_full") for b in range(8)]
        taken = [sem(f"bank{b}_taken") for b in range(8)]
        ps = Psum(banks, full, taken)

        loaded = sem("inputs_loaded")
        w_land = [sem(f"weights{i}_landed") for i in range(WSLOTS)]
        gb_land = sem("norm_rows_landed")
        landed = [sem(f"row{i}_landed") for i in range(RING)]
        ring_used = sem("rows_used")
        staged = sem("indices_staged")
        gelu_done = sem("gelu_done")
        wts_ready = sem("weights_of_rows_ready")
        idx_ready = sem("indices_ready")
        vec = sem("vector_step")
        act = sem("scalar_step")
        rs_asked = sem("rsqrt_asked")
        rs_said = sem("rsqrt_said")
        sil_in = sem("conv_done")
        sil_out = sem("silu_done")
        zero_ok = sem("raw_zeroed")
        g_ready = sem("log_decay_ready")
        sm_in = sem("small_in")
        sm_out = sem("small_out")
        dec_in = sem("decay_exponent_ready")
        dec_out = sem("decay_ready")
        sq_o = sem("squares_done")
        od_ready = sem("delta_output_ready")
        vb_ready = sem("delta_targets_ready")
        od_sum = sem("delta_output_summed")
        t_init = sem("inverse_started")
        x_ready = sem("x_normed")
        gx_in = sem("gate_exponent_ready")
        gx_out = sem("gate_exp_done")
        roped = sem("roped")
        p_done = sem("probabilities_done")
        nmx = sem("negated_max_ready")
        stored = sem("output_stored")

        ident = consts[:, C_ID:C_ID + P]
        tri = consts[:, C_TRI:C_TRI + P]
        negmask = consts[:, C_NEG:C_NEG + P]
        attmask = consts[:, C_ATT:C_ATT + GROUPS * SEQ].rearrange("p (g k) -> p g k", g=GROUPS)
        iota16 = consts[:, C_IOTA:C_IOTA + 16]

        slices = weight_slices(w_in, w_out, w_kv, w_q, a_out, w_query, sub_keys)
        slot_of = {key: n for n, (key, _, _) in enumerate(slices)}

        def weights(*key):
            s = slot_of[key] % WSLOTS
            return wbuf[:, s * KB * SLICE:(s + 1) * KB * SLICE].rearrange("p (k n) -> p k n", k=KB)

        def heads4(ap):
            return ap.rearrange("p (h d) -> p h d", h=HALF)

        def half(ap, f):
            return ap[:, f * HALF * P:(f + 1) * HALF * P]

        def xtile(t):
            return x[:, t * D:(t + 1) * D]

        def xTb(k, t):
            return xT[:, k * SEQ + t * P:k * SEQ + (t + 1) * P]

        def channels(blk, t):
            return qkvT[:, blk * SEQ + t * P:blk * SEQ + (t + 1) * P]

        def spread(cols, n=P):
            return cols.unsqueeze(2).to_broadcast([P, cols.shape[1], n])

        def kq_turn(n):
            return n if n < 3 else n - 3

        def kq_slot(n):
            s = kq_turn(n) % 2
            return kq[:, s * SLICE:(s + 1) * SLICE]

        def tile_heads(first, second, t, kt, f, grp, h, n):
            buf, at = (first, grp * HEADS + f * HALF + h) if kt == 0 else (second, grp * HALF + h)
            return buf[:, at * P:(at + n) * P]

        def k_heads(t, kt, f, grp, h, n):
            return tile_heads(kT0, kT1, t, kt, f, grp, h, n)

        def v_heads(t, kt, f, grp, h, n):
            return tile_heads(v0, v1, t, kt, f, grp, h, n)

        def conv_rows(n):
            s = n % 2
            w = SEQ + CONV - 1
            return raw[:, s * 2 * w:(s + 1) * 2 * w].rearrange("p (b k) -> p b k", b=2)

        def gather_steps(steps):
            room = BLOCKS - 4
            return [steps[b * len(steps) // room:(b + 1) * len(steps) // room] for b in range(room)]

        def delta_steps(t):
            return ([("keys", t, f) for f in range(2)] + [("scaled", t, f) for f in range(2)]
                    + [("grams", t, f) for f in range(2)]
                    + [(kind, t, s) for s in range(LEVELS) for kind in ("masked", "doubled")]
                    + ([("carried", t, 0)] if t else [])
                    + [("summed", t, f) for f in range(2)] + [("gated", t, f) for f in range(2)]
                    + [("mixed", 0, t)])

        def head_steps(g):
            return ([("scores", g, 0)] + [("top", g, n) for n in range(4)] + [("pairs", g, 0)]
                    + [("best", g, n) for n in range(4)] + [("gates", g, 0)]
                    + [("experts", g, c) for c in range(2)])

        def attend_steps(t):
            out = [("x2", t, 0)]
            for f in range(2):
                out += [("slice", t, (f, n)) for n in range(9)]
                for h in range(HALF):
                    out += [("soft", t, (f, h)), ("weigh", t, (f, h))]
                out += [("heads", t, f)]
            return out + [("mixed", 1, t)]

        beside = [delta_steps(1) + head_steps(1), attend_steps(0) + head_steps(2),
                  attend_steps(1) + head_steps(3)]
        norms = norm_order()
        block = ctx.enter_context(nc.Block())

        @block.sync
        def _(eng):
            eng.dma_start(xtile(0), x_d[0:P, :]).then_inc(loaded, 16)
            eng.dma_start(consts[:, :], const_d).then_inc(loaded, 16)
            eng.dma_start(xtile(1), x_d[P:SEQ, :]).then_inc(loaded, 16)
            eng.dma_start(cw_in[0:24 * CONV, :], conv_d.rearrange("j (b p) -> (j b) p", p=P)).then_inc(loaded, 16)
            eng.dma_start(wab[:, :].rearrange("p (k n) -> p k n", k=KB),
                          w_in.rearrange("(k p) n -> p k n", p=P)[:, :, 4 * D:4 * D + 16]).then_inc(loaded, 16)
            eng.dma_start(alog[:, :], alog_d.to_broadcast([P, HEADS])).then_inc(loaded, 16)
            eng.dma_start(dtb[:, :], dtb_d.to_broadcast([P, HEADS])).then_inc(loaded, 16)
            eng.dma_start(normw[:, :], normw_d.to_broadcast([P, P])).then_inc(loaded, 16)

            def load_weights(key, view):
                n = slot_of[key]
                if n >= WSLOTS:
                    eng.wait_ge(*ps.full(*slices[n - WSLOTS][2]))
                slot = wbuf[:, (n % WSLOTS) * KB * SLICE:(n % WSLOTS + 1) * KB * SLICE]
                if key[0] == "sk":
                    eng.dma_start(slot[:, 0:16 * P].rearrange("p (s d) -> p s d", s=16), view)\
                       .then_inc(w_land[n % WSLOTS], 16)
                else:
                    eng.dma_start(slot.rearrange("p (k n) -> p k n", k=KB), view).then_inc(w_land[n % WSLOTS], 16)

            def load_norm(i):
                which, layer, _ = norms[i]
                if i:
                    eng.wait_ge(x_ready, i)
                g, b = (gmix, bmix) if which == "mix" else (gffn, bffn)
                eng.dma_start(gb[:, 0:D], g[layer:layer + 1, :].to_broadcast([P, D])).then_inc(gb_land, 16)
                eng.dma_start(gb[:, D:2 * D], b[layer:layer + 1, :].to_broadcast([P, D])).then_inc(gb_land, 16)

            mixes = {("mix", layer, t): norms.index(("mix", layer, t)) for layer in range(2) for t in range(TILES)}
            for key, view, _ in slices:
                load_weights(key, view)
                if key[:3] in mixes and key[3] == 1:
                    load_norm(mixes[key[:3]])
                if key[0] == "query" and key[1] >= 1 and key[2] == 3:
                    load_norm(norms.index(("ffn", (key[1] - 1) // 2, (key[1] - 1) % 2)))
            load_norm(7)
            for t in range(TILES):
                eng.wait_ge(x_ready, 4 + 2 + t + 1)
                eng.dma_start(out_d[t * P:(t + 1) * P, :], xtile(t)).then_inc(stored, 16)
            eng.wait_ge(stored, 16 * TILES)

        @block.gpsimd
        def _(eng):
            for g in range(4):
                table = (u_tab[g // 2], v_tab[g // 2])
                eng.wait_ge(idx_ready, g + 1)
                with eng.Fori(0, HEADS // 2) as r:
                    for par in range(2):
                        h = 2 * r + par
                        copies = HEADS * g + h
                        eng.wait_ge(ring_used, RING * (BLOCKS * g + 4 * h) + 1)
                        eng.tensor_copy(stage[:, par * TOPK:(par + 1) * TOPK],
                                        idx[:, bass.ds((g % 2) * P + TOPK * h, TOPK)]).then_inc(staged, 1)
                        eng.wait_ge(staged, copies + 1)
                        for side in range(2):
                            for j in range(TOPK):
                                slot = j % RING
                                blk = BLOCKS * g + 4 * h + 2 * side + j // RING
                                eng.wait_ge(ring_used, RING * blk + slot + 1)
                                eng.nop(nofuse=True)
                                eng.indirect_dma_start(
                                    ring[:, slot * D:(slot + 1) * D], None, table[side],
                                    bass.IndirectOffsetOnAxis(ap=stage[:, par * TOPK + j:par * TOPK + j + 1],
                                                              axis=0)).then_inc(landed[slot], 16)

        @block.tensor
        def _(eng):
            def transposes(key, sources):
                ps.free(eng, *key)
                bank = ps.bank(*key)
                for i, src in enumerate(sources):
                    rows = src.shape[0]
                    ins = eng.transpose(bank[:, i * P:i * P + rows], src, ident[0:rows, 0:rows])
                ins.then_inc(ps.sem_full(*key), 1)

            def products(key, pairs, cols=P, wait_free=True):
                if wait_free:
                    ps.free(eng, *key)
                bank = ps.bank(*key)
                for i, terms in enumerate(pairs):
                    for n, (a, b) in enumerate(terms):
                        ins = eng.matmul(bank[:, i * cols:(i + 1) * cols], lhsT=a, rhs=b,
                                         start=n == 0, stop=n == len(terms) - 1)
                ins.then_inc(ps.sem_full(*key), 1)

            def weights_here(*key):
                n = slot_of[key]
                eng.wait_ge(w_land[n % WSLOTS], 16 * (n // WSLOTS + 1))
                return weights(*key)

            def x_transposed(key, t):
                for n in range(2):
                    transposes(key + (n,), [xtile(t)[:, (4 * n + i) * P:(4 * n + i + 1) * P] for i in range(4)])

            eng.wait_ge(loaded, 16 * INITIAL_LOADS)
            for t in range(TILES):
                x_transposed(("x0T", t), t)
            transposes(("convw",), [cw_in[0:24 * CONV, :]])

            for t in range(TILES):
                for n in range(2):
                    eng.wait_ge(*ps.taken("x0T", t, n))
            for s in range(6):
                w = weights_here("qkv", s)
                for pair in range(2):
                    products(("qkv", 2 * s + pair),
                             [[(w[:, k, c * P:(c + 1) * P], xT[:, k * SEQ:(k + 1) * SEQ]) for k in range(KB)]
                              for c in (2 * pair, 2 * pair + 1)], SEQ)
            for s in range(2):
                w = weights_here("z", s)
                for t in range(TILES):
                    products(("z", 2 * s + t), [[(xTb(k, t), w[:, k, :]) for k in range(KB)]], SLICE)
            products(("ab",), [[(xTb(k, t), wab[:, k * 16:(k + 1) * 16]) for k in range(KB)]
                               for t in range(TILES)], 16)
            eng.wait_ge(g_ready, 1)
            products(("gcum",), [[(tri, glog[:, :])]], TILES * HEADS)

            def delta(t):
                for f in range(2):
                    hs = range(f * HALF, (f + 1) * HALF)
                    if t == 0:
                        eng.wait_ge(sil_out, 12)
                    transposes(("kt", t, f), [channels(8 + h, t) for h in hs])
                    transposes(("vt", t, f), [channels(16 + h, t) for h in hs])
                    transposes(("qt", t, f), [channels(h, t) for h in hs])
                    products(("gB", t, f), [[(glog[:, t * HEADS + h:t * HEADS + h + 1].to_broadcast([P, P]), tri)]
                                            for h in hs])
                for f in range(2):
                    eng.wait_ge(*ps.taken("kt", t, f))
                    transposes(("kbT", t, f), [half(kb, f)[:, i * P:(i + 1) * P] for i in range(HALF)])
                    products(("A", t, f), [[(channels(8 + h, t), channels(h, t))]
                                           for h in range(f * HALF, (f + 1) * HALF)])
                for f in range(2):
                    eng.wait_ge(*ps.taken("kbT", t, f))
                    products(("M", t, f), [[(channels(8 + h, t), kbT[:, h * P:(h + 1) * P])]
                                           for h in range(f * HALF, (f + 1) * HALF)])
                eng.wait_ge(t_init, t + 1)
                for s in range(LEVELS):
                    for f in range(2):
                        hs = range(f * HALF, (f + 1) * HALF)
                        if s:
                            eng.wait_ge(*ps.taken("Z", t, s - 1, f))
                            eng.wait_ge(*ps.taken("ZT", t, s - 1, f))
                        else:
                            eng.wait_ge(*ps.taken("M", t, f))
                        products(("Y", t, s, f), [[(MT[:, h * P:(h + 1) * P], Tm[:, h * P:(h + 1) * P])]
                                                  for h in hs])
                    for f in range(2):
                        hs = range(f * HALF, (f + 1) * HALF)
                        eng.wait_ge(*ps.taken("Y", t, s, f))
                        if s < LEVELS - 1:
                            products(("Z", t, s, f), [[(TT[:, h * P:(h + 1) * P], Ybuf[:, h * P:(h + 1) * P])]
                                                      for h in hs])
                        products(("ZT", t, s, f), [[(Ybuf[:, h * P:(h + 1) * P], TT[:, h * P:(h + 1) * P])]
                                                   for h in hs])
                if t:
                    for f in range(2):
                        eng.wait_ge(*ps.taken("S", 0, f))
                        products(("kS", t, f), [[(channels(8 + h, t), S1[:, h * P:(h + 1) * P])]
                                                for h in range(f * HALF, (f + 1) * HALF)])
                    for f in range(2):
                        products(("qS", t, f), [[(channels(h, t), S1[:, h * P:(h + 1) * P])]
                                                for h in range(f * HALF, (f + 1) * HALF)])
                for f in range(2):
                    eng.wait_ge(*ps.taken("ZT", t, LEVELS - 1, f))
                    if t:
                        eng.wait_ge(vb_ready, f + 1)
                    else:
                        eng.wait_ge(*ps.taken("vt", t, f))
                    products(("vn", t, f), [[(TT[:, h * P:(h + 1) * P], vb[:, h * P:(h + 1) * P])]
                                            for h in range(f * HALF, (f + 1) * HALF)])
                for f in range(2):
                    eng.wait_ge(*ps.taken("vn", t, f))
                    eng.wait_ge(*ps.taken("A", t, f))
                    products(("o", t, f), [[(AT[:, h * P:(h + 1) * P], vn[:, h * P:(h + 1) * P])]
                                           for h in range(f * HALF, (f + 1) * HALF)])
                if not t:
                    for f in range(2):
                        products(("S", t, f), [[(kS[:, h * P:(h + 1) * P], vn[:, h * P:(h + 1) * P])]
                                               for h in range(f * HALF, (f + 1) * HALF)])
                for f in range(2):
                    eng.wait_ge(od_ready, 2 * t + f + 1)
                    transposes(("oT", t, f), [od[:, h * P:(h + 1) * P] for h in range(f * HALF, (f + 1) * HALF)])
                for f in range(2):
                    eng.wait_ge(*ps.taken("oT", t, f))
                mixed_out(0, t, oT)

            def mixed_out(layer, t, oTb):
                for s in range(2):
                    w = weights_here("mix", layer, t, s)
                    products(("mix", layer, t, s), [[(oTb[:, k * P:(k + 1) * P], w[:, k, :]) for k in range(KB)]],
                             SLICE)
                eng.wait_ge(x_ready, norms.index(("mix", layer, t)) + 1)
                x_transposed(("x1T", layer, t), t)
                for n in range(2):
                    eng.wait_ge(*ps.taken("x1T", layer, t, n))

            def head(g):
                t = g % 2
                if t == 0:
                    w = weights_here("sk", g // 2)
                    sk = w.rearrange("p k n -> p (k n)")
                    for i in range(4):
                        transposes(("skT", g // 2, i), [sk[:, (4 * i + c) * P:(4 * i + c + 1) * P] for c in range(4)])
                for s in range(4):
                    w = weights_here("query", g, s)
                    products(("query", g, s), [[(w[:, k, c * P:(c + 1) * P], xTb(k, t)) for k in range(KB)]
                                               for c in range(4)])
                if t == 0:
                    for i in range(4):
                        eng.wait_ge(*ps.taken("skT", g // 2, i))
                for s in range(4):
                    eng.wait_ge(*ps.taken("query", g, s))
                    products(("sc", g, s), [[(qhT[:, c * P:(c + 1) * P], skT[:, c * P:(c + 1) * P])]
                                            for c in range(4 * s, 4 * s + 4)])

            def attend(t):
                eng.wait_ge(x_ready, norms.index(("ffn", 0, t)) + 1)
                x_transposed(("x2T", t), t)
                for n in range(2):
                    eng.wait_ge(*ps.taken("x2T", t, n))
                for f in range(2):
                    for n in range(9):
                        w = weights_here("kvq", t, f, n)
                        products(("kvq", t, f, n), [[(xTb(k, t), w[:, k, :]) for k in range(KB)]], SLICE)
                        for m in ([n - 1] if n else []) + ([8] if n == 8 else []):
                            if m // 3 == 1:
                                continue
                            eng.wait_ge(roped, (t * 2 + f) * 6 + kq_turn(m) + 1)
                            transposes(("kqT", t, f, m), [kq_slot(m)[:, i * P:(i + 1) * P] for i in range(HALF)])
                    for h in range(HALF):
                        ps.free(eng, "score", t, f, h)
                        if h == 0:
                            eng.wait_ge(*ps.taken("kqT", t, f, 8))
                            for n in range(3, 6):
                                eng.wait_ge(*ps.taken("kvq", t, f, n))
                        sb2 = banks[:, 2 * SLICE:2 * SLICE + GROUPS * (t + 1) * P]
                        for grp in range(GROUPS):
                            for kt in range(t + 1):
                                col = (grp * (t + 1) + kt) * P
                                ins = eng.matmul(sb2[:, col:col + P], lhsT=qT[:, (grp * HALF + h) * P:(grp * HALF + h + 1) * P],
                                                 rhs=k_heads(t, kt, f, grp, h, 1),
                                                 start=True, stop=True)
                        ins.then_inc(ps.sem_full("score", t, f, h), 1)
                        ps.free(eng, "pT", t, f, h)
                        eng.wait_ge(p_done, (t * 2 + f) * HALF + h + 1)
                        for i in range(GROUPS * (t + 1)):
                            ins = eng.transpose(banks[:, 4 * SLICE + i * P:4 * SLICE + (i + 1) * P], prob[:, i * P:(i + 1) * P], ident)
                        ins.then_inc(ps.sem_full("pT", t, f, h), 1)
                        eng.wait_ge(*ps.taken("pT", t, f, h))
                        n_terms = GROUPS * (t + 1)
                        products(("pv", t, f, h), [[(probT[:, i * P:(i + 1) * P],
                                                     v_heads(t, i % (t + 1), f, i // (t + 1), h, 1))
                                                    for i in range(n_terms)]])
                    eng.wait_ge(*ps.taken("pv", t, f, HALF - 1))
                    transposes(("aoT", t, f), [oh[:, h * P:(h + 1) * P] for h in range(HALF)])
                for f in range(2):
                    eng.wait_ge(*ps.taken("aoT", t, f))
                mixed_out(1, t, oaT)

            delta(0)
            head(0)
            delta(1)
            head(1)
            attend(0)
            head(2)
            attend(1)
            head(3)

        @block.scalar
        def _(eng):
            did = Steps(eng, act)
            rs_n = [0]

            def copy_out(key, out, in_=None, func=ACT.Copy):
                eng.wait_ge(*ps.full(*key))
                eng.activation(out, ps.bank(*key) if in_ is None else in_, func).then_inc(ps.sem_taken(*key), 1)

            def x_out(key, t):
                for n in range(2):
                    out = xT[:, :].rearrange("p (k n) -> p k n", k=KB)[:, 4 * n:4 * n + 4, t * P:(t + 1) * P]
                    copy_out(key + (n,), out, heads4(ps.bank(*key, n)))

            def rsqrt_start(n):
                rs_n[0] += 1
                eng.wait_ge(rs_asked, rs_n[0])
                did(eng.activation(rs_y[:, 0:n], rs_in[:, 0:n], ACT.Ln))
                did.wait()
                eng.activation(rs_y[:, 0:n], rs_y[:, 0:n], ACT.Exp, scale=-0.5).then_inc(rs_said, 1)

            def keys(t, f):
                copy_out(("kt", t, f), half(MT, f), func=ACT.Square)
                copy_out(("qt", t, f), half(AT, f), func=ACT.Square)
                eng.wait_ge(dec_in, 2 * t + f + 1)
                eng.activation(half(dec, f), half(dec, f), ACT.Exp).then_inc(dec_out, 1)

            def scaled(t, f):
                rsqrt_start(8)
                if f:
                    for m in (Tm, TT):
                        ins = eng.activation(m.rearrange("p (h d) -> p h d", h=HEADS),
                                             ident.unsqueeze(1).to_broadcast([P, HEADS, P]), ACT.Copy)
                    ins.then_inc(t_init, 1)

            def grams(t, f):
                copy_out(("kbT", t, f), half(kbT, f))

            def summed(t, f):
                copy_out(("vn", t, f), half(vn, f))
                if t:
                    eng.wait_ge(od_sum, f + 1)
                else:
                    eng.wait_ge(*ps.taken("o", t, f))
                eng.activation(half(Ybuf, f), half(od, f), ACT.Square).then_inc(sq_o, 1)

            def gated(t, f):
                rsqrt_start(HALF)
                if not t:
                    copy_out(("S", t, f), half(S1, f))
                copy_out(("oT", t, f), half(oT, f))

            def mixed(layer, t):
                rsqrt_start(1)
                x_out(("x1T", layer, t), t)

            def scores(g):
                if g:
                    eng.wait_ge(idx_ready, g)
                if g % 2 == 0:
                    for i in range(4):
                        copy_out(("skT", g // 2, i), skT[:, 4 * i * P:(4 * i + 4) * P])
                for n in range(4):
                    copy_out(("query", g, n), qhT[:, 4 * n * P:(4 * n + 4) * P])
                for n in range(4):
                    copy_out(("sc", g, n), sc[:, 4 * n * P:(4 * n + 4) * P])

            def gates(g):
                eng.wait_ge(gx_in, g + 1)
                eng.activation(gate[:, (g % 2) * P:(g % 2 + 1) * P], best[:, :], ACT.Exp).then_inc(gx_out, 1)

            def kv_slice(t, f, n):
                key = ("kvq", t, f, n)
                if n // 3 == 1:
                    copy_out(key, v_heads(t, t, f, n - 3, 0, HALF))
                else:
                    turn = kq_turn(n)
                    if turn >= 2:
                        before = turn - 2
                        eng.wait_ge(*ps.full("kqT", t, f, before if before < 3 else before + 3))
                    copy_out(key, kq_slot(n))
                for m in ([n - 1] if n else []) + ([8] if n == 8 else []):
                    if m // 3 != 1:
                        out = (k_heads(t, t, f, m, 0, HALF) if m < 3
                               else qT[:, (m - 6) * HALF * P:(m - 5) * HALF * P])
                        copy_out(("kqT", t, f, m), out)

            def soft(t, f, h):
                n = (t * 2 + f) * HALF + h
                wide = GROUPS * (t + 1) * P
                eng.wait_ge(nmx, n + 1)
                eng.activation(prob[:, 0:wide], prob[:, 0:wide], ACT.Exp, bias=mxs[:, 1:2], scale=SCALE,
                               accum_out=mxs[:, 2:3]).then_inc(p_done, 1)
                if n:
                    eng.wait_ge(*ps.full("pv", *((t, f, h - 1) if h else ((t, f - 1, HALF - 1) if f
                                                                         else (t - 1, 1, HALF - 1)))))
                copy_out(("pT", t, f, h), probT[:, 0:wide], banks[:, 4 * SLICE:4 * SLICE + wide])

            def step(kind, a, b):
                if kind == "keys":
                    keys(a, b)
                elif kind == "scaled":
                    scaled(a, b)
                elif kind == "grams":
                    grams(a, b)
                elif kind == "summed":
                    summed(a, b)
                elif kind == "gated":
                    gated(a, b)
                elif kind == "mixed":
                    mixed(a, b)
                elif kind == "scores":
                    scores(a)
                elif kind == "gates":
                    gates(a)
                elif kind == "x2":
                    x_out(("x2T", a), a)
                elif kind == "slice":
                    kv_slice(a, *b)
                elif kind == "soft":
                    soft(a, *b)
                elif kind == "heads":
                    copy_out(("aoT", a, b), half(oaT, b))

            def gelu(blk, j):
                eng.wait_ge(ring_used, RING * (blk + 2))
                eng.activation(gel[:, j * RING:(j + 1) * RING], dots[:, j * RING:(j + 1) * RING],
                               ACT.Gelu).then_inc(gelu_done, 1)

            for t in range(TILES):
                x_out(("x0T", t), t)
            copy_out(("convw",), cw[:, :], ps.bank("convw")[:, 0:24 * CONV])

            def silu(n):
                eng.wait_ge(sil_in, n + 1)
                pair = qkvT[:, 2 * n * SEQ:(2 * n + 2) * SEQ]
                eng.activation(pair, pair, ACT.Silu).then_inc(sil_out, 1)

            eng.wait_ge(zero_ok, 1)
            for n in range(12):
                if n >= 2:
                    eng.wait_ge(sil_in, n - 1)
                copy_out(("qkv", n), conv_rows(n)[:, :, CONV - 1:],
                         ps.bank("qkv", n).rearrange("p (b k) -> p b k", b=2))
                if n:
                    silu(n - 1)
            silu(11)
            for s in range(2):
                for t in range(TILES):
                    copy_out(("z", 2 * s + t), zs[:, t * D + s * SLICE:t * D + (s + 1) * SLICE], func=ACT.Silu)
            eng.wait_ge(sm_in, 1)
            did(eng.activation(gtmp[:, 16:32], gtmp[:, 16:32], ACT.Exp))
            eng.activation(gtmp[:, 32:48], gtmp[:, 32:48], ACT.Exp, scale=-1.0)
            eng.activation(alog[:, :], alog[:, :], ACT.Exp)
            did.wait()
            eng.activation(gtmp[:, 16:32], gtmp[:, 16:32], ACT.Ln, bias=1.0).then_inc(sm_out, 1)
            eng.wait_ge(*ps.taken("gcum"))
            eng.activation(egc[:, :], gcum[:, :], ACT.Exp).then_inc(sm_out, 1)

            for st in delta_steps(0) + head_steps(0):
                step(*st)
            for g in range(4):
                if g < 3:
                    for b, steps in enumerate(gather_steps(beside[g])):
                        if b % 4 < 2:
                            gelu(BLOCKS * g + b, b % 4)
                        for st in steps:
                            step(*st)
                    for b in range(2):
                        gelu(BLOCKS * g + BLOCKS - 4 + b, b)
                else:
                    with eng.Fori(0, HEADS) as h:
                        for b in range(2):
                            gelu(BLOCKS * g + 4 * h + b, b)
                rsqrt_start(1)

        @block.vector
        def _(eng):
            did = Steps(eng, vec)
            rs_n = [0]
            norm_n = [0]

            def tt(out, a, b, op):
                return eng.tensor_tensor(out, a, b, op)

            def rsqrt(source, n, out, scale, eps):
                rs_n[0] += 1
                eng.tensor_scalar(rs_in[:, 0:n], source, scale, eps, ALU.mult, ALU.add).then_inc(rs_asked, 1)
                eng.wait_ge(rs_said, rs_n[0])
                did(tt(rs_t[:, 0:n], rs_y[:, 0:n], rs_y[:, 0:n], ALU.mult))
                did.wait()
                did(tt(rs_t[:, 0:n], rs_t[:, 0:n], rs_in[:, 0:n], ALU.mult))
                did.wait()
                did(eng.tensor_scalar(rs_t[:, 0:n], rs_t[:, 0:n], -0.5, 1.5, ALU.mult, ALU.add))
                did.wait()
                did(tt(out, rs_y[:, 0:n], rs_t[:, 0:n], ALU.mult))
                did.wait()

            def keys(t, f):
                cols = slice(t * HEADS + f * HALF, t * HEADS + (f + 1) * HALF)
                eng.wait_ge(*ps.full("gB", t, f))
                tt(heads4(half(dec, f)), heads4(ps.bank("gB", t, f)), spread(gcum[:, cols]),
                   ALU.subtract).then_inc(ps.sem_taken("gB", t, f), 1)
                eng.wait_ge(*ps.taken("gB", t, f))
                tt(heads4(half(dec, f)), heads4(half(dec, f)), negmask.unsqueeze(1).to_broadcast([P, HALF, P]),
                   ALU.add).then_inc(dec_in, 1)
                eng.wait_ge(*ps.full("vt", t, f))
                tt(heads4(half(vb, f)), heads4(ps.bank("vt", t, f)), spread(beta[:, cols]),
                   ALU.mult).then_inc(ps.sem_taken("vt", t, f), 1)

            def scaled(t, f):
                cols = slice(t * HEADS + f * HALF, t * HEADS + (f + 1) * HALF)
                hs = slice(f * HALF, (f + 1) * HALF)
                eng.wait_ge(*ps.taken("qt", t, f))
                r = rqk[:, 8 * f:8 * f + 8]
                did(eng.tensor_reduce(ss[:, 8 * f:8 * f + HALF], heads4(half(AT, f)), AX_X, ALU.add))
                did(eng.tensor_reduce(ss[:, 8 * f + HALF:8 * f + 8], heads4(half(MT, f)), AX_X, ALU.add))
                did.wait()
                rsqrt(ss[:, 8 * f:8 * f + 8], 8, r, 1.0, NORM_EPS)
                rq, rk = r[:, 0:HALF], r[:, HALF:8]
                did(tt(coef[:, hs], rk, beta[:, cols], ALU.mult))
                did(eng.tensor_scalar(c_query[:, hs], rq, SCALE, None, ALU.mult))
                eng.wait_ge(dec_out, 2 * t + f + 1)
                did(tt(heads4(half(dec, f)), heads4(half(dec, f)), spread(rk), ALU.mult))
                did.wait()
                if t:
                    did(tt(c_state[:, hs], coef[:, hs], egc[:, cols], ALU.mult))
                    did(tt(c_carry[:, hs], c_query[:, hs], egc[:, cols], ALU.mult))
                ins = tt(heads4(half(kb, f)), heads4(ps.bank("kt", t, f)), spread(coef[:, hs]), ALU.mult)
                if not t:
                    ins = tt(heads4(half(kS, f)), heads4(ps.bank("kt", t, f)),
                             heads4(half(dec, f))[:, :, P - 1:P].to_broadcast([P, HALF, P]), ALU.mult)
                ins.then_inc(ps.sem_taken("kt", t, f), 1)

            def grams(t, f):
                for key, out in (("A", AT), ("M", MT)):
                    eng.wait_ge(*ps.full(key, t, f))
                    tt(half(out, f), ps.bank(key, t, f), half(dec, f), ALU.mult)\
                        .then_inc(ps.sem_taken(key, t, f), 1)

            def masked(t, s):
                level = consts[:, C_LVL + s * P:C_LVL + (s + 1) * P]
                for f in range(2):
                    eng.wait_ge(*ps.full("Y", t, s, f))
                    tt(heads4(half(Ybuf, f)), heads4(ps.bank("Y", t, s, f)),
                       level.unsqueeze(1).to_broadcast([P, HALF, P]), ALU.mult)\
                        .then_inc(ps.sem_taken("Y", t, s, f), 1)

            def doubled(t, s):
                for f in range(2):
                    for key, m in (("Z", Tm), ("ZT", TT)):
                        if key == "Z" and s == LEVELS - 1:
                            continue
                        eng.wait_ge(*ps.full(key, t, s, f))
                        tt(half(m, f), half(m, f), ps.bank(key, t, s, f), ALU.add)\
                            .then_inc(ps.sem_taken(key, t, s, f), 1)

            def carried(t):
                for f in range(2):
                    hs = slice(f * HALF, (f + 1) * HALF)
                    eng.wait_ge(*ps.full("kS", t, f))
                    tt(heads4(half(Ybuf, f)), heads4(ps.bank("kS", t, f)), spread(c_state[:, hs]), ALU.mult)\
                        .then_inc(ps.sem_taken("kS", t, f), 1)
                    eng.wait_ge(*ps.taken("kS", t, f))
                    tt(half(vb, f), half(vb, f), half(Ybuf, f), ALU.subtract).then_inc(vb_ready, 1)
                    eng.wait_ge(*ps.full("qS", t, f))
                    tt(heads4(half(MT, f)), heads4(ps.bank("qS", t, f)), spread(c_carry[:, hs]), ALU.mult)\
                        .then_inc(ps.sem_taken("qS", t, f), 1)

            def summed(t, f):
                hs = slice(f * HALF, (f + 1) * HALF)
                eng.wait_ge(*ps.full("o", t, f))
                tt(heads4(half(od, f)), heads4(ps.bank("o", t, f)), spread(c_query[:, hs]), ALU.mult)\
                    .then_inc(ps.sem_taken("o", t, f), 1)
                if t:
                    eng.wait_ge(*ps.taken("o", t, f))
                    eng.wait_ge(*ps.taken("qS", t, f))
                    tt(half(od, f), half(od, f), half(MT, f), ALU.add).then_inc(od_sum, 1)

            def gated(t, f):
                eng.wait_ge(sq_o, 2 * t + f + 1)
                did(eng.tensor_reduce(ss[:, 8 * f:8 * f + HALF], heads4(half(Ybuf, f)), AX_X, ALU.add))
                did.wait()
                rsqrt(ss[:, 8 * f:8 * f + HALF], HALF, rqk[:, 8 * f:8 * f + HALF], 1.0 / P, NORM_EPS)
                did(tt(heads4(half(od, f)), heads4(half(od, f)), spread(rqk[:, 8 * f:8 * f + HALF]), ALU.mult))
                did.wait()
                tt(half(od, f), half(od, f), half(zs[:, t * D:(t + 1) * D], f), ALU.mult).then_inc(od_ready, 1)

            def layer_norm(t):
                xt = xtile(t)
                i = norm_n[0]
                norm_n[0] += 1
                for s in range(2):
                    did(eng.bn_stats(bn[:, 6 * s:6 * s + 6], xt[:, s * SLICE:(s + 1) * SLICE]))
                did.wait()
                did(eng.bn_aggr(mv[:, :], bn[:, :].rearrange("p (s c) -> p s c", s=2)))
                did.wait()
                rsqrt(mv[:, 1:2], 1, rs_t[:, 8:9], 1.0, LN_EPS)
                did(eng.tensor_scalar(xt, xt, mv[:, 0:1], rs_t[:, 8:9], ALU.subtract, ALU.mult))
                did.wait()
                eng.wait_ge(gb_land, 32 * (i + 1))
                did(tt(xt, xt, gb[:, 0:D], ALU.mult))
                did.wait()
                tt(xt, xt, gb[:, D:2 * D], ALU.add).then_inc(x_ready, 1)

            def mixed(layer, t):
                for s in range(2):
                    eng.wait_ge(*ps.full("mix", layer, t, s))
                    xs = xtile(t)[:, s * SLICE:(s + 1) * SLICE]
                    eng.scalar_tensor_tensor(xs, xs, ALPHA, ps.bank("mix", layer, t, s), ALU.mult, ALU.add)\
                        .then_inc(ps.sem_taken("mix", layer, t, s), 1)
                for s in range(2):
                    eng.wait_ge(*ps.taken("mix", layer, t, s))
                layer_norm(t)

            def top16(rows, values, places):
                for row, v, _ in rows:
                    did(eng.max(v[:, 0:8], row))
                did.wait()
                for row, v, p in rows:
                    did(eng.max_index(p[:, 0:8], v[:, 0:8], row))
                did.wait()
                for row, v, _ in rows:
                    did(eng.match_replace(row, v[:, 0:8], row, -3.0e38))
                did.wait()
                for row, v, _ in rows:
                    did(eng.max(v[:, 8:16], row))
                did.wait()
                for row, v, p in rows:
                    did(eng.max_index(p[:, 8:16], v[:, 8:16], row))
                did.wait()

            def top(g, n):
                eng.wait_ge(*ps.taken("sc", g, n))
                top16([(sc[:, s * P:(s + 1) * P], topv[:, s * TOPK:(s + 1) * TOPK],
                        topi[:, s * TOPK:(s + 1) * TOPK]) for s in range(4 * n, 4 * n + 4)], None, None)

            def pairs(g):
                did(eng.tensor_copy(topf[:, :], topi[:, :]))
                tv = topv[:, :].rearrange("p (h c k) -> p h c k", h=HEADS, c=2)
                did(tt(qhT[:, :].rearrange("p (h i j) -> p h i j", h=HEADS, i=TOPK),
                       tv[:, :, 0, :].unsqueeze(3).to_broadcast([P, HEADS, TOPK, TOPK]),
                       tv[:, :, 1, :].unsqueeze(2).to_broadcast([P, HEADS, TOPK, TOPK]), ALU.add))
                did.wait()

            def best_of(g, n):
                wide = TOPK * TOPK
                top16([(qhT[:, h * wide:(h + 1) * wide], best[:, h * TOPK:(h + 1) * TOPK],
                        pos[:, h * TOPK:(h + 1) * TOPK]) for h in (2 * n, 2 * n + 1)], None, None)

            def gates(g):
                gt = gate[:, (g % 2) * P:(g % 2 + 1) * P].rearrange("p (h k) -> p h k", h=HEADS)
                b3 = best[:, :].rearrange("p (h k) -> p h k", h=HEADS)
                did(eng.tensor_copy(gden[:, 0:HEADS].unsqueeze(2), b3[:, :, 0:1]))
                did(eng.tensor_scalar(posc[:, 0:P], pos[:, :], 4, None, ALU.logical_shift_right))
                did(eng.tensor_scalar(posc[:, P:2 * P], pos[:, :], 15, None, ALU.bitwise_and))
                did.wait()
                tt(b3, b3, spread(gden[:, 0:HEADS], TOPK), ALU.subtract).then_inc(gx_in, 1)
                did(eng.tensor_copy(posf[:, :], posc[:, :]))
                eng.wait_ge(gx_out, g + 1)
                did(eng.tensor_reduce(gden[:, 0:HEADS], gt, AX_X, ALU.add))
                did.wait()
                did(eng.reciprocal(gden[:, HEADS:], gden[:, 0:HEADS]))
                did.wait()
                did(tt(gt, gt, spread(gden[:, HEADS:], TOPK), ALU.mult))
                did.wait()

            def experts(g, c):
                hot = sc[:, :].rearrange("p (h k i) -> p h k i", h=HEADS, k=TOPK)
                place = posf[:, c * P:(c + 1) * P].rearrange("p (h k) -> p h k", h=HEADS)
                names = topf[:, :].rearrange("p (h c k) -> p h c k", h=HEADS, c=2)[:, :, c, :]
                four = [P, HEADS, TOPK, TOPK]
                did(tt(hot, place.unsqueeze(3).to_broadcast(four),
                       iota16.unsqueeze(1).unsqueeze(1).to_broadcast(four), ALU.is_equal))
                did.wait()
                did(tt(hot, hot, names.unsqueeze(2).to_broadcast(four), ALU.mult))
                did.wait()
                did(eng.tensor_reduce(expert[:, c * P:(c + 1) * P].rearrange("p (h k) -> p h k", h=HEADS), hot,
                                      AX_X, ALU.add))
                did.wait()
                if c:
                    eng.scalar_tensor_tensor(idx[:, (g % 2) * P:(g % 2 + 1) * P], expert[:, 0:P], float(P),
                                             expert[:, P:2 * P], ALU.mult, ALU.add).then_inc(idx_ready, 1)

            def kv_slice(t, f, n):
                if n // 3 == 1:
                    return
                eng.wait_ge(*ps.taken("kvq", t, f, n))
                if t or f or n:
                    eng.wait_ge(roped, (t * 2 + f) * 6 + kq_turn(n))
                rot = heads4(kq_slot(n))[:, :, 0:32]
                halves = rot.rearrange("p h (a c) -> p h a c", a=2)
                four = [P, HALF, 2, 16]
                table = [consts[:, C_ROPE + (t * 2 + i) * 16:C_ROPE + (t * 2 + i + 1) * 16]
                         .unsqueeze(1).unsqueeze(1).to_broadcast(four) for i in range(2)]
                cos_part = rope[:, 0:P].rearrange("p (h a c) -> p h a c", h=HALF, a=2)
                sin_part = rope[:, P:2 * P].rearrange("p (h a c) -> p h a c", h=HALF, a=2)
                did(tt(cos_part, halves, table[0], ALU.mult))
                did(tt(sin_part, halves, table[1], ALU.mult))
                did.wait()
                did(tt(halves[:, :, 0, :], cos_part[:, :, 0, :], sin_part[:, :, 1, :], ALU.subtract))
                tt(halves[:, :, 1, :], cos_part[:, :, 1, :], sin_part[:, :, 0, :], ALU.add).then_inc(roped, 1)

            def soft(t, f, h):
                n = (t * 2 + f) * HALF + h
                wide = (t + 1) * P
                if n:
                    before = (t, f, h - 1) if h else ((t, f - 1, HALF - 1) if f else (t - 1, 1, HALF - 1))
                    eng.wait_ge(*ps.full("pT", *before))
                eng.wait_ge(*ps.full("score", t, f, h))
                scored = banks[:, 2 * SLICE:2 * SLICE + GROUPS * wide].rearrange("p (g k) -> p g k", g=GROUPS)
                masked3 = prob[:, 0:GROUPS * wide].rearrange("p (g k) -> p g k", g=GROUPS)
                eng.tensor_tensor_reduce(masked3, scored, attmask[:, :, SEQ - wide:], 1.0, 2.0 * NEG,
                                         ALU.add, ALU.max, mxs[:, 0:1]).then_inc(ps.sem_taken("score", t, f, h), 1)
                eng.wait_ge(*ps.taken("score", t, f, h))
                eng.tensor_scalar(mxs[:, 1:2], mxs[:, 0:1], -SCALE, None, ALU.mult).then_inc(nmx, 1)

            def weigh(t, f, h):
                n = (t * 2 + f) * HALF + h
                eng.wait_ge(p_done, n + 1)
                did(eng.reciprocal(mxs[:, 3:4], mxs[:, 2:3]))
                did.wait()
                if h == 0 and (t or f):
                    eng.wait_ge(*ps.full("aoT", *((t, 0) if f else (t - 1, 1))))
                eng.wait_ge(*ps.full("pv", t, f, h))
                eng.tensor_scalar(oh[:, h * P:(h + 1) * P], ps.bank("pv", t, f, h)[:, 0:P], mxs[:, 3:4], None,
                                  ALU.mult).then_inc(ps.sem_taken("pv", t, f, h), 1)

            def step(kind, a, b):
                if kind == "keys":
                    keys(a, b)
                elif kind == "scaled":
                    scaled(a, b)
                elif kind == "grams":
                    grams(a, b)
                elif kind == "masked":
                    masked(a, b)
                elif kind == "doubled":
                    doubled(a, b)
                elif kind == "carried":
                    carried(a)
                elif kind == "summed":
                    summed(a, b)
                elif kind == "gated":
                    gated(a, b)
                elif kind == "mixed":
                    mixed(a, b)
                elif kind == "top":
                    top(a, b)
                elif kind == "pairs":
                    pairs(a)
                elif kind == "best":
                    best_of(a, b)
                elif kind == "gates":
                    gates(a)
                elif kind == "experts":
                    experts(a, b)
                elif kind == "slice":
                    kv_slice(a, *b)
                elif kind == "soft":
                    soft(a, *b)
                elif kind == "weigh":
                    weigh(a, *b)

            def row(slot):
                return ring[:, slot * D:(slot + 1) * D]

            def dot_rows(g, blk, j):
                for s in range(RING):
                    eng.wait_ge(landed[s], 16 * (blk + 1))
                    c = j * RING + s
                    eng.tensor_tensor_reduce(row(s), row(s), xtile(g % 2), 1.0, 0.0, ALU.mult, ALU.add,
                                             dots[:, c:c + 1]).then_inc(ring_used, 1)

            def add_rows(g, h, blk, j):
                turn = 2 * (HEADS * g + h) + j + 1
                cols = slice(j * RING, (j + 1) * RING)
                eng.wait_ge(gelu_done, turn)
                first = (g % 2) * P + h * TOPK + j * RING
                tt(wts[:, cols], gel[:, cols], gate[:, bass.ds(first, RING)], ALU.mult).then_inc(wts_ready, 1)
                eng.wait_ge(wts_ready, turn)
                for s in range(RING):
                    eng.wait_ge(landed[s], 16 * (blk + 1))
                    eng.wait_ge(ring_used, RING * (blk + 1) + s - 1)
                    a = acc[:, (s % 2) * D:(s % 2 + 1) * D]
                    c = j * RING + s
                    eng.scalar_tensor_tensor(a, row(s), wts[:, c:c + 1], a, ALU.mult, ALU.add)\
                        .then_inc(ring_used, 1)

            for n in range(2):
                did(eng.memset(conv_rows(n)[:, :, 0:CONV - 1], 0.0))
            did.wait()
            eng.memset(gden[:, :], 0.0).then_inc(zero_ok, 1)
            eng.wait_ge(zero_ok, 1)
            eng.memset(gden[:, :], 0.0).then_inc(ring_used, RING)
            eng.wait_ge(*ps.taken("convw"))
            for n in range(12):
                eng.wait_ge(*ps.taken("qkv", n))
                for j in range(CONV - 1, -1, -1):
                    for b in range(2):
                        blk = 2 * n + b
                        out = qkvT[:, blk * SEQ:(blk + 1) * SEQ]
                        src = conv_rows(n)[:, b, j:j + SEQ]
                        w = cw[:, j * 24 + blk:j * 24 + blk + 1]
                        if j == CONV - 1:
                            did(eng.tensor_scalar(out, src, w, None, ALU.mult))
                        else:
                            ins = eng.scalar_tensor_tensor(out, src, w, out, ALU.mult, ALU.add)
                            if j == 0 and b == 1:
                                ins.then_inc(sil_in, 1)
                            else:
                                did(ins)
                    if j:
                        did.wait()

            eng.wait_ge(*ps.full("ab"))
            eng.tensor_copy(ab[:, :], ps.bank("ab")[:, 0:TILES * 16]).then_inc(ps.sem_taken("ab"), 1)
            eng.wait_ge(*ps.taken("ab"))
            ab3 = ab[:, :].rearrange("p (t c) -> p t c", t=TILES)
            small = [gtmp[:, 16 * i:16 * i + 16] for i in range(3)]
            u3 = small[0].rearrange("p (t h) -> p t h", t=TILES)
            did(tt(u3, ab3[:, :, 0:HEADS], dtb[:, :].unsqueeze(1).to_broadcast([P, TILES, HEADS]), ALU.add))
            did(eng.tensor_copy(small[2].rearrange("p (t h) -> p t h", t=TILES), ab3[:, :, HEADS:16]))
            did.wait()
            did(eng.tensor_scalar(small[1], small[0], -1.0, None, ALU.mult))
            did.wait()
            tt(small[1], small[0], small[1], ALU.min).then_inc(sm_in, 1)
            did(eng.tensor_scalar(small[0], small[0], 0.0, None, ALU.max))
            did.wait()
            eng.wait_ge(sm_out, 1)
            did(tt(small[0], small[0], small[1], ALU.add))
            did(eng.tensor_scalar(small[2], small[2], 1.0, None, ALU.add))
            did.wait()
            did(eng.scalar_tensor_tensor(u3, u3, -1.0, alog[:, :].unsqueeze(1).to_broadcast([P, TILES, HEADS]),
                                         ALU.mult, ALU.mult))
            did(eng.reciprocal(beta[:, :], small[2]))
            did.wait()
            eng.tensor_copy(glog[:, :], small[0]).then_inc(g_ready, 1)
            eng.wait_ge(*ps.full("gcum"))
            eng.tensor_copy(gcum[:, :], ps.bank("gcum")[:, 0:TILES * HEADS]).then_inc(ps.sem_taken("gcum"), 1)
            for n in range(4):
                eng.wait_ge(*ps.taken("z", n))
            for t in range(TILES):
                z3 = zs[:, t * D:(t + 1) * D].rearrange("p (h d) -> p h d", h=HEADS)
                did(tt(z3, z3, normw[:, :].unsqueeze(1).to_broadcast([P, HEADS, P]), ALU.mult))
            did.wait()
            eng.wait_ge(sm_out, 2)
            eng.wait_ge(*ps.taken("gcum"))

            for st in delta_steps(0) + head_steps(0):
                step(*st)
            for g in range(4):
                did(eng.memset(acc[:, :], 0.0))
                did.wait()
                if g < 3:
                    for b, steps in enumerate(gather_steps(beside[g]) + [[]] * 4):
                        blk, h = BLOCKS * g + b, b // 4
                        if b % 4 < 2:
                            dot_rows(g, blk, b % 4)
                        else:
                            add_rows(g, h, blk, b % 4 - 2)
                        for st in steps:
                            step(*st)
                else:
                    with eng.Fori(0, HEADS) as h:
                        for b in range(4):
                            blk = BLOCKS * g + 4 * h + b
                            if b < 2:
                                dot_rows(g, blk, b)
                            else:
                                add_rows(g, h, blk, b - 2)
                eng.wait_ge(ring_used, RING * (BLOCKS * (g + 1) + 1))
                xt = xtile(g % 2)
                did(eng.scalar_tensor_tensor(xt, xt, ALPHA, acc[:, 0:D], ALU.mult, ALU.add))
                did.wait()
                did(tt(xt, xt, acc[:, D:2 * D], ALU.add))
                did.wait()
                layer_norm(g % 2)


def constants():
    import numpy as np

    c = np.zeros((P, C_ALL), np.float32)
    i, j = np.arange(P)[:, None], np.arange(P)[None, :]
    c[:, C_ID:C_ID + P] = i == j
    c[:, C_TRI:C_TRI + P] = i <= j
    c[:, C_NEG:C_NEG + P] = np.where(j >= i, 0.0, NEG)
    for s in range(LEVELS):
        w = 1 << s
        low_left = (i // (2 * w) == j // (2 * w)) & (i % (2 * w) >= w) & (j % (2 * w) < w)
        c[:, C_LVL + s * P:C_LVL + (s + 1) * P] = -1.0 * low_left
    rel = P + i - np.arange(SEQ)[None, :]
    for g, (window, dilation) in enumerate(((128, 1), (512, 4), (2048, 16))):
        ok = (rel >= 0) & (rel % dilation == 0) & (rel <= window)
        c[:, C_ATT + g * SEQ:C_ATT + (g + 1) * SEQ] = np.where(ok, 0.0, NEG)
    inv = np.float32(500000.0) ** (-np.arange(16, dtype=np.float32) * np.float32(2.0) / np.float32(32))
    for t in range(TILES):
        ang = (np.arange(P, dtype=np.float32) + t * P)[:, None] * inv.astype(np.float32)[None, :]
        c[:, C_ROPE + 32 * t:C_ROPE + 32 * t + 16] = np.cos(ang)
        c[:, C_ROPE + 32 * t + 16:C_ROPE + 32 * t + 32] = np.sin(ang)
    c[:, C_IOTA:C_IOTA + 16] = np.arange(16)[None, :]
    return c


def kernel(**inputs):
    import numpy as np
    import concourse.bacc as bacc
    from concourse.bass_utils import run_bass_kernel_spmd

    nc = bacc.Bacc("TRN2", target_bir_lowering=False, num_devices=1)
    shapes = {
        "x": (SEQ, D), "dn_w_in": (D, 4 * D + 16), "dn_conv": (CONV, 3 * D), "dn_a_log": (1, HEADS),
        "dn_dt_bias": (1, HEADS), "dn_norm_w": (1, P), "dn_w_out": (D, D), "shared_w_kv": (D, 6 * D),
        "attn_w_q": (D, 3 * D), "attn_w_out": (D, D), "peer_w_query": (2, D, 2 * D),
        "peer_sub_keys": (2, 16, P, P), "peer_u": (2 * P * P, D), "peer_v": (2 * P * P, D),
        "ln_mix_g": (2, D), "ln_mix_b": (2, D), "ln_ffn_g": (2, D), "ln_ffn_b": (2, D),
    }
    arrays, aps = {}, {}
    for name, shape in shapes.items():
        a = np.ascontiguousarray(inputs[name]).reshape(shape)
        parts = {name: a}
        if name in ("peer_u", "peer_v"):
            parts = {f"{name}_{i}": a[i * P * P:(i + 1) * P * P] for i in range(2)}
        for key, value in parts.items():
            arrays[key] = value
            aps[key] = nc.dram_tensor(key, value.shape, mybir.dt.from_np(value.dtype), kind="ExternalInput").ap()
    arrays["constants"] = constants()
    const_ap = nc.dram_tensor("constants", (P, C_ALL), F32, kind="ExternalInput").ap()
    out = nc.dram_tensor("out", (SEQ, D), F32, kind="ExternalOutput").ap()
    sub_keys = [aps["peer_sub_keys"][i].rearrange("s k d -> k s d") for i in range(2)]
    yoco_deltanet_dilated_peer(
        nc, aps["x"], aps["dn_w_in"], aps["dn_conv"], aps["dn_a_log"], aps["dn_dt_bias"], aps["dn_norm_w"],
        aps["dn_w_out"], aps["shared_w_kv"], aps["attn_w_q"], aps["attn_w_out"],
        [aps["peer_w_query"][i] for i in range(2)], sub_keys,
        [aps[f"peer_u_{i}"][:, :] for i in range(2)], [aps[f"peer_v_{i}"][:, :] for i in range(2)],
        aps["ln_mix_g"], aps["ln_mix_b"], aps["ln_ffn_g"], aps["ln_ffn_b"], const_ap, out)
    r = run_bass_kernel_spmd(nc, [arrays], core_ids=[0])
    return r.results[0]["out"].reshape(1, SEQ, D)
```

```python
from contextlib import ExitStack

import concourse.bass as bass
from concourse import mybir

F32 = mybir.dt.float32
U32 = mybir.dt.uint32
ALU = mybir.AluOpType
ACT = mybir.ActivationFunctionType
AX_X = mybir.AxisListType.X

P = 128
SEQ, D = 256, 1024
TILES = SEQ // P
KB = D // P
HEADS = 8
HALF = HEADS // 2
GROUPS = 3
TOPK = 16
CONV = 4
ALPHA = 4.0 ** 0.25
LN_EPS = 1e-5
NORM_EPS = 1e-6
SCALE = float(P) ** -0.5
NEG = -1e30
LEVELS = 7
RING = 8
BLOCKS = 4 * HEADS
WSLOTS = 2
SLICE = 512

C_ID = 0
C_TRI = C_ID + P
C_NEG = C_TRI + P
C_LVL = C_NEG + P
C_ATT = C_LVL + LEVELS * P
C_ROPE = C_ATT + GROUPS * SEQ
C_IOTA = C_ROPE + TILES * 2 * 16
C_ALL = C_IOTA + 16

SMALL_LOADS = 6


def qkv_blocks(n):
    first = (8, 10, 0, 2, 12, 14, 4, 6)[n] if n < 8 else 2 * n
    return first, first + 1


def level_steps(t, beside):
    out = []
    for s in range(1, LEVELS):
        out += [("masked", t, s)] + [(kind, n, 0) for kind, n in beside.get(s, [])] + [("doubled", t, s)]
        if s == 4:
            out += [("values", t, 0)]
    return out


def delta_end(t):
    return ([("carried", t, 0)] if t else []) + [("summed", t, f) for f in range(2)] \
        + [("gated", t, f) for f in range(2)]


def opening_steps():
    def qkv(*ns):
        return [("qkv", n, 0) for n in ns]

    out = [("inputs", 0, 0)] + qkv(0, 1) + [("decays", 0, 0)] + qkv(2, 3, 4) + [("keys", 0, 0)] + qkv(5, 6)
    out += [("scaled", 0, 0)] + qkv(7, 8) + [("keys", 0, 1), ("grams", 0, 0)] + qkv(9)
    out += [("scaled", 0, 1)] + qkv(10) + [("grams", 0, 1), ("started", 0, 0)]
    out += level_steps(0, {1: [("qkv", 11)], 2: [("z", 0)], 3: [("z", 1)], 5: [("z", 2)], 6: [("z", 3)]})
    return out + delta_end(0) + [("mixed", 0, 0), ("scores", 0, 0)] + choice_steps(0, 0)


def choice_steps(g, n):
    return [(kind, g, n) for kind in ("top", "best", "gates", "experts")]


def attend_steps(t):
    out = [("x2", t, 0)]
    for f in range(2):
        out += [("slice", t, (f, n)) for n in range(9)]
        for h in range(HALF):
            out += [("soft", t, (f, h)), ("weigh", t, (f, h))]
        out += [("heads", t, f)]
    return out


def gather_steps(g):
    placed = []

    def chain(steps, first, last):
        weight = [0.45 if st[0] in ("soft", "weigh", "heads") else 1.0 for st in steps]
        total = sum(weight[1:]) or 1.0
        at = first
        for i, st in enumerate(steps):
            at += weight[i] * (last - first) / total if i else 0.0
            placed.append((at, st))

    chain([("scores", g, n) for n in range(1, 4)], *SCORES_AT)
    for n in range(1, 4):
        chain(choice_steps(g, n), 8 * n - 7 + (n == 1), 8 * n - 3)
    if g < 3:
        if g == 0:
            chain([("keys", 1, 0), ("keys", 1, 1), ("scaled", 1, 0), ("scaled", 1, 1), ("grams", 1, 0),
                   ("grams", 1, 1), ("started", 1, 0)] + level_steps(1, {}) + delta_end(1), *DELTA_AT)
        else:
            chain(attend_steps(g - 1), *ATTEND_AT)
        chain([("mixed", min(g, 1), (g + 1) % 2)], MIXED_AT, MIXED_AT)
        chain([("scores", g + 1, 0)] + choice_steps(g + 1, 0), *NEXT_AT)
    out = [[] for _ in range(BLOCKS)]
    for at, st in sorted(placed, key=lambda p: p[0]):
        out[int(at)].append(st)
    return out


SCORES_AT = (0.5, 2.5)
DELTA_AT = (3.0, 24.5)
ATTEND_AT = (3.5, 25.5)
MIXED_AT = 27.5
NEXT_AT = (29.6, 31.7)


def all_steps():
    return opening_steps() + [st for g in range(4) for steps in gather_steps(g) for st in steps]


def fills(kind, a, b):
    if kind == "inputs":
        return ([(("x0T", t, i), 2 * t + i, 1) for t in range(TILES) for i in range(2)]
                + [(("convw",), 4, 1), (("ab",), 5, 1)])
    if kind == "decays":
        return [(("gcum",), 5, 1)]
    if kind in ("qkv", "z"):
        return [((kind, a), a % 2, 1)]
    if kind == "keys":
        return [(("kt", a, b), 2 + b, 2), (("qt", a, b), 6 + b, 1), (("gB", a, b), 4 + b, 1)]
    if kind == "grams":
        return [(("kbT", a, b), 4 + b, 1), (("A", a, b), 6 + b, 1), (("M", a, b), 2 + b, 1)]
    if kind == "started":
        return [(("T", a, 0, f), 4 + f, 1) for f in range(2)]
    if kind == "masked":
        return [(("Y", a, b, f), 2 + f, 1) for f in range(2)]
    if kind == "doubled":
        return ([(("ZT", a, b, f), 6 + f, 1) for f in range(2)]
                + [(("T", a, b, f), 4 + f, 1) for f in range(2) if b < LEVELS - 1])
    if kind == "values":
        return [(("vt", a, f), 2 + f, 1) for f in range(2)]
    if kind == "carried":
        return [(("kS", a, f), 2 + f, 1) for f in range(2)] + [(("qS", a, f), 6 + f, 1) for f in range(2)]
    if kind == "summed":
        return [(("vn", a, b), 4 + b, 1), (("o", a, b), 6 + b, 1)] + ([] if a else [(("S", a, b), 2 + b, 1)])
    if kind == "gated":
        return [(("oT", a, b), 4 + b, 1)]
    if kind == "mixed":
        return ([(("mix", a, b, n), n, 1) for n in range(2)] + [(("x1T", a, b, n), 2 + n, 1) for n in range(2)])
    if kind == "scores":
        first = [(("skT", a // 2, i), 4 + i, 1) for i in range(4)] if a % 2 == 0 and b == 0 else []
        return first + [(("query", a, b), b % 2, 1), (("sc", a, b), 2 + b % 2, 1)]
    if kind == "x2":
        return [(("x2T", a, n), 2 + n, 1) for n in range(2)]
    if kind == "slice":
        f, n = b
        out = [(("kvq", a, f, n), n % 2, 1)]
        return out + [(("kqT", a, f, m), 6 + m % 2, 1) for m in late_slices(n)]
    if kind == "soft":
        return [(("score", a, *b), 2, 1), (("pT", a, *b), 4, 1)]
    if kind == "weigh":
        return [(("pv", a, *b), 6, 1)]
    if kind == "heads":
        return [(("aoT", a, b), 7, 1)]
    return []


def late_slices(n):
    return [m for m in ([n - 1] if n else []) + ([8] if n == 8 else []) if m // 3 != 1]


class Psum:

    def __init__(self, banks, full, taken):
        self.banks, self.full_sem, self.taken_sem = banks, full, taken
        self.at = {}
        filled, taken_count = [0] * 8, [0] * 8
        for step in all_steps():
            for key, bank, releases in fills(*step):
                before = taken_count[bank]
                filled[bank] += 1
                taken_count[bank] += releases
                self.at[key] = (bank, filled[bank], before, taken_count[bank])

    def bank(self, *key):
        b = self.at[key][0]
        return self.banks[:, b * SLICE:(b + 1) * SLICE]

    def full(self, *key):
        b, n, _, _ = self.at[key]
        return self.full_sem[b], n

    def taken(self, *key):
        b, _, _, n = self.at[key]
        return self.taken_sem[b], n

    def sem_full(self, *key):
        return self.full_sem[self.at[key][0]]

    def sem_taken(self, *key):
        return self.taken_sem[self.at[key][0]]

    def free(self, eng, *key):
        b, _, before, _ = self.at[key]
        if before:
            eng.wait_ge(self.taken_sem[b], before)


def step_weights(kind, a, b):
    if kind in ("qkv", "z") and a % 2 == 0:
        return [(kind, a // 2)]
    if kind == "scores":
        return ([("sk", a // 2)] if a % 2 == 0 and b == 0 else []) + [("query", a, b)]
    if kind == "slice":
        return [("kvq", a, *b)]
    if kind == "mixed":
        return [("mix", a, b, n) for n in range(2)]
    return []


def last_reader(key):
    if key[0] in ("qkv", "z"):
        return (key[0], 2 * key[1] + 1)
    if key[0] == "sk":
        return ("skT", key[1], 3)
    return key


def norm_order():
    return [("mix", 0, 0), ("mix", 0, 1), ("ffn", 0, 0), ("mix", 1, 0), ("ffn", 0, 1), ("mix", 1, 1),
            ("ffn", 1, 0), ("ffn", 1, 1)]


class Steps:

    def __init__(self, eng, sem):
        self.eng, self.sem, self.n = eng, sem, 0

    def __call__(self, ins):
        self.n += 1
        return ins.then_inc(self.sem, 1)

    def wait(self):
        self.eng.wait_ge(self.sem, self.n)


def yoco_deltanet_dilated_peer(nc, x_d, w_in, conv_d, alog_d, dtb_d, normw_d, w_out, w_kv, w_q, a_out,
                               w_query, sub_keys, u_tab, v_tab, gmix, bmix, gffn, bffn, const_d, out_d):
    with ExitStack() as ctx:
        def sb(name, cols, dt=F32):
            return ctx.enter_context(nc.sbuf_tensor(name, [P, cols], dt))

        def sem(name):
            return ctx.enter_context(nc.semaphore(name))

        ring = sb("ring", RING * D)
        wbuf = sb("wbuf", WSLOTS * KB * SLICE)
        x = sb("x_rows", TILES * D)
        xT = sb("xT", KB * SEQ)
        skT = sb("skT", 16 * P)
        consts = sb("consts", C_ALL)
        gb = sb("gb", 2 * D)
        acc = sb("acc", 2 * D)
        choice = sb("choice", 8 * SLICE)
        qhT = choice[:, 0:2 * SLICE]
        sc = choice[:, 2 * SLICE:6 * SLICE]
        cand = choice[:, 6 * SLICE:7 * SLICE]
        hot = choice[:, 7 * SLICE:8 * SLICE]
        raw = choice[:, 2 * SLICE:2 * SLICE + 2 * 2 * (SEQ + CONV - 1)]
        topv = sb("topv", 16 * TOPK)
        topi = sb("topi", 16 * TOPK, U32)
        topf = sb("topf", 16 * TOPK)
        best = sb("best", P)
        pos = sb("pos", P, U32)
        posf = sb("posf", 2 * P)
        expert = sb("expert", 2 * P)
        posc = expert[:, :].bitcast(U32)
        idx = sb("idx", 2 * P, U32)
        stage = sb("stage", 2 * TOPK, U32)
        gate = sb("gate", 2 * P)
        gden = sb("gden", 2 * HEADS)
        dots = sb("dots", TOPK)
        gel = sb("gel", TOPK)
        wts = sb("wts", TOPK)
        ab = sb("ab", TILES * 16)
        alog = sb("alog", HEADS)
        dtb = sb("dtb", HEADS)
        normw = sb("normw", P)
        cw = sb("cw", 24 * CONV)
        glog = sb("glog", TILES * HEADS)
        gtmp = sb("gtmp", 3 * TILES * HEADS)
        beta = sb("beta", TILES * HEADS)
        gcum = sb("gcum", TILES * HEADS)
        egc = sb("egc", TILES * HEADS)
        decl = sb("decl", HEADS)
        ss = sb("ss", 16)
        c_state = sb("c_state", HEADS)
        c_query = sb("c_query", HEADS)
        c_carry = sb("c_carry", HEADS)
        coef = sb("coef", HEADS)
        rs_in = sb("rs_in", 16)
        rs_y = sb("rs_y", 16)
        rs_t = sb("rs_t", 16)
        rqk = sb("rqk", 16)
        bn = sb("bn", 2 * 6)
        mv = sb("mv", 2)
        mxs = sb("mxs", 4)
        arena = sb("arena", 17 * D)

        def part(first, cols):
            return arena[:, first:first + cols]

        qkvT = part(0, 24 * SEQ)
        zs = part(6 * D, 2 * D)
        dec = part(8 * D, D)
        Ybuf = dec
        MT = part(9 * D, D)
        AT = part(10 * D, D)
        Tm = part(11 * D, D)
        oT = Tm
        TT = part(12 * D, D)
        vb = part(13 * D, D)
        kb = part(14 * D, D)
        vn = kb
        kbT = part(15 * D, D)
        od = kbT
        S1 = part(16 * D, D)
        kS = acc[:, 0:D]
        cw_in = acc[:, D:D + P]
        wab = acc[:, D + P:D + 2 * P]
        kT0 = part(0, 24 * P)
        v0 = part(3 * D, 24 * P)
        kT1 = part(6 * D, 12 * P)
        v1 = part(7 * D + 512, 12 * P)
        qT = part(9 * D, 12 * P)
        kq = part(10 * D + 512, 2 * SLICE)
        rope = part(11 * D + 512, 2 * P)
        prob = part(12 * D, GROUPS * SEQ)
        probT = part(13 * D, GROUPS * SEQ)
        oh = part(14 * D, HALF * P)
        oaT = part(15 * D, D)

        banks = ctx.enter_context(nc.psum_tensor("banks", [P, 8 * SLICE], F32))
        full = [sem(f"bank{b}_full") for b in range(8)]
        taken = [sem(f"bank{b}_taken") for b in range(8)]
        ps = Psum(banks, full, taken)

        loaded = sem("tokens_loaded")
        loaded_small = sem("small_inputs_loaded")
        w_land = [sem(f"weights{i}_landed") for i in range(WSLOTS)]
        gb_land = sem("norm_rows_landed")
        landed = [sem(f"row{i}_landed") for i in range(RING)]
        ring_used = sem("rows_used")
        staged = sem("indices_staged")
        gelu_done = sem("gelu_done")
        wts_ready = sem("weights_of_rows_ready")
        idx_ready = sem("indices_ready")
        vec = sem("vector_step")
        act = sem("scalar_step")
        rs_asked = sem("rsqrt_asked")
        rs_said = sem("rsqrt_said")
        sil_in = sem("conv_done")
        sil_out = sem("silu_done")
        zero_ok = sem("raw_zeroed")
        g_ready = sem("log_decay_ready")
        sm_in = sem("small_in")
        sm_out = sem("small_out")
        dec_in = sem("decay_exponent_ready")
        dec_out = sem("decay_ready")
        sq_o = sem("squares_done")
        od_ready = sem("delta_output_ready")
        vb_ready = sem("delta_targets_ready")
        od_sum = sem("delta_output_summed")
        tt_ready = sem("inverse_started")
        x_ready = sem("x_normed")
        gx_in = sem("gate_exponent_ready")
        gx_out = sem("gate_exp_done")
        roped = sem("roped")
        p_done = sem("probabilities_done")
        nmx = sem("negated_max_ready")
        stored = sem("output_stored")

        ident = consts[:, C_ID:C_ID + P]
        tri = consts[:, C_TRI:C_TRI + P]
        negmask = consts[:, C_NEG:C_NEG + P]
        attmask = consts[:, C_ATT:C_ATT + GROUPS * SEQ].rearrange("p (g k) -> p g k", g=GROUPS)
        iota16 = consts[:, C_IOTA:C_IOTA + 16]

        slices = [key for st in all_steps() for key in step_weights(*st)]
        slot_of = {key: n for n, key in enumerate(slices)}

        def weights(*key):
            s = slot_of[key] % WSLOTS
            return wbuf[:, s * KB * SLICE:(s + 1) * KB * SLICE].rearrange("p (k n) -> p k n", k=KB)

        def heads4(ap):
            return ap.rearrange("p (h d) -> p h d", h=HALF)

        def half(ap, f):
            return ap[:, f * HALF * P:(f + 1) * HALF * P]

        def xtile(t):
            return x[:, t * D:(t + 1) * D]

        def xTb(k, t):
            return xT[:, k * SEQ + t * P:k * SEQ + (t + 1) * P]

        def channels(blk, t):
            return qkvT[:, blk * SEQ + t * P:blk * SEQ + (t + 1) * P]

        def spread(cols, n=P):
            return cols.unsqueeze(2).to_broadcast([P, cols.shape[1], n])

        def kq_turn(n):
            return n if n < 3 else n - 3

        def kq_slot(n):
            s = kq_turn(n) % 2
            return kq[:, s * SLICE:(s + 1) * SLICE]

        def tile_heads(first, second, t, kt, f, grp, h, n):
            buf, at = (first, grp * HEADS + f * HALF + h) if kt == 0 else (second, grp * HALF + h)
            return buf[:, at * P:(at + n) * P]

        def k_heads(t, kt, f, grp, h, n):
            return tile_heads(kT0, kT1, t, kt, f, grp, h, n)

        def v_heads(t, kt, f, grp, h, n):
            return tile_heads(v0, v1, t, kt, f, grp, h, n)

        def conv_rows(n):
            s = n % 2
            w = SEQ + CONV - 1
            return raw[:, s * 2 * w:(s + 1) * 2 * w].rearrange("p (b k) -> p b k", b=2)

        norms = norm_order()
        block = ctx.enter_context(nc.Block())

        @block.sync
        def _(eng):
            eng.dma_start(consts[:, C_ID:C_ID + P], const_d[:, C_ID:C_ID + P]).then_inc(loaded, 16)
            for t in range(TILES):
                eng.dma_start(xtile(t), x_d[t * P:(t + 1) * P, :]).then_inc(loaded, 16)

            def small_loads():
                eng.dma_start(cw_in[0:24 * CONV, :], conv_d.rearrange("j (b p) -> (j b) p", p=P))\
                   .then_inc(loaded_small, 16)
                eng.dma_start(wab[:, :].rearrange("p (k n) -> p k n", k=KB),
                              w_in.rearrange("(k p) n -> p k n", p=P)[:, :, 4 * D:4 * D + 16])\
                   .then_inc(loaded_small, 16)
                eng.dma_start(alog[:, :], alog_d.to_broadcast([P, HEADS])).then_inc(loaded_small, 16)
                eng.dma_start(dtb[:, :], dtb_d.to_broadcast([P, HEADS])).then_inc(loaded_small, 16)
                eng.dma_start(normw[:, :], normw_d.to_broadcast([P, P])).then_inc(loaded_small, 16)
                eng.dma_start(consts[:, C_TRI:C_ALL], const_d[:, C_TRI:C_ALL]).then_inc(loaded_small, 16)

            def view(key):
                def cols(w, c):
                    return w.rearrange("(k p) n -> p k n", p=P)[:, :, c:c + SLICE]

                if key[0] == "qkv":
                    return cols(w_in, qkv_blocks(2 * key[1])[0] * P)
                if key[0] == "z":
                    return cols(w_in, 3 * D + key[1] * SLICE)
                if key[0] == "mix":
                    return cols((w_out, a_out)[key[1]], key[3] * SLICE)
                if key[0] == "query":
                    return cols(w_query[key[1] // 2], key[2] * SLICE)
                if key[0] == "sk":
                    return sub_keys[key[1]]
                what, grp = divmod(key[3], 3)
                return cols(w_kv if what < 2 else w_q,
                            (what * GROUPS * D if what < 2 else 0) + grp * D + key[2] * SLICE)

            def load_weights(key):
                n = slot_of[key]
                if n >= WSLOTS:
                    eng.wait_ge(*ps.full(*last_reader(slices[n - WSLOTS])))
                slot = wbuf[:, (n % WSLOTS) * KB * SLICE:(n % WSLOTS + 1) * KB * SLICE]
                if key[0] == "sk":
                    eng.dma_start(slot[:, 0:16 * P].rearrange("p (s d) -> p s d", s=16), view(key))\
                       .then_inc(w_land[n % WSLOTS], 16)
                else:
                    eng.dma_start(slot.rearrange("p (k n) -> p k n", k=KB), view(key))\
                       .then_inc(w_land[n % WSLOTS], 16)

            def load_norm(i):
                which, layer, _ = norms[i]
                if i:
                    eng.wait_ge(x_ready, i)
                g, b = (gmix, bmix) if which == "mix" else (gffn, bffn)
                eng.dma_start(gb[:, 0:D], g[layer:layer + 1, :].to_broadcast([P, D])).then_inc(gb_land, 16)
                eng.dma_start(gb[:, D:2 * D], b[layer:layer + 1, :].to_broadcast([P, D])).then_inc(gb_land, 16)

            def step_loads(st):
                for key in step_weights(*st):
                    load_weights(key)
                    if key == ("qkv", 0):
                        small_loads()
                if st[0] == "mixed":
                    load_norm(norms.index(("mix", st[1], st[2])))

            for st in opening_steps():
                step_loads(st)
            for g in range(4):
                for steps in gather_steps(g):
                    for st in steps:
                        step_loads(st)
                load_norm(norms.index(("ffn", g // 2, g % 2)))
            for t in range(TILES):
                eng.wait_ge(x_ready, 4 + 2 + t + 1)
                eng.dma_start(out_d[t * P:(t + 1) * P, :], xtile(t)).then_inc(stored, 16)
            eng.wait_ge(stored, 16 * TILES)

        @block.gpsimd
        def _(eng):
            for g in range(4):
                table = (u_tab[g // 2], v_tab[g // 2])
                with eng.Fori(0, HEADS // 2) as r:
                    eng.wait_ge(idx_ready, 4 * g + r + 1)
                    eng.nop(nofuse=True)
                    for par in range(2):
                        h = 2 * r + par
                        copies = HEADS * g + h
                        eng.wait_ge(ring_used, RING * (BLOCKS * g + 4 * h) + 1)
                        eng.tensor_copy(stage[:, par * TOPK:(par + 1) * TOPK],
                                        idx[:, bass.ds((g % 2) * P + TOPK * h, TOPK)]).then_inc(staged, 1)
                        eng.wait_ge(staged, copies + 1)
                        for side in range(2):
                            for j in range(TOPK):
                                slot = j % RING
                                blk = BLOCKS * g + 4 * h + 2 * side + j // RING
                                eng.wait_ge(ring_used, RING * blk + slot + 1)
                                eng.nop(nofuse=True)
                                eng.indirect_dma_start(
                                    ring[:, slot * D:(slot + 1) * D], None, table[side],
                                    bass.IndirectOffsetOnAxis(ap=stage[:, par * TOPK + j:par * TOPK + j + 1],
                                                              axis=0)).then_inc(landed[slot], 16)

        @block.tensor
        def _(eng):
            def transposes(key, sources):
                ps.free(eng, *key)
                bank = ps.bank(*key)
                for i, src in enumerate(sources):
                    rows = src.shape[0]
                    ins = eng.transpose(bank[:, i * P:i * P + rows], src, ident[0:rows, 0:rows])
                ins.then_inc(ps.sem_full(*key), 1)

            def products(key, pairs, cols=P, wait_free=True):
                if wait_free:
                    ps.free(eng, *key)
                bank = ps.bank(*key)
                for i, terms in enumerate(pairs):
                    for n, (a, b) in enumerate(terms):
                        ins = eng.matmul(bank[:, i * cols:(i + 1) * cols], lhsT=a, rhs=b,
                                         start=n == 0, stop=n == len(terms) - 1)
                ins.then_inc(ps.sem_full(*key), 1)

            def weights_here(*key):
                n = slot_of[key]
                eng.wait_ge(w_land[n % WSLOTS], 16 * (n // WSLOTS + 1))
                return weights(*key)

            def x_transposed(key, t):
                for n in range(2):
                    transposes(key + (n,), [xtile(t)[:, (4 * n + i) * P:(4 * n + i + 1) * P] for i in range(4)])

            def heads_of(f):
                return range(f * HALF, (f + 1) * HALF)

            def head(buf, h):
                return buf[:, h * P:(h + 1) * P]

            def inputs():
                eng.wait_ge(loaded, 16 * (TILES + 1))
                for t in range(TILES):
                    x_transposed(("x0T", t), t)
                eng.wait_ge(loaded_small, 16 * SMALL_LOADS)
                transposes(("convw",), [cw_in[0:24 * CONV, :]])
                for t in range(TILES):
                    for n in range(2):
                        eng.wait_ge(*ps.taken("x0T", t, n))
                products(("ab",), [[(xTb(k, t), wab[:, k * 16:(k + 1) * 16]) for k in range(KB)]
                                   for t in range(TILES)], 16)

            def decays():
                eng.wait_ge(g_ready, 1)
                products(("gcum",), [[(tri, glog[:, :])]], TILES * HEADS)

            def qkv(n):
                w = weights_here("qkv", n // 2)
                products(("qkv", n), [[(w[:, k, c * P:(c + 1) * P], xT[:, k * SEQ:(k + 1) * SEQ])
                                       for k in range(KB)] for c in (2 * (n % 2), 2 * (n % 2) + 1)], SEQ)

            def z(n):
                w = weights_here("z", n // 2)
                products(("z", n), [[(xTb(k, n % 2), w[:, k, :]) for k in range(KB)]], SLICE)

            def keys(t, f):
                if t == 0:
                    eng.wait_ge(sil_out, 4 * f + 4)
                transposes(("kt", t, f), [channels(8 + h, t) for h in heads_of(f)])
                transposes(("qt", t, f), [channels(h, t) for h in heads_of(f)])
                if t == 0 and f == 0:
                    eng.wait_ge(g_ready, 1)
                products(("gB", t, f), [[(glog[:, t * HEADS + h:t * HEADS + h + 1].to_broadcast([P, P]), tri)]
                                        for h in heads_of(f)])

            def grams(t, f):
                eng.wait_ge(*ps.taken("kt", t, f))
                transposes(("kbT", t, f), [head(kb, h) for h in heads_of(f)])
                products(("A", t, f), [[(channels(8 + h, t), channels(h, t))] for h in heads_of(f)])
                eng.wait_ge(*ps.taken("kbT", t, f))
                products(("M", t, f), [[(channels(8 + h, t), head(kbT, h))] for h in heads_of(f)])

            def inverse_transposed(t, s):
                for f in range(2):
                    if s:
                        eng.wait_ge(*ps.taken("ZT", t, s, f))
                    else:
                        eng.wait_ge(tt_ready, 2 * t + f + 1)
                    transposes(("T", t, s, f), [head(TT, h) for h in heads_of(f)])

            def masked(t, s):
                for f in range(2):
                    eng.wait_ge(*ps.taken("T", t, s - 1, f))
                    products(("Y", t, s, f), [[(head(MT, h), head(Tm, h))] for h in heads_of(f)])

            def doubled(t, s):
                for f in range(2):
                    eng.wait_ge(*ps.taken("Y", t, s, f))
                    products(("ZT", t, s, f), [[(head(Ybuf, h), head(TT, h))] for h in heads_of(f)])
                if s < LEVELS - 1:
                    inverse_transposed(t, s)

            def values(t):
                if t == 0:
                    eng.wait_ge(sil_out, 12)
                for f in range(2):
                    transposes(("vt", t, f), [channels(16 + h, t) for h in heads_of(f)])

            def carried(t):
                for f in range(2):
                    eng.wait_ge(*ps.taken("S", 0, f))
                    products(("kS", t, f), [[(channels(8 + h, t), head(S1, h))] for h in heads_of(f)])
                    products(("qS", t, f), [[(channels(h, t), head(S1, h))] for h in heads_of(f)])

            def summed(t, f):
                eng.wait_ge(*ps.taken("ZT", t, LEVELS - 1, f))
                if t:
                    eng.wait_ge(vb_ready, f + 1)
                else:
                    eng.wait_ge(*ps.taken("vt", t, f))
                products(("vn", t, f), [[(head(TT, h), head(vb, h))] for h in heads_of(f)])
                eng.wait_ge(*ps.taken("vn", t, f))
                eng.wait_ge(*ps.taken("A", t, f))
                products(("o", t, f), [[(head(AT, h), head(vn, h))] for h in heads_of(f)])
                if not t:
                    products(("S", t, f), [[(head(kS, h), head(vn, h))] for h in heads_of(f)])

            def gated(t, f):
                eng.wait_ge(od_ready, 2 * t + f + 1)
                transposes(("oT", t, f), [head(od, h) for h in heads_of(f)])

            def mixed(layer, t):
                last, source = ("aoT", oaT) if layer else ("oT", oT)
                for f in range(2):
                    eng.wait_ge(*ps.taken(last, t, f))
                for s in range(2):
                    w = weights_here("mix", layer, t, s)
                    products(("mix", layer, t, s), [[(head(source, k), w[:, k, :]) for k in range(KB)]], SLICE)
                eng.wait_ge(x_ready, norms.index(("mix", layer, t)) + 1)
                x_transposed(("x1T", layer, t), t)
                for n in range(2):
                    eng.wait_ge(*ps.taken("x1T", layer, t, n))

            def scores(g, n):
                t = g % 2
                if t == 0 and n == 0:
                    sk = weights_here("sk", g // 2).rearrange("p k n -> p (k n)")
                    for i in range(4):
                        transposes(("skT", g // 2, i), [head(sk, 4 * i + c) for c in range(4)])
                w = weights_here("query", g, n)
                products(("query", g, n), [[(w[:, k, c * P:(c + 1) * P], xTb(k, t)) for k in range(KB)]
                                           for c in range(4)])
                if t == 0:
                    eng.wait_ge(*ps.taken("skT", g // 2, n))
                eng.wait_ge(*ps.taken("query", g, n))
                products(("sc", g, n), [[(head(qhT, 4 * (n % 2) + c), head(skT, 4 * n + c))] for c in range(4)])

            def x2(t):
                eng.wait_ge(x_ready, norms.index(("ffn", 0, t)) + 1)
                x_transposed(("x2T", t), t)
                for n in range(2):
                    eng.wait_ge(*ps.taken("x2T", t, n))

            def kv_slice(t, f, n):
                w = weights_here("kvq", t, f, n)
                products(("kvq", t, f, n), [[(xTb(k, t), w[:, k, :]) for k in range(KB)]], SLICE)
                for m in late_slices(n):
                    eng.wait_ge(roped, (t * 2 + f) * 6 + kq_turn(m) + 1)
                    transposes(("kqT", t, f, m), [head(kq_slot(m), i) for i in range(HALF)])

            def soft(t, f, h):
                ps.free(eng, "score", t, f, h)
                if h == 0:
                    for m in (0, 1, 2, 6, 7, 8):
                        eng.wait_ge(*ps.taken("kqT", t, f, m))
                    for m in range(3, 6):
                        eng.wait_ge(*ps.taken("kvq", t, f, m))
                for grp in range(GROUPS):
                    for kt in range(t + 1):
                        col = 2 * SLICE + (grp * (t + 1) + kt) * P
                        ins = eng.matmul(banks[:, col:col + P], lhsT=head(qT, grp * HALF + h),
                                         rhs=k_heads(t, kt, f, grp, h, 1), start=True, stop=True)
                ins.then_inc(ps.sem_full("score", t, f, h), 1)
                ps.free(eng, "pT", t, f, h)
                eng.wait_ge(p_done, (t * 2 + f) * HALF + h + 1)
                for i in range(GROUPS * (t + 1)):
                    ins = eng.transpose(banks[:, 4 * SLICE + i * P:4 * SLICE + (i + 1) * P], head(prob, i), ident)
                ins.then_inc(ps.sem_full("pT", t, f, h), 1)

            def weigh(t, f, h):
                eng.wait_ge(*ps.taken("pT", t, f, h))
                products(("pv", t, f, h), [[(head(probT, i), v_heads(t, i % (t + 1), f, i // (t + 1), h, 1))
                                            for i in range(GROUPS * (t + 1))]])

            def heads(t, f):
                eng.wait_ge(*ps.taken("pv", t, f, HALF - 1))
                transposes(("aoT", t, f), [head(oh, h) for h in range(HALF)])

            def step(kind, a, b):
                if kind == "inputs":
                    inputs()
                elif kind == "decays":
                    decays()
                elif kind == "qkv":
                    qkv(a)
                elif kind == "z":
                    z(a)
                elif kind == "keys":
                    keys(a, b)
                elif kind == "grams":
                    grams(a, b)
                elif kind == "started":
                    inverse_transposed(a, 0)
                elif kind == "masked":
                    masked(a, b)
                elif kind == "doubled":
                    doubled(a, b)
                elif kind == "values":
                    values(a)
                elif kind == "carried":
                    carried(a)
                elif kind == "summed":
                    summed(a, b)
                elif kind == "gated":
                    gated(a, b)
                elif kind == "mixed":
                    mixed(a, b)
                elif kind == "scores":
                    scores(a, b)
                elif kind == "x2":
                    x2(a)
                elif kind == "slice":
                    kv_slice(a, *b)
                elif kind == "soft":
                    soft(a, *b)
                elif kind == "weigh":
                    weigh(a, *b)
                elif kind == "heads":
                    heads(a, b)

            for st in opening_steps():
                step(*st)
            for g in range(4):
                for steps in gather_steps(g):
                    for st in steps:
                        step(*st)

        @block.scalar
        def _(eng):
            did = Steps(eng, act)
            rs_n = [0]

            def copy_out(key, out, in_=None, func=ACT.Copy):
                eng.wait_ge(*ps.full(*key))
                eng.activation(out, ps.bank(*key) if in_ is None else in_, func).then_inc(ps.sem_taken(*key), 1)

            def x_out(key, t):
                for n in range(2):
                    out = xT[:, :].rearrange("p (k n) -> p k n", k=KB)[:, 4 * n:4 * n + 4, t * P:(t + 1) * P]
                    copy_out(key + (n,), out, heads4(ps.bank(*key, n)))

            def rsqrt_start(n):
                rs_n[0] += 1
                eng.wait_ge(rs_asked, rs_n[0])
                did(eng.activation(rs_y[:, 0:n], rs_in[:, 0:n], ACT.Ln))
                did.wait()
                eng.activation(rs_y[:, 0:n], rs_y[:, 0:n], ACT.Exp, scale=-0.5).then_inc(rs_said, 1)

            def keys(t, f):
                copy_out(("kt", t, f), half(MT, f), func=ACT.Square)
                copy_out(("qt", t, f), half(AT, f), func=ACT.Square)
                eng.wait_ge(dec_in, 2 * t + f + 1)
                eng.activation(half(dec, f), half(dec, f), ACT.Exp).then_inc(dec_out, 1)

            def scaled(t, f):
                rsqrt_start(8)

            def grams(t, f):
                copy_out(("kbT", t, f), half(kbT, f))

            def summed(t, f):
                copy_out(("vn", t, f), half(vn, f))
                if t:
                    eng.wait_ge(od_sum, f + 1)
                else:
                    eng.wait_ge(*ps.taken("o", t, f))
                eng.activation(half(Ybuf, f), half(od, f), ACT.Square).then_inc(sq_o, 1)

            def gated(t, f):
                rsqrt_start(HALF)
                if not t:
                    copy_out(("S", t, f), half(S1, f))
                copy_out(("oT", t, f), half(oT, f))

            def mixed(layer, t):
                rsqrt_start(1)
                x_out(("x1T", layer, t), t)

            def inverse_out(t, s):
                for f in range(2):
                    copy_out(("T", t, s, f), half(Tm, f))

            def silu(n):
                eng.wait_ge(sil_in, n + 1)
                first = qkv_blocks(n)[0]
                pair = qkvT[:, first * SEQ:(first + 2) * SEQ]
                eng.activation(pair, pair, ACT.Silu).then_inc(sil_out, 1)

            def qkv(n):
                if n >= 2:
                    eng.wait_ge(sil_in, n - 1)
                copy_out(("qkv", n), conv_rows(n)[:, :, CONV - 1:],
                         ps.bank("qkv", n).rearrange("p (b k) -> p b k", b=2))
                if n:
                    silu(n - 1)

            def z(n):
                if n == 0:
                    silu(11)
                s, t = n // 2, n % 2
                copy_out(("z", n), zs[:, t * D + s * SLICE:t * D + (s + 1) * SLICE], func=ACT.Silu)

            def scores(g, n):
                if g % 2 == 0 and n == 0:
                    for i in range(4):
                        copy_out(("skT", g // 2, i), skT[:, 4 * i * P:(4 * i + 4) * P])
                at = (n % 2) * SLICE
                copy_out(("query", g, n), qhT[:, at:at + SLICE])
                if g:
                    eng.wait_ge(idx_ready, 4 * (g - 1) + n + 1)
                copy_out(("sc", g, n), sc[:, n * SLICE:(n + 1) * SLICE])

            def gates(g, n):
                eng.wait_ge(gx_in, 4 * g + n + 1)
                at = (g % 2) * P + 2 * n * TOPK
                eng.activation(gate[:, at:at + 2 * TOPK], best[:, 2 * n * TOPK:2 * (n + 1) * TOPK], ACT.Exp)\
                   .then_inc(gx_out, 1)

            def kv_slice(t, f, n):
                key = ("kvq", t, f, n)
                if n // 3 == 1:
                    copy_out(key, v_heads(t, t, f, n - 3, 0, HALF))
                else:
                    turn = kq_turn(n)
                    if turn >= 2:
                        before = turn - 2
                        eng.wait_ge(*ps.full("kqT", t, f, before if before < 3 else before + 3))
                    copy_out(key, kq_slot(n))
                for m in late_slices(n):
                    out = (k_heads(t, t, f, m, 0, HALF) if m < 3
                           else qT[:, (m - 6) * HALF * P:(m - 5) * HALF * P])
                    copy_out(("kqT", t, f, m), out)

            def soft(t, f, h):
                n = (t * 2 + f) * HALF + h
                wide = GROUPS * (t + 1) * P
                eng.wait_ge(nmx, n + 1)
                eng.activation(prob[:, 0:wide], prob[:, 0:wide], ACT.Exp, bias=mxs[:, 1:2], scale=SCALE,
                               accum_out=mxs[:, 2:3]).then_inc(p_done, 1)
                if n:
                    eng.wait_ge(*ps.full("pv", *((t, f, h - 1) if h else ((t, f - 1, HALF - 1) if f
                                                                         else (t - 1, 1, HALF - 1)))))
                copy_out(("pT", t, f, h), probT[:, 0:wide], banks[:, 4 * SLICE:4 * SLICE + wide])

            def step(kind, a, b):
                if kind == "keys":
                    keys(a, b)
                elif kind == "scaled":
                    scaled(a, b)
                elif kind == "grams":
                    grams(a, b)
                elif kind == "summed":
                    summed(a, b)
                elif kind == "gated":
                    gated(a, b)
                elif kind == "mixed":
                    mixed(a, b)
                elif kind == "started":
                    inverse_out(a, 0)
                elif kind == "doubled" and b < LEVELS - 1:
                    inverse_out(a, b)
                elif kind == "inputs":
                    inputs()
                elif kind == "decays":
                    decays()
                elif kind == "qkv":
                    qkv(a)
                elif kind == "z":
                    z(a)
                elif kind == "scores":
                    scores(a, b)
                elif kind == "gates":
                    gates(a, b)
                elif kind == "x2":
                    x_out(("x2T", a), a)
                elif kind == "slice":
                    kv_slice(a, *b)
                elif kind == "soft":
                    soft(a, *b)
                elif kind == "heads":
                    copy_out(("aoT", a, b), half(oaT, b))

            def gelu(blk, j):
                eng.wait_ge(ring_used, RING * (blk + 2))
                eng.activation(gel[:, j * RING:(j + 1) * RING], dots[:, j * RING:(j + 1) * RING],
                               ACT.Gelu).then_inc(gelu_done, 1)

            def inputs():
                for t in range(TILES):
                    x_out(("x0T", t), t)
                copy_out(("convw",), cw[:, :], ps.bank("convw")[:, 0:24 * CONV])
                eng.wait_ge(sm_in, 1)
                did(eng.activation(gtmp[:, 16:32], gtmp[:, 16:32], ACT.Exp))
                eng.activation(gtmp[:, 32:48], gtmp[:, 32:48], ACT.Exp, scale=-1.0)
                eng.activation(alog[:, :], alog[:, :], ACT.Exp)
                did.wait()
                eng.activation(gtmp[:, 16:32], gtmp[:, 16:32], ACT.Ln, bias=1.0).then_inc(sm_out, 1)
                eng.wait_ge(zero_ok, 1)

            def decays():
                eng.wait_ge(*ps.taken("gcum"))
                eng.activation(egc[:, :], gcum[:, :], ACT.Exp).then_inc(sm_out, 1)

            for st in opening_steps():
                step(*st)
            for g in range(4):
                placed = gather_steps(g)
                alone = 4 * (1 + max(b for b, steps in enumerate(placed) if steps) // 4) if g == 3 else BLOCKS
                for b in range(alone):
                    if b % 4 < 2:
                        gelu(BLOCKS * g + b, b % 4)
                    for st in placed[b]:
                        step(*st)
                if alone < BLOCKS:
                    with eng.Fori(alone // 4, HEADS) as h:
                        for b in range(2):
                            gelu(BLOCKS * g + 4 * h + b, b)
                rsqrt_start(1)

        @block.vector
        def _(eng):
            did = Steps(eng, vec)
            rs_n = [0]
            norm_n = [0]

            def tt(out, a, b, op):
                return eng.tensor_tensor(out, a, b, op)

            def rsqrt(source, n, out, scale, eps):
                rs_n[0] += 1
                eng.tensor_scalar(rs_in[:, 0:n], source, scale, eps, ALU.mult, ALU.add).then_inc(rs_asked, 1)
                eng.wait_ge(rs_said, rs_n[0])
                did(tt(rs_t[:, 0:n], rs_y[:, 0:n], rs_y[:, 0:n], ALU.mult))
                did.wait()
                did(tt(rs_t[:, 0:n], rs_t[:, 0:n], rs_in[:, 0:n], ALU.mult))
                did.wait()
                did(eng.tensor_scalar(rs_t[:, 0:n], rs_t[:, 0:n], -0.5, 1.5, ALU.mult, ALU.add))
                did.wait()
                did(tt(out, rs_y[:, 0:n], rs_t[:, 0:n], ALU.mult))
                did.wait()

            def keys(t, f):
                cols = slice(t * HEADS + f * HALF, t * HEADS + (f + 1) * HALF)
                eng.wait_ge(*ps.full("gB", t, f))
                tt(heads4(half(dec, f)), heads4(ps.bank("gB", t, f)), spread(gcum[:, cols]),
                   ALU.subtract).then_inc(ps.sem_taken("gB", t, f), 1)
                eng.wait_ge(*ps.taken("gB", t, f))
                tt(heads4(half(dec, f)), heads4(half(dec, f)), negmask.unsqueeze(1).to_broadcast([P, HALF, P]),
                   ALU.add).then_inc(dec_in, 1)

            def values(t):
                for f in range(2):
                    cols = slice(t * HEADS + f * HALF, t * HEADS + (f + 1) * HALF)
                    eng.wait_ge(*ps.full("vt", t, f))
                    tt(heads4(half(vb, f)), heads4(ps.bank("vt", t, f)), spread(beta[:, cols]),
                       ALU.mult).then_inc(ps.sem_taken("vt", t, f), 1)
                for n in (t, 2 + t):
                    eng.wait_ge(*ps.taken("z", n))
                z3 = zs[:, t * D:(t + 1) * D].rearrange("p (h d) -> p h d", h=HEADS)
                did(tt(z3, z3, normw[:, :].unsqueeze(1).to_broadcast([P, HEADS, P]), ALU.mult))

            def scaled(t, f):
                cols = slice(t * HEADS + f * HALF, t * HEADS + (f + 1) * HALF)
                hs = slice(f * HALF, (f + 1) * HALF)
                eng.wait_ge(*ps.taken("qt", t, f))
                r = rqk[:, 8 * f:8 * f + 8]
                did(eng.tensor_reduce(ss[:, 8 * f:8 * f + HALF], heads4(half(AT, f)), AX_X, ALU.add))
                did(eng.tensor_reduce(ss[:, 8 * f + HALF:8 * f + 8], heads4(half(MT, f)), AX_X, ALU.add))
                did.wait()
                rsqrt(ss[:, 8 * f:8 * f + 8], 8, r, 1.0, NORM_EPS)
                rq, rk = r[:, 0:HALF], r[:, HALF:8]
                did(tt(coef[:, hs], rk, beta[:, cols], ALU.mult))
                did(eng.tensor_scalar(c_query[:, hs], rq, SCALE, None, ALU.mult))
                eng.wait_ge(dec_out, 2 * t + f + 1)
                did(tt(heads4(half(dec, f)), heads4(half(dec, f)), spread(rk), ALU.mult))
                did.wait()
                if t:
                    did(tt(c_state[:, hs], coef[:, hs], egc[:, cols], ALU.mult))
                    did(tt(c_carry[:, hs], c_query[:, hs], egc[:, cols], ALU.mult))
                ins = tt(heads4(half(kb, f)), heads4(ps.bank("kt", t, f)), spread(coef[:, hs]), ALU.mult)
                if not t:
                    ins = tt(heads4(half(kS, f)), heads4(ps.bank("kt", t, f)),
                             heads4(half(dec, f))[:, :, P - 1:P].to_broadcast([P, HALF, P]), ALU.mult)
                ins.then_inc(ps.sem_taken("kt", t, f), 1)

            def grams(t, f):
                for key, out in (("A", AT), ("M", MT)):
                    eng.wait_ge(*ps.full(key, t, f))
                    tt(half(out, f), ps.bank(key, t, f), half(dec, f), ALU.mult)\
                        .then_inc(ps.sem_taken(key, t, f), 1)

            def started(t):
                first = consts[:, C_LVL:C_LVL + P].unsqueeze(1).to_broadcast([P, HALF, P])
                for f in range(2):
                    eng.wait_ge(*ps.taken("M", t, f))
                    did(tt(heads4(half(TT, f)), heads4(half(MT, f)), first, ALU.mult))
                did.wait()
                for f in range(2):
                    tt(heads4(half(TT, f)), heads4(half(TT, f)), ident.unsqueeze(1).to_broadcast([P, HALF, P]),
                       ALU.add).then_inc(tt_ready, 1)

            def masked(t, s):
                level = consts[:, C_LVL + s * P:C_LVL + (s + 1) * P]
                for f in range(2):
                    eng.wait_ge(*ps.full("Y", t, s, f))
                    tt(heads4(half(Ybuf, f)), heads4(ps.bank("Y", t, s, f)),
                       level.unsqueeze(1).to_broadcast([P, HALF, P]), ALU.mult)\
                        .then_inc(ps.sem_taken("Y", t, s, f), 1)

            def doubled(t, s):
                for f in range(2):
                    eng.wait_ge(*ps.full("ZT", t, s, f))
                    tt(half(TT, f), half(TT, f), ps.bank("ZT", t, s, f), ALU.add)\
                        .then_inc(ps.sem_taken("ZT", t, s, f), 1)

            def carried(t):
                for f in range(2):
                    hs = slice(f * HALF, (f + 1) * HALF)
                    eng.wait_ge(*ps.full("kS", t, f))
                    tt(heads4(half(Ybuf, f)), heads4(ps.bank("kS", t, f)), spread(c_state[:, hs]), ALU.mult)\
                        .then_inc(ps.sem_taken("kS", t, f), 1)
                    eng.wait_ge(*ps.taken("kS", t, f))
                    tt(half(vb, f), half(vb, f), half(Ybuf, f), ALU.subtract).then_inc(vb_ready, 1)
                    eng.wait_ge(*ps.full("qS", t, f))
                    tt(heads4(half(MT, f)), heads4(ps.bank("qS", t, f)), spread(c_carry[:, hs]), ALU.mult)\
                        .then_inc(ps.sem_taken("qS", t, f), 1)

            def summed(t, f):
                hs = slice(f * HALF, (f + 1) * HALF)
                eng.wait_ge(*ps.full("o", t, f))
                tt(heads4(half(od, f)), heads4(ps.bank("o", t, f)), spread(c_query[:, hs]), ALU.mult)\
                    .then_inc(ps.sem_taken("o", t, f), 1)
                if t:
                    eng.wait_ge(*ps.taken("o", t, f))
                    eng.wait_ge(*ps.taken("qS", t, f))
                    tt(half(od, f), half(od, f), half(MT, f), ALU.add).then_inc(od_sum, 1)

            def gated(t, f):
                eng.wait_ge(sq_o, 2 * t + f + 1)
                did(eng.tensor_reduce(ss[:, 8 * f:8 * f + HALF], heads4(half(Ybuf, f)), AX_X, ALU.add))
                did.wait()
                rsqrt(ss[:, 8 * f:8 * f + HALF], HALF, rqk[:, 8 * f:8 * f + HALF], 1.0 / P, NORM_EPS)
                did(tt(heads4(half(od, f)), heads4(half(od, f)), spread(rqk[:, 8 * f:8 * f + HALF]), ALU.mult))
                did.wait()
                tt(half(od, f), half(od, f), half(zs[:, t * D:(t + 1) * D], f), ALU.mult).then_inc(od_ready, 1)

            def layer_norm(t):
                xt = xtile(t)
                i = norm_n[0]
                norm_n[0] += 1
                for s in range(2):
                    did(eng.bn_stats(bn[:, 6 * s:6 * s + 6], xt[:, s * SLICE:(s + 1) * SLICE]))
                did.wait()
                did(eng.bn_aggr(mv[:, :], bn[:, :].rearrange("p (s c) -> p s c", s=2)))
                did.wait()
                rsqrt(mv[:, 1:2], 1, rs_t[:, 8:9], 1.0, LN_EPS)
                did(eng.tensor_scalar(xt, xt, mv[:, 0:1], rs_t[:, 8:9], ALU.subtract, ALU.mult))
                did.wait()
                eng.wait_ge(gb_land, 32 * (i + 1))
                did(tt(xt, xt, gb[:, 0:D], ALU.mult))
                did.wait()
                tt(xt, xt, gb[:, D:2 * D], ALU.add).then_inc(x_ready, 1)

            def mixed(layer, t):
                for s in range(2):
                    eng.wait_ge(*ps.full("mix", layer, t, s))
                    xs = xtile(t)[:, s * SLICE:(s + 1) * SLICE]
                    eng.scalar_tensor_tensor(xs, xs, ALPHA, ps.bank("mix", layer, t, s), ALU.mult, ALU.add)\
                        .then_inc(ps.sem_taken("mix", layer, t, s), 1)
                for s in range(2):
                    eng.wait_ge(*ps.taken("mix", layer, t, s))
                layer_norm(t)

            def top16(rows):
                for row, v, _ in rows:
                    did(eng.max(v[:, 0:8], row))
                did.wait()
                for row, v, p in rows:
                    did(eng.max_index(p[:, 0:8], v[:, 0:8], row))
                did.wait()
                for row, v, _ in rows:
                    did(eng.match_replace(row, v[:, 0:8], row, -3.0e38))
                did.wait()
                for row, v, _ in rows:
                    did(eng.max(v[:, 8:16], row))
                did.wait()
                for row, v, p in rows:
                    did(eng.max_index(p[:, 8:16], v[:, 8:16], row))
                did.wait()

            def top(g, n):
                eng.wait_ge(*ps.taken("sc", g, n))
                rows = []
                for i in range(4):
                    at, s = n * SLICE + i * P, 4 * n + i
                    rows.append((sc[:, at:at + P], topv[:, s * TOPK:(s + 1) * TOPK],
                                 topi[:, s * TOPK:(s + 1) * TOPK]))
                top16(rows)

            def best_of(g, n):
                mine = slice(4 * n * TOPK, 4 * (n + 1) * TOPK)
                did(eng.tensor_copy(topf[:, mine], topi[:, mine]))
                tv = topv[:, mine].rearrange("p (h c k) -> p h c k", h=2, c=2)
                four = [P, 2, TOPK, TOPK]
                did(tt(cand[:, :].rearrange("p (h i j) -> p h i j", h=2, i=TOPK),
                       tv[:, :, 0, :].unsqueeze(3).to_broadcast(four),
                       tv[:, :, 1, :].unsqueeze(2).to_broadcast(four), ALU.add))
                did.wait()
                wide = TOPK * TOPK
                top16([(cand[:, i * wide:(i + 1) * wide], best[:, (2 * n + i) * TOPK:(2 * n + i + 1) * TOPK],
                        pos[:, (2 * n + i) * TOPK:(2 * n + i + 1) * TOPK]) for i in range(2)])

            def gates(g, n):
                mine = slice(2 * n * TOPK, 2 * (n + 1) * TOPK)
                hs, hs2 = slice(2 * n, 2 * n + 2), slice(HEADS + 2 * n, HEADS + 2 * n + 2)
                at = (g % 2) * P + 2 * n * TOPK
                gt = gate[:, at:at + 2 * TOPK].rearrange("p (h k) -> p h k", h=2)
                b3 = best[:, mine].rearrange("p (h k) -> p h k", h=2)
                did(eng.tensor_copy(gden[:, hs].unsqueeze(2), b3[:, :, 0:1]))
                did(eng.tensor_scalar(posc[:, 0:2 * TOPK], pos[:, mine], 4, None, ALU.logical_shift_right))
                did(eng.tensor_scalar(posc[:, 2 * TOPK:4 * TOPK], pos[:, mine], 15, None, ALU.bitwise_and))
                did.wait()
                tt(b3, b3, spread(gden[:, hs], TOPK), ALU.subtract).then_inc(gx_in, 1)
                did(eng.tensor_copy(posf[:, 0:4 * TOPK], posc[:, 0:4 * TOPK]))
                eng.wait_ge(gx_out, 4 * g + n + 1)
                did(eng.tensor_reduce(gden[:, hs], gt, AX_X, ALU.add))
                did.wait()
                did(eng.reciprocal(gden[:, hs2], gden[:, hs]))
                did.wait()
                did(tt(gt, gt, spread(gden[:, hs2], TOPK), ALU.mult))
                did.wait()

            def experts(g, n):
                hot4 = hot[:, :].rearrange("p (h k i) -> p h k i", h=2, k=TOPK)
                four = [P, 2, TOPK, TOPK]
                for c in range(2):
                    place = posf[:, c * 2 * TOPK:(c + 1) * 2 * TOPK].rearrange("p (h k) -> p h k", h=2)
                    names = topf[:, 4 * n * TOPK:4 * (n + 1) * TOPK]\
                        .rearrange("p (h c k) -> p h c k", h=2, c=2)[:, :, c, :]
                    did(tt(hot4, place.unsqueeze(3).to_broadcast(four),
                           iota16.unsqueeze(1).unsqueeze(1).to_broadcast(four), ALU.is_equal))
                    did.wait()
                    did(tt(hot4, hot4, names.unsqueeze(2).to_broadcast(four), ALU.mult))
                    did.wait()
                    did(eng.tensor_reduce(expert[:, c * 2 * TOPK:(c + 1) * 2 * TOPK]
                                          .rearrange("p (h k) -> p h k", h=2), hot4, AX_X, ALU.add))
                    did.wait()
                at = (g % 2) * P + 2 * n * TOPK
                eng.scalar_tensor_tensor(idx[:, at:at + 2 * TOPK], expert[:, 0:2 * TOPK], float(P),
                                         expert[:, 2 * TOPK:4 * TOPK], ALU.mult, ALU.add).then_inc(idx_ready, 1)

            def kv_slice(t, f, n):
                if n // 3 == 1:
                    return
                eng.wait_ge(*ps.taken("kvq", t, f, n))
                if t or f or n:
                    eng.wait_ge(roped, (t * 2 + f) * 6 + kq_turn(n))
                rot = heads4(kq_slot(n))[:, :, 0:32]
                halves = rot.rearrange("p h (a c) -> p h a c", a=2)
                four = [P, HALF, 2, 16]
                table = [consts[:, C_ROPE + (t * 2 + i) * 16:C_ROPE + (t * 2 + i + 1) * 16]
                         .unsqueeze(1).unsqueeze(1).to_broadcast(four) for i in range(2)]
                cos_part = rope[:, 0:P].rearrange("p (h a c) -> p h a c", h=HALF, a=2)
                sin_part = rope[:, P:2 * P].rearrange("p (h a c) -> p h a c", h=HALF, a=2)
                did(tt(cos_part, halves, table[0], ALU.mult))
                did(tt(sin_part, halves, table[1], ALU.mult))
                did.wait()
                did(tt(halves[:, :, 0, :], cos_part[:, :, 0, :], sin_part[:, :, 1, :], ALU.subtract))
                tt(halves[:, :, 1, :], cos_part[:, :, 1, :], sin_part[:, :, 0, :], ALU.add).then_inc(roped, 1)

            def soft(t, f, h):
                n = (t * 2 + f) * HALF + h
                wide = (t + 1) * P
                if n:
                    before = (t, f, h - 1) if h else ((t, f - 1, HALF - 1) if f else (t - 1, 1, HALF - 1))
                    eng.wait_ge(*ps.full("pT", *before))
                eng.wait_ge(*ps.full("score", t, f, h))
                scored = banks[:, 2 * SLICE:2 * SLICE + GROUPS * wide].rearrange("p (g k) -> p g k", g=GROUPS)
                masked3 = prob[:, 0:GROUPS * wide].rearrange("p (g k) -> p g k", g=GROUPS)
                eng.tensor_tensor_reduce(masked3, scored, attmask[:, :, SEQ - wide:], 1.0, 2.0 * NEG,
                                         ALU.add, ALU.max, mxs[:, 0:1]).then_inc(ps.sem_taken("score", t, f, h), 1)
                eng.wait_ge(*ps.taken("score", t, f, h))
                eng.tensor_scalar(mxs[:, 1:2], mxs[:, 0:1], -SCALE, None, ALU.mult).then_inc(nmx, 1)

            def weigh(t, f, h):
                n = (t * 2 + f) * HALF + h
                eng.wait_ge(p_done, n + 1)
                did(eng.reciprocal(mxs[:, 3:4], mxs[:, 2:3]))
                did.wait()
                if h == 0 and (t or f):
                    eng.wait_ge(*ps.full("aoT", *((t, 0) if f else (t - 1, 1))))
                eng.wait_ge(*ps.full("pv", t, f, h))
                eng.tensor_scalar(oh[:, h * P:(h + 1) * P], ps.bank("pv", t, f, h)[:, 0:P], mxs[:, 3:4], None,
                                  ALU.mult).then_inc(ps.sem_taken("pv", t, f, h), 1)

            def step(kind, a, b):
                if kind == "keys":
                    keys(a, b)
                elif kind == "scaled":
                    scaled(a, b)
                elif kind == "grams":
                    grams(a, b)
                elif kind == "masked":
                    masked(a, b)
                elif kind == "doubled":
                    doubled(a, b)
                elif kind == "carried":
                    carried(a)
                elif kind == "summed":
                    summed(a, b)
                elif kind == "gated":
                    gated(a, b)
                elif kind == "mixed":
                    mixed(a, b)
                elif kind == "started":
                    started(a)
                elif kind == "values":
                    values(a)
                elif kind == "inputs":
                    inputs()
                elif kind == "decays":
                    decays()
                elif kind == "qkv":
                    convolve(a)
                elif kind == "top":
                    top(a, b)
                elif kind == "best":
                    best_of(a, b)
                elif kind == "gates":
                    gates(a, b)
                elif kind == "experts":
                    experts(a, b)
                elif kind == "slice":
                    kv_slice(a, *b)
                elif kind == "soft":
                    soft(a, *b)
                elif kind == "weigh":
                    weigh(a, *b)

            def row(slot):
                return ring[:, slot * D:(slot + 1) * D]

            def dot_rows(g, blk, j):
                for s in range(RING):
                    eng.wait_ge(landed[s], 16 * (blk + 1))
                    c = j * RING + s
                    eng.tensor_tensor_reduce(row(s), row(s), xtile(g % 2), 1.0, 0.0, ALU.mult, ALU.add,
                                             dots[:, c:c + 1]).then_inc(ring_used, 1)

            def add_rows(g, h, blk, j):
                turn = 2 * (HEADS * g + h) + j + 1
                cols = slice(j * RING, (j + 1) * RING)
                eng.wait_ge(gelu_done, turn)
                first = (g % 2) * P + h * TOPK + j * RING
                tt(wts[:, cols], gel[:, cols], gate[:, bass.ds(first, RING)], ALU.mult).then_inc(wts_ready, 1)
                eng.wait_ge(wts_ready, turn)
                for s in range(RING):
                    eng.wait_ge(landed[s], 16 * (blk + 1))
                    eng.wait_ge(ring_used, RING * (blk + 1) + s - 1)
                    a = acc[:, (s % 2) * D:(s % 2 + 1) * D]
                    c = j * RING + s
                    eng.scalar_tensor_tensor(a, row(s), wts[:, c:c + 1], a, ALU.mult, ALU.add)\
                        .then_inc(ring_used, 1)

            for n in range(2):
                did(eng.memset(conv_rows(n)[:, :, 0:CONV - 1], 0.0))
            did.wait()
            eng.memset(gden[:, :], 0.0).then_inc(zero_ok, 1)
            eng.wait_ge(zero_ok, 1)
            eng.memset(gden[:, :], 0.0).then_inc(ring_used, RING)
            def convolve(n):
                eng.wait_ge(*ps.taken("qkv", n))
                for j in range(CONV - 1, -1, -1):
                    for b, blk in enumerate(qkv_blocks(n)):
                        out = qkvT[:, blk * SEQ:(blk + 1) * SEQ]
                        src = conv_rows(n)[:, b, j:j + SEQ]
                        w = cw[:, j * 24 + blk:j * 24 + blk + 1]
                        if j == CONV - 1:
                            did(eng.tensor_scalar(out, src, w, None, ALU.mult))
                        else:
                            ins = eng.scalar_tensor_tensor(out, src, w, out, ALU.mult, ALU.add)
                            if j == 0 and b == 1:
                                ins.then_inc(sil_in, 1)
                            else:
                                did(ins)
                    if j:
                        did.wait()

            def inputs():
                eng.wait_ge(*ps.full("ab"))
                eng.tensor_copy(ab[:, :], ps.bank("ab")[:, 0:TILES * 16]).then_inc(ps.sem_taken("ab"), 1)
                eng.wait_ge(*ps.taken("ab"))
                ab3 = ab[:, :].rearrange("p (t c) -> p t c", t=TILES)
                small = [gtmp[:, 16 * i:16 * i + 16] for i in range(3)]
                u3 = small[0].rearrange("p (t h) -> p t h", t=TILES)
                did(tt(u3, ab3[:, :, 0:HEADS], dtb[:, :].unsqueeze(1).to_broadcast([P, TILES, HEADS]), ALU.add))
                did(eng.tensor_copy(small[2].rearrange("p (t h) -> p t h", t=TILES), ab3[:, :, HEADS:16]))
                did.wait()
                did(eng.tensor_scalar(small[1], small[0], -1.0, None, ALU.mult))
                did.wait()
                tt(small[1], small[0], small[1], ALU.min).then_inc(sm_in, 1)
                did(eng.tensor_scalar(small[0], small[0], 0.0, None, ALU.max))
                did.wait()
                eng.wait_ge(sm_out, 1)
                did(tt(small[0], small[0], small[1], ALU.add))
                did(eng.tensor_scalar(small[2], small[2], 1.0, None, ALU.add))
                did.wait()
                did(eng.scalar_tensor_tensor(u3, u3, -1.0, alog[:, :].unsqueeze(1).to_broadcast([P, TILES, HEADS]),
                                             ALU.mult, ALU.mult))
                did(eng.reciprocal(beta[:, :], small[2]))
                did.wait()
                eng.tensor_copy(glog[:, :], small[0]).then_inc(g_ready, 1)
                eng.wait_ge(*ps.taken("convw"))

            def decays():
                eng.wait_ge(*ps.full("gcum"))
                eng.tensor_copy(gcum[:, :], ps.bank("gcum")[:, 0:TILES * HEADS]).then_inc(ps.sem_taken("gcum"), 1)
                eng.wait_ge(*ps.taken("gcum"))
                eng.wait_ge(sm_out, 2)

            for st in opening_steps():
                step(*st)
            for g in range(4):
                did(eng.memset(acc[:, :], 0.0))
                did.wait()
                placed = gather_steps(g)
                alone = 4 * (1 + max(b for b, steps in enumerate(placed) if steps) // 4) if g == 3 else BLOCKS
                for b in range(alone):
                    if b % 4 < 2:
                        dot_rows(g, BLOCKS * g + b, b % 4)
                    else:
                        add_rows(g, b // 4, BLOCKS * g + b, b % 4 - 2)
                    for st in placed[b]:
                        step(*st)
                if alone < BLOCKS:
                    with eng.Fori(alone // 4, HEADS) as h:
                        for b in range(4):
                            blk = BLOCKS * g + 4 * h + b
                            if b < 2:
                                dot_rows(g, blk, b)
                            else:
                                add_rows(g, h, blk, b - 2)
                eng.wait_ge(ring_used, RING * (BLOCKS * (g + 1) + 1))
                xt = xtile(g % 2)
                did(eng.scalar_tensor_tensor(xt, xt, ALPHA, acc[:, 0:D], ALU.mult, ALU.add))
                did.wait()
                did(tt(xt, xt, acc[:, D:2 * D], ALU.add))
                did.wait()
                layer_norm(g % 2)


def constants():
    import numpy as np

    c = np.zeros((P, C_ALL), np.float32)
    i, j = np.arange(P)[:, None], np.arange(P)[None, :]
    c[:, C_ID:C_ID + P] = i == j
    c[:, C_TRI:C_TRI + P] = i <= j
    c[:, C_NEG:C_NEG + P] = np.where(j >= i, 0.0, NEG)
    for s in range(LEVELS):
        w = 1 << s
        low_left = (i // (2 * w) == j // (2 * w)) & (i % (2 * w) >= w) & (j % (2 * w) < w)
        if s == 0:
            low_left = low_left.T
        c[:, C_LVL + s * P:C_LVL + (s + 1) * P] = -1.0 * low_left
    rel = P + i - np.arange(SEQ)[None, :]
    for g, (window, dilation) in enumerate(((128, 1), (512, 4), (2048, 16))):
        ok = (rel >= 0) & (rel % dilation == 0) & (rel <= window)
        c[:, C_ATT + g * SEQ:C_ATT + (g + 1) * SEQ] = np.where(ok, 0.0, NEG)
    inv = np.float32(500000.0) ** (-np.arange(16, dtype=np.float32) * np.float32(2.0) / np.float32(32))
    for t in range(TILES):
        ang = (np.arange(P, dtype=np.float32) + t * P)[:, None] * inv.astype(np.float32)[None, :]
        c[:, C_ROPE + 32 * t:C_ROPE + 32 * t + 16] = np.cos(ang)
        c[:, C_ROPE + 32 * t + 16:C_ROPE + 32 * t + 32] = np.sin(ang)
    c[:, C_IOTA:C_IOTA + 16] = np.arange(16)[None, :]
    return c


def kernel(**inputs):
    import numpy as np
    import concourse.bacc as bacc
    from concourse.bass_utils import run_bass_kernel_spmd

    nc = bacc.Bacc("TRN2", target_bir_lowering=False, num_devices=1)
    shapes = {
        "x": (SEQ, D), "dn_w_in": (D, 4 * D + 16), "dn_conv": (CONV, 3 * D), "dn_a_log": (1, HEADS),
        "dn_dt_bias": (1, HEADS), "dn_norm_w": (1, P), "dn_w_out": (D, D), "shared_w_kv": (D, 6 * D),
        "attn_w_q": (D, 3 * D), "attn_w_out": (D, D), "peer_w_query": (2, D, 2 * D),
        "peer_sub_keys": (2, 16, P, P), "peer_u": (2 * P * P, D), "peer_v": (2 * P * P, D),
        "ln_mix_g": (2, D), "ln_mix_b": (2, D), "ln_ffn_g": (2, D), "ln_ffn_b": (2, D),
    }
    arrays, aps = {}, {}
    for name, shape in shapes.items():
        a = np.ascontiguousarray(inputs[name]).reshape(shape)
        parts = {name: a}
        if name in ("peer_u", "peer_v"):
            parts = {f"{name}_{i}": a[i * P * P:(i + 1) * P * P] for i in range(2)}
        for key, value in parts.items():
            arrays[key] = value
            aps[key] = nc.dram_tensor(key, value.shape, mybir.dt.from_np(value.dtype), kind="ExternalInput").ap()
    arrays["constants"] = constants()
    const_ap = nc.dram_tensor("constants", (P, C_ALL), F32, kind="ExternalInput").ap()
    out = nc.dram_tensor("out", (SEQ, D), F32, kind="ExternalOutput").ap()
    sub_keys = [aps["peer_sub_keys"][i].rearrange("s k d -> k s d") for i in range(2)]
    yoco_deltanet_dilated_peer(
        nc, aps["x"], aps["dn_w_in"], aps["dn_conv"], aps["dn_a_log"], aps["dn_dt_bias"], aps["dn_norm_w"],
        aps["dn_w_out"], aps["shared_w_kv"], aps["attn_w_q"], aps["attn_w_out"],
        [aps["peer_w_query"][i] for i in range(2)], sub_keys,
        [aps[f"peer_u_{i}"][:, :] for i in range(2)], [aps[f"peer_v_{i}"][:, :] for i in range(2)],
        aps["ln_mix_g"], aps["ln_mix_b"], aps["ln_ffn_g"], aps["ln_ffn_b"], const_ap, out)
    r = run_bass_kernel_spmd(nc, [arrays], core_ids=[0])
    return r.results[0]["out"].reshape(1, SEQ, D)
```

```python
from contextlib import ExitStack

import concourse.bass as bass
from concourse import mybir

F32 = mybir.dt.float32
U32 = mybir.dt.uint32
ALU = mybir.AluOpType
ACT = mybir.ActivationFunctionType
AX_X = mybir.AxisListType.X

P = 128
SEQ, D = 256, 1024
TILES = SEQ // P
KB = D // P
HEADS = 8
HALF = HEADS // 2
GROUPS = 3
TOPK = 16
CONV = 4
ALPHA = 4.0 ** 0.25
LN_EPS = 1e-5
NORM_EPS = 1e-6
SCALE = float(P) ** -0.5
NEG = -1e30
LEVELS = 7
RING = 8
BLOCKS = 4 * HEADS
PE_SLOTS = (2, 4, 7)
VE_SLOTS = tuple(s for s in range(RING) if s not in PE_SLOTS)
PE_N, VE_N = len(PE_SLOTS), len(VE_SLOTS)
HALVES = (range(RING // 2), range(RING // 2, RING))
VE_HEAD = 2 * (RING + VE_N)
PE_HEAD = 2 * PE_N
WSLOTS = 2
IN_RING = {("mix", 0, 0, 0): 2, ("mix", 0, 0, 1): 3, ("sk", 0): 2, ("query", 0, 0): 3}
SLICE = 512

C_ID = 0
C_TRI = C_ID + P
C_NEG = C_TRI + P
C_LVL = C_NEG + P
C_ATT = C_LVL + LEVELS * P
C_ROPE = C_ATT + GROUPS * SEQ
C_IOTA = C_ROPE + TILES * 2 * 16
C_ALL = C_IOTA + 16

SMALL_LOADS = 6


def qkv_blocks(n):
    first = (8, 10, 0, 2, 12, 14, 4, 6)[n] if n < 8 else 2 * n
    return first, first + 1



SPLIT = ("keys", "grams", "masked", "doubled", "values", "carried", "summed")


def inverse_steps(t, beside):
    out = [[("started", t, 0)], [("flipped", t, 0)]]
    for s in range(1, LEVELS):
        out += [[("masked", t, s)], [("after_masked", t, s)] + beside.get(s, []) + [("doubled", t, s)],
                [("after_doubled", t, s)] + [("flipped", t, s)] * (s < LEVELS - 1)]
        if s == 4:
            out += [[("values", t, 0)], [("after_values", t, 0)]]
    return out


def output_steps(t):
    out = [[("carried", t, 0)], [("after_carried", t, 0)]] if t else []
    both = [[(kind, t, f) for f in range(2)] for kind in ("targets", "summed", "after_summed")]
    return out + both + [[("gated", t, 0)], [("gated", t, 1)]]


def flat(places):
    return [st for steps in places for st in steps]


def opening_steps():
    def qkv(*ns):
        return [("qkv", n, 0) for n in ns]

    def whole(kind, f):
        return [(kind, 0, f), ("after_" + kind, 0, f)]

    out = [("inputs", 0, 0)] + qkv(0) + [("smalls", 0, 0)] + qkv(1, 2) + [("decays", 0, 0)] + qkv(3, 4)
    out += whole("keys", 0) + qkv(5, 6)
    out += [("scaled", 0, 0)] + qkv(7, 8) + whole("keys", 1) + [("betas", 0, 0)] + whole("grams", 0) + qkv(9)
    out += [("scaled", 0, 1)] + qkv(10) + [("betas", 0, 1)] + whole("grams", 1)
    out += flat(inverse_steps(0, {1: [("qkv", 11, 0)], 2: [("z", 0, 0)], 4: [("z", 2, 0)]}))
    end = flat(output_steps(0))
    out += end[:-1] + [("begun", 0, 0)] + end[-1:] + [("finished", 0, 0), ("normed", 0, 0)]
    out += [("subkeys", 0, 0), ("mixed", 0, 0)]
    return out + [("scores", 0, 0), ("z", 1, 0), ("z", 3, 0)] + choice_steps(0, (0, 0)) + choice_steps(0, (0, 1))


def choice_steps(g, n):
    return [(kind, g, n) for kind in ("top", "best", "gates", "experts")]


def attend_steps(t):
    out = [(0.0, ("x2", t, 0))]
    turned = (0, 1, 2, 6, 7, 8)

    def put(weight, steps):
        for st in steps:
            out.append((weight, st))
            weight = 0.0

    for f in range(2):
        def of(kind, n):
            return [(kind, t, (f, n))] if n in turned else []

        for n in range(9):
            back = turned.index(n) - 2 if n in turned else -1
            before = of("turned", turned[back]) if back >= 0 else []
            put(1.0, before + [("slice", t, (f, n))] + of("rotated", n - 1))
        put(1.0, of("turned", 7) + of("rotated", 8))
        put(0.7, of("turned", 8))
        for h in range(HALF + 2):
            def head(kind, h):
                return [(kind, t, (f, h))] if 0 <= h < HALF else []

            put(0.7, head("pturn", h - 1) + head("score", h) + head("out", h - 2))
            put(0.7 if h <= HALF else 0.0, head("weigh", h - 1) + head("soft", h))
        put(0.3, [("heads", t, f)])
    return out


def gather_steps(g):
    placed = []

    def chain(steps, first, last):
        weighted = [st if isinstance(st[0], float) else (1.0, st) for st in steps]
        total = sum(w for w, _ in weighted[1:]) or 1.0
        at = first
        for i, (w, st) in enumerate(weighted):
            at += w * (last - first) / total if i else 0.0
            placed.append((at, st))

    chain([("scores", g, n) for n in range(1, 4)], *SCORES_AT)
    for n in range(1, 4):
        chain(choice_steps(g, n), 8 * n - 6.5 + 0.5 * (n == 1), 8 * n - 2.3)
    if g < 3:
        if g == 0:
            places = [[("keys", 1, 0), ("keys", 1, 1)], [("after_keys", 1, 0), ("after_keys", 1, 1)],
                      [("scaled", 1, 0), ("betas", 1, 0)], [("scaled", 1, 1), ("betas", 1, 1), ("grams", 1, 0)],
                      [("after_grams", 1, 0), ("grams", 1, 1)], [("after_grams", 1, 1)]]
            places += inverse_steps(1, {}) + output_steps(1)
            chain([(float(i == 0), st) for steps in places for i, st in enumerate(steps)], *DELTA_AT)
        else:
            chain(attend_steps(g - 1), *ATTEND_AT)
        chain([(float(kind == "normed"), (kind, min(g, 1), (g + 1) % 2)) for kind in ("begun", "normed", "mixed")],
              *MIXED_AT)
        chain([("subkeys", g + 1, 0)] * (g == 1) + [("scores", g + 1, 0)] + choice_steps(g + 1, 0), *NEXT_AT)
    out = [[] for _ in range(2 * BLOCKS)]
    for at, st in sorted(placed, key=lambda p: p[0]):
        out[int(2 * at)].append(st)
    return out


SCORES_AT = (0.3, 2.3)
DELTA_AT = (2.6, 24.3)
ATTEND_AT = (2.6, 25.0)
MIXED_AT = (25.1, 26.6)
NEXT_AT = (28.0, 30.4)


AHEAD = ("slice", "turned", "score", "pturn", "scores", "x2", "begun")


def blocks_alone(g, placed):
    return 4 * (1 + max(i for i, steps in enumerate(placed) if steps) // 8) if g == 3 else BLOCKS


def chosen(n):
    return (2 * n[0] + n[1], 1) if isinstance(n, tuple) else (2 * n, 2)


def all_steps():
    return opening_steps() + [st for g in range(4) for steps in gather_steps(g) for st in steps]


def fills(kind, a, b):
    if kind == "inputs":
        return [(("x0T", t, i), 2 * t + i, 1) for t in range(TILES) for i in range(2)]
    if kind == "smalls":
        return [(("convw",), 4, 1), (("ab",), 5, 1)]
    if kind == "decays":
        return [(("gcum",), 5, 1)]
    if kind == "qkv":
        return [((kind, a), a % 2, 1)]
    if kind == "z":
        return [((kind, a), a // 2, 1)]
    if kind == "keys":
        return [(("kt", a, b), 2 + b, 2), (("qt", a, b), 6 + b, 1), (("gB", a, b), 4 + b, 1)]
    if kind == "betas":
        return [(("kbT", a, b), 4 + b, 1)]
    if kind == "grams":
        return [(("A", a, b), 6 + b, 1), (("M", a, b), 2 + b, 1)]
    if kind == "flipped":
        return [(("T", a, b, f), 4 + f, 1) for f in range(2)]
    if kind == "masked":
        return [(("Y", a, b, f), 2 + f, 1) for f in range(2)]
    if kind == "doubled":
        return [(("ZT", a, b, f), 6 + f, 1) for f in range(2)]
    if kind == "values":
        return [(("vt", a, f), 2 + f, 1) for f in range(2)]
    if kind == "carried":
        return [(("kS", a, f), 2 + f, 1) for f in range(2)] + [(("qS", a, f), 6 + f, 1) for f in range(2)]
    if kind == "summed":
        return [(("o", a, b), 6 + b, 1)] + ([] if a else [(("S", a, b), 2 + b, 1)])
    if kind == "targets":
        return [(("vn", a, b), 4 + b, 1)]
    if kind == "gated":
        return [(("oT", a, b), 4 + b, 1)]
    if kind == "begun":
        return [(("mix", a, b, n), n if a + b == 0 else 4 + n, 1) for n in range(2)]
    if kind == "mixed":
        return [(("x1T", a, b, n), 2 + n, 1) for n in range(2)]
    if kind == "scores":
        return [(("query", a, b), 4 + b % 2, 1), (("sc", a, b), 2 + b % 2, 1)]
    if kind == "subkeys":
        return [(("skT", a // 2, i), 4 + i, 1) for i in range(4)]
    if kind == "x2":
        return [(("x2T", a, n), 2 + n, 1) for n in range(2)]
    if kind == "slice":
        return [(("kvq", a, *b), 2 + b[1] % 2, 1)]
    if kind == "turned":
        return [(("kqT", a, *b), 6 + b[1] % 2, 1)]
    if kind == "score":
        return [(("score", a, *b), 2, 1)]
    if kind == "pturn":
        return [(("pT", a, *b), 4, 1)]
    if kind == "weigh":
        return [(("pv", a, *b), 6, 1)]
    if kind == "heads":
        return [(("aoT", a, b), 7, 1)]
    return []


class Psum:

    def __init__(self, banks, full, taken):
        self.banks, self.full_sem, self.taken_sem = banks, full, taken
        self.at = {}
        filled, taken_count = [0] * 8, [0] * 8
        for step in all_steps():
            for key, bank, releases in fills(*step):
                before = taken_count[bank]
                filled[bank] += 1
                taken_count[bank] += releases
                self.at[key] = (bank, filled[bank], before, taken_count[bank])

    def bank(self, *key):
        b = self.at[key][0]
        return self.banks[:, b * SLICE:(b + 1) * SLICE]

    def full(self, *key):
        b, n, _, _ = self.at[key]
        return self.full_sem[b], n

    def taken(self, *key):
        b, _, _, n = self.at[key]
        return self.taken_sem[b], n

    def sem_full(self, *key):
        return self.full_sem[self.at[key][0]]

    def sem_taken(self, *key):
        return self.taken_sem[self.at[key][0]]

    def free(self, eng, *key):
        b, _, before, _ = self.at[key]
        if before:
            eng.wait_ge(self.taken_sem[b], before)


def vector_rows(head, blk):
    return VE_N + VE_HEAD * head + (RING * blk if blk < 3 else 2 * RING + VE_N)


def tensor_rows(head, j):
    return PE_N + PE_HEAD * head + PE_N * j


def step_weights(kind, a, b):
    if kind in ("qkv", "z") and a % 2 == 0:
        return [(kind, a // 2)]
    if kind == "scores":
        return [("query", a, b)]
    if kind == "subkeys":
        return [("sk", a // 2)]
    if kind == "slice":
        return [("kvq", a, *b)]
    if kind == "begun":
        return [("mix", a, b, n) for n in range(2)]
    return []


def last_reader(key):
    if key[0] in ("qkv", "z"):
        return (key[0], 2 * key[1] + 1)
    if key[0] == "sk":
        return ("skT", key[1], 3)
    return key


def norm_order():
    return [("mix", 0, 0), ("mix", 0, 1), ("ffn", 0, 0), ("mix", 1, 0), ("ffn", 0, 1), ("mix", 1, 1),
            ("ffn", 1, 0), ("ffn", 1, 1)]


class Steps:

    def __init__(self, eng, sem):
        self.eng, self.sem, self.n = eng, sem, 0

    def __call__(self, ins):
        self.n += 1
        return ins.then_inc(self.sem, 1)

    def wait(self):
        self.eng.wait_ge(self.sem, self.n)


def yoco_deltanet_dilated_peer(nc, x_d, w_in, conv_d, alog_d, dtb_d, normw_d, w_out, w_kv, w_q, a_out,
                               w_query, sub_keys, u_tab, v_tab, gmix, bmix, gffn, bffn, const_d, out_d):
    with ExitStack() as ctx:
        def sb(name, cols, dt=F32):
            return ctx.enter_context(nc.sbuf_tensor(name, [P, cols], dt))

        def sem(name):
            return ctx.enter_context(nc.semaphore(name))

        ring = sb("ring", RING * D)
        wbuf = sb("wbuf", WSLOTS * KB * SLICE)
        x = sb("x_rows", TILES * D)
        xT = sb("xT", KB * SEQ)
        skT = sb("skT", 16 * P)
        consts = sb("consts", C_ALL)
        gb = sb("gb", 2 * D)
        acc = sb("acc", 2 * D)
        choice = sb("choice", 7 * SLICE)
        qhT = choice[:, 0:2 * SLICE]
        sc = choice[:, 2 * SLICE:6 * SLICE]
        cand = choice[:, 6 * SLICE:7 * SLICE]
        hot = cand
        raw = choice[:, 2 * SLICE:2 * SLICE + 2 * 2 * (SEQ + CONV - 1)]
        topv = sb("topv", 16 * TOPK)
        topi = sb("topi", 16 * TOPK, U32)
        topf = sb("topf", 16 * TOPK)
        best = sb("best", P)
        pos = sb("pos", P, U32)
        posf = sb("posf", 2 * P)
        expert = sb("expert", 2 * P)
        posc = expert[:, :].bitcast(U32)
        idx = sb("idx", 2 * P, U32)
        stage = sb("stage", 2 * TOPK, U32)
        gate = sb("gate", 2 * P)
        gden = sb("gden", 2 * HEADS)
        dots = sb("dots", TOPK)
        gel = sb("gel", TOPK)
        diag = sb("diag", PE_N * P)
        wts = sb("wts", TOPK)
        ab = sb("ab", TILES * 16)
        alog = sb("alog", HEADS)
        dtb = sb("dtb", HEADS)
        normw = sb("normw", P)
        cw = sb("cw", 24 * CONV)
        glog = sb("glog", TILES * HEADS)
        gtmp = sb("gtmp", 3 * TILES * HEADS)
        beta = sb("beta", TILES * HEADS)
        gcum = sb("gcum", TILES * HEADS)
        egc = sb("egc", TILES * HEADS)
        decl = sb("decl", HEADS)
        ss = sb("ss", 16)
        c_state = sb("c_state", HEADS)
        c_query = sb("c_query", HEADS)
        c_carry = sb("c_carry", HEADS)
        coef = sb("coef", HEADS)
        rs_in = sb("rs_in", 16)
        rs_y = sb("rs_y", 16)
        rs_t = sb("rs_t", 16)
        rqk = sb("rqk", 16)
        bn = sb("bn", 2 * 6)
        mv = sb("mv", 2)
        mxs = sb("mxs", 2 * 4)
        arena = sb("arena", 17 * D)

        def part(first, cols):
            return arena[:, first:first + cols]

        qkvT = part(0, 24 * SEQ)
        zs = part(6 * D, 2 * D)
        dec = part(8 * D, D)
        Ybuf = dec
        MT = part(9 * D, D)
        AT = part(10 * D, D)
        Tm = part(11 * D, D)
        oT = Tm
        TT = part(12 * D, D)
        vb = part(13 * D, D)
        kb = part(14 * D, D)
        vn = kb
        kbT = part(15 * D, D)
        od = kbT
        S1 = part(16 * D, D)
        kS = acc[:, 0:D]
        cw_in = acc[:, D:D + P]
        wab = acc[:, D + P:D + 2 * P]
        kT0 = part(0, 24 * P)
        v0 = part(3 * D, 24 * P)
        kT1 = part(6 * D, 12 * P)
        v1 = part(7 * D + 512, 12 * P)
        qT = part(9 * D, 12 * P)
        kq = part(10 * D + 512, 2 * SLICE)
        rope = part(11 * D + 512, 2 * P)
        prob = part(12 * D, GROUPS * SEQ)
        probT = part(13 * D, GROUPS * SEQ)
        oh = part(14 * D, HALF * P)
        oaT = part(15 * D, D)

        banks = ctx.enter_context(nc.psum_tensor("banks", [P, 8 * SLICE], F32))
        full = [sem(f"bank{b}_full") for b in range(8)]
        taken = [sem(f"bank{b}_taken") for b in range(8)]
        ps = Psum(banks, full, taken)

        loaded = sem("tokens_loaded")
        loaded_small = sem("small_inputs_loaded")
        w_land = [sem(f"weights{i}_landed") for i in range(WSLOTS + 2)]
        gb_land = sem("norm_rows_landed")
        landed = [sem(f"row{i}_landed") for i in range(RING)]
        ring_used = sem("rows_used_by_vector")
        pe_used = sem("rows_used_by_tensor")
        diag_ready = sem("diagonals_ready")
        sums_taken = sem("tensor_sums_taken")
        staged = sem("indices_staged")
        gelu_done = sem("gelu_done")
        wts_ready = sem("weights_of_rows_ready")
        idx_ready = sem("indices_ready")
        vec = sem("vector_step")
        act = sem("scalar_step")
        rs_asked = sem("rsqrt_asked")
        rs_said = sem("rsqrt_said")
        sil_in = sem("conv_done")
        sil_out = sem("silu_done")
        zero_ok = sem("raw_zeroed")
        g_ready = sem("log_decay_ready")
        sm_in = sem("small_in")
        sm_out = sem("small_out")
        dec_in = sem("decay_exponent_ready")
        dec_out = sem("decay_ready")
        sq_o = sem("squares_done")
        od_ready = sem("delta_output_ready")
        vb_ready = sem("delta_targets_ready")
        od_sum = sem("delta_output_summed")
        tt_ready = sem("inverse_started")
        x_ready = sem("x_normed")
        gx_in = sem("gate_exponent_ready")
        gx_out = sem("gate_exp_done")
        roped = sem("roped")
        p_done = sem("probabilities_done")
        nmx = sem("negated_max_ready")
        stored = sem("output_stored")

        ident = consts[:, C_ID:C_ID + P]
        tri = consts[:, C_TRI:C_TRI + P]
        negmask = consts[:, C_NEG:C_NEG + P]
        attmask = consts[:, C_ATT:C_ATT + GROUPS * SEQ].rearrange("p (g k) -> p g k", g=GROUPS)
        iota16 = consts[:, C_IOTA:C_IOTA + 16]

        slot_of, held, turn = {}, {}, 0
        for st in all_steps():
            for key in step_weights(*st):
                slot = IN_RING.get(key)
                if slot is None:
                    slot, turn = turn % WSLOTS, turn + 1
                earlier = held.setdefault(slot, [])
                slot_of[key] = (slot, len(earlier), earlier[-1] if earlier else None)
                earlier.append(key)

        def weight_slot(slot):
            n = KB * SLICE
            return ring[:, (slot - WSLOTS) * n:(slot - WSLOTS + 1) * n] if slot >= WSLOTS \
                else wbuf[:, slot * n:(slot + 1) * n]

        def weights(*key):
            return weight_slot(slot_of[key][0]).rearrange("p (k n) -> p k n", k=KB)

        def heads4(ap):
            return ap.rearrange("p (h d) -> p h d", h=HALF)

        def half(ap, f):
            return ap[:, f * HALF * P:(f + 1) * HALF * P]

        def xtile(t):
            return x[:, t * D:(t + 1) * D]

        def xTb(k, t):
            return xT[:, k * SEQ + t * P:k * SEQ + (t + 1) * P]

        def channels(blk, t):
            return qkvT[:, blk * SEQ + t * P:blk * SEQ + (t + 1) * P]

        def spread(cols, n=P):
            return cols.unsqueeze(2).to_broadcast([P, cols.shape[1], n])

        def mx_of(n):
            return mxs[:, 4 * (n % 2):4 * (n % 2) + 4]

        def kq_turn(n):
            return n if n < 3 else n - 3

        def kq_slot(n):
            s = kq_turn(n) % 2
            return kq[:, s * SLICE:(s + 1) * SLICE]

        def tile_heads(first, second, t, kt, f, grp, h, n):
            buf, at = (first, grp * HEADS + f * HALF + h) if kt == 0 else (second, grp * HALF + h)
            return buf[:, at * P:(at + n) * P]

        def k_heads(t, kt, f, grp, h, n):
            return tile_heads(kT0, kT1, t, kt, f, grp, h, n)

        def v_heads(t, kt, f, grp, h, n):
            return tile_heads(v0, v1, t, kt, f, grp, h, n)

        def conv_rows(n):
            s = n % 2
            w = SEQ + CONV - 1
            return raw[:, s * 2 * w:(s + 1) * 2 * w].rearrange("p (b k) -> p b k", b=2)

        norms = norm_order()
        block = ctx.enter_context(nc.Block())

        @block.sync
        def _(eng):
            eng.dma_start(consts[:, C_ID:C_ID + P], const_d[:, C_ID:C_ID + P]).then_inc(loaded, 16)
            for t in range(TILES):
                eng.dma_start(xtile(t), x_d[t * P:(t + 1) * P, :]).then_inc(loaded, 16)

            def small_loads():
                eng.dma_start(cw_in[0:24 * CONV, :], conv_d.rearrange("j (b p) -> (j b) p", p=P))\
                   .then_inc(loaded_small, 16)
                eng.dma_start(wab[:, :].rearrange("p (k n) -> p k n", k=KB),
                              w_in.rearrange("(k p) n -> p k n", p=P)[:, :, 4 * D:4 * D + 16])\
                   .then_inc(loaded_small, 16)
                eng.dma_start(alog[:, :], alog_d.to_broadcast([P, HEADS])).then_inc(loaded_small, 16)
                eng.dma_start(dtb[:, :], dtb_d.to_broadcast([P, HEADS])).then_inc(loaded_small, 16)
                eng.dma_start(normw[:, :], normw_d.to_broadcast([P, P])).then_inc(loaded_small, 16)
                eng.dma_start(consts[:, C_TRI:C_ALL], const_d[:, C_TRI:C_ALL]).then_inc(loaded_small, 16)

            def view(key):
                def cols(w, c):
                    return w.rearrange("(k p) n -> p k n", p=P)[:, :, c:c + SLICE]

                if key[0] == "qkv":
                    return cols(w_in, qkv_blocks(2 * key[1])[0] * P)
                if key[0] == "z":
                    return cols(w_in, 3 * D + key[1] * SLICE)
                if key[0] == "mix":
                    return cols((w_out, a_out)[key[1]], key[3] * SLICE)
                if key[0] == "query":
                    return cols(w_query[key[1] // 2], key[2] * SLICE)
                if key[0] == "sk":
                    return sub_keys[key[1]]
                what, grp = divmod(key[3], 3)
                return cols(w_kv if what < 2 else w_q,
                            (what * GROUPS * D if what < 2 else 0) + grp * D + key[2] * SLICE)

            def load_weights(key):
                at, _, earlier = slot_of[key]
                if earlier:
                    eng.wait_ge(*ps.full(*last_reader(earlier)))
                slot = weight_slot(at)
                if key[0] == "sk":
                    eng.dma_start(slot[:, 0:16 * P].rearrange("p (s d) -> p s d", s=16), view(key))\
                       .then_inc(w_land[at], 16)
                else:
                    eng.dma_start(slot.rearrange("p (k n) -> p k n", k=KB), view(key)).then_inc(w_land[at], 16)

            def load_norm(i):
                which, layer, _ = norms[i]
                if i:
                    eng.wait_ge(x_ready, i)
                g, b = (gmix, bmix) if which == "mix" else (gffn, bffn)
                eng.dma_start(gb[:, 0:D], g[layer:layer + 1, :].to_broadcast([P, D])).then_inc(gb_land, 16)
                eng.dma_start(gb[:, D:2 * D], b[layer:layer + 1, :].to_broadcast([P, D])).then_inc(gb_land, 16)

            def step_loads(st):
                for key in step_weights(*st):
                    load_weights(key)
                    if key == ("qkv", 0):
                        small_loads()
                if st[0] == "normed":
                    load_norm(norms.index(("mix", st[1], st[2])))

            for st in opening_steps():
                step_loads(st)
            for g in range(4):
                for steps in gather_steps(g):
                    for st in steps:
                        step_loads(st)
                load_norm(norms.index(("ffn", g // 2, g % 2)))
            for t in range(TILES):
                eng.wait_ge(x_ready, 4 + 2 + t + 1)
                eng.dma_start(out_d[t * P:(t + 1) * P, :], xtile(t)).then_inc(stored, 16)
            eng.wait_ge(stored, 16 * TILES)

        @block.gpsimd
        def _(eng):
            for g in range(4):
                table = (u_tab[g // 2], v_tab[g // 2])
                with eng.Fori(0, HEADS // 2) as r:
                    for par in range(2):
                        head = HEADS * g + 2 * r + par
                        eng.wait_ge(idx_ready, head + 1)
                        eng.wait_ge(ring_used, VE_HEAD * head + 1)
                        eng.wait_ge(pe_used, PE_HEAD * head + 1)
                        eng.nop(nofuse=True)
                        eng.tensor_copy(stage[:, par * TOPK:(par + 1) * TOPK],
                                        idx[:, bass.ds((g % 2) * P + TOPK * (2 * r + par), TOPK)])\
                           .then_inc(staged, 1)
                        eng.wait_ge(staged, head + 1)
                        for side in range(2):
                            for j in range(TOPK):
                                slot = j % RING
                                blk = 2 * side + j // RING
                                if slot not in PE_SLOTS and blk in (0, 3):
                                    before = vector_rows(head, blk - 1) if blk else vector_rows(head, 0) - VE_N
                                    eng.wait_ge(ring_used, before + VE_SLOTS.index(slot) + 1)
                                elif blk in (0, 3):
                                    before = tensor_rows(head, 0) if blk else tensor_rows(head, -1)
                                    eng.wait_ge(pe_used, before + PE_SLOTS.index(slot) + 1)
                                else:
                                    eng.wait_ge(ring_used, vector_rows(head, blk - 1) + slot + 1)
                                eng.nop(nofuse=True)
                                eng.indirect_dma_start(
                                    ring[:, slot * D:(slot + 1) * D], None, table[side],
                                    bass.IndirectOffsetOnAxis(ap=stage[:, par * TOPK + j:par * TOPK + j + 1],
                                                              axis=0)).then_inc(landed[slot], 16)

        @block.tensor
        def _(eng):
            def transposes(key, sources):
                ps.free(eng, *key)
                bank = ps.bank(*key)
                for i, src in enumerate(sources):
                    rows = src.shape[0]
                    ins = eng.transpose(bank[:, i * P:i * P + rows], src, ident[0:rows, 0:rows])
                ins.then_inc(ps.sem_full(*key), 1)

            def products(key, pairs, cols=P, wait_free=True):
                if wait_free:
                    ps.free(eng, *key)
                bank = ps.bank(*key)
                for i, terms in enumerate(pairs):
                    for n, (a, b) in enumerate(terms):
                        ins = eng.matmul(bank[:, i * cols:(i + 1) * cols], lhsT=a, rhs=b,
                                         start=n == 0, stop=n == len(terms) - 1)
                ins.then_inc(ps.sem_full(*key), 1)

            def weights_here(*key):
                slot, before, _ = slot_of[key]
                eng.wait_ge(w_land[slot], 16 * (before + 1))
                return weights(*key)

            def x_transposed(key, t):
                for n in range(2):
                    transposes(key + (n,), [xtile(t)[:, (4 * n + i) * P:(4 * n + i + 1) * P] for i in range(4)])

            def heads_of(f):
                return range(f * HALF, (f + 1) * HALF)

            def head(buf, h):
                return buf[:, h * P:(h + 1) * P]

            def inputs():
                eng.wait_ge(loaded, 16 * (TILES + 1))
                for t in range(TILES):
                    x_transposed(("x0T", t), t)
                for t in range(TILES):
                    for n in range(2):
                        eng.wait_ge(*ps.taken("x0T", t, n))

            def smalls():
                eng.wait_ge(loaded_small, 16 * SMALL_LOADS)
                transposes(("convw",), [cw_in[0:24 * CONV, :]])
                products(("ab",), [[(xTb(k, t), wab[:, k * 16:(k + 1) * 16]) for k in range(KB)]
                                   for t in range(TILES)], 16)

            def decays():
                eng.wait_ge(g_ready, 1)
                products(("gcum",), [[(tri, glog[:, :])]], TILES * HEADS)

            def qkv(n):
                w = weights_here("qkv", n // 2)
                products(("qkv", n), [[(w[:, k, c * P:(c + 1) * P], xT[:, k * SEQ:(k + 1) * SEQ])
                                       for k in range(KB)] for c in (2 * (n % 2), 2 * (n % 2) + 1)], SEQ)

            def z(n):
                w = weights_here("z", n // 2)
                products(("z", n), [[(xTb(k, n % 2), w[:, k, :]) for k in range(KB)]], SLICE)

            def keys(t, f):
                if t == 0:
                    eng.wait_ge(sil_out, 4 * f + 4)
                transposes(("kt", t, f), [channels(8 + h, t) for h in heads_of(f)])
                transposes(("qt", t, f), [channels(h, t) for h in heads_of(f)])
                if t == 0 and f == 0:
                    eng.wait_ge(g_ready, 1)
                products(("gB", t, f), [[(glog[:, t * HEADS + h:t * HEADS + h + 1].to_broadcast([P, P]), tri)]
                                        for h in heads_of(f)])

            def betas(t, f):
                eng.wait_ge(*ps.taken("kt", t, f))
                transposes(("kbT", t, f), [head(kb, h) for h in heads_of(f)])

            def grams(t, f):
                products(("A", t, f), [[(channels(8 + h, t), channels(h, t))] for h in heads_of(f)])
                eng.wait_ge(*ps.taken("kbT", t, f))
                products(("M", t, f), [[(channels(8 + h, t), head(kbT, h))] for h in heads_of(f)])

            def inverse_transposed(t, s):
                for f in range(2):
                    if s:
                        eng.wait_ge(*ps.taken("ZT", t, s, f))
                    else:
                        eng.wait_ge(tt_ready, 2 * t + f + 1)
                    transposes(("T", t, s, f), [head(TT, h) for h in heads_of(f)])

            def masked(t, s):
                for f in range(2):
                    eng.wait_ge(*ps.taken("T", t, s - 1, f))
                    products(("Y", t, s, f), [[(head(MT, h), head(Tm, h))] for h in heads_of(f)])

            def doubled(t, s):
                for f in range(2):
                    eng.wait_ge(*ps.taken("Y", t, s, f))
                    products(("ZT", t, s, f), [[(head(Ybuf, h), head(TT, h))] for h in heads_of(f)])

            def values(t):
                if t == 0:
                    eng.wait_ge(sil_out, 12)
                for f in range(2):
                    transposes(("vt", t, f), [channels(16 + h, t) for h in heads_of(f)])

            def carried(t):
                for f in range(2):
                    eng.wait_ge(*ps.taken("S", 0, f))
                    products(("kS", t, f), [[(channels(8 + h, t), head(S1, h))] for h in heads_of(f)])
                    products(("qS", t, f), [[(channels(h, t), head(S1, h))] for h in heads_of(f)])

            def targets(t, f):
                eng.wait_ge(*ps.taken("ZT", t, LEVELS - 1, f))
                if t:
                    eng.wait_ge(vb_ready, f + 1)
                else:
                    eng.wait_ge(*ps.taken("vt", t, f))
                products(("vn", t, f), [[(head(TT, h), head(vb, h))] for h in heads_of(f)])

            def summed(t, f):
                eng.wait_ge(*ps.taken("vn", t, f))
                eng.wait_ge(*ps.taken("A", t, f))
                products(("o", t, f), [[(head(AT, h), head(vn, h))] for h in heads_of(f)])
                if not t:
                    products(("S", t, f), [[(head(kS, h), head(vn, h))] for h in heads_of(f)])

            def gated(t, f):
                eng.wait_ge(od_ready, 2 * t + f + 1)
                transposes(("oT", t, f), [head(od, h) for h in heads_of(f)])

            def half_mixed(layer, t, f):
                last, source = ("aoT", oaT) if layer else ("oT", oT)
                eng.wait_ge(*ps.taken(last, t, f))
                for s in range(2):
                    key = ("mix", layer, t, s)
                    w = weights_here(*key)
                    if f == 0:
                        ps.free(eng, *key)
                    for k in heads_of(f):
                        ins = eng.matmul(ps.bank(*key), lhsT=head(source, k), rhs=w[:, k, :],
                                         start=k == 0, stop=k == KB - 1)
                    if f:
                        ins.then_inc(ps.sem_full(*key), 1)

            def mixed(layer, t):
                eng.wait_ge(x_ready, norms.index(("mix", layer, t)) + 1)
                x_transposed(("x1T", layer, t), t)
                for n in range(2):
                    eng.wait_ge(*ps.taken("x1T", layer, t, n))

            def subkeys(g):
                sk = weights_here("sk", g // 2).rearrange("p k n -> p (k n)")
                for i in range(4):
                    transposes(("skT", g // 2, i), [head(sk, 4 * i + c) for c in range(4)])

            def scores(g, n):
                t = g % 2
                w = weights_here("query", g, n)
                products(("query", g, n), [[(w[:, k, c * P:(c + 1) * P], xTb(k, t)) for k in range(KB)]
                                           for c in range(4)])
                if t == 0:
                    eng.wait_ge(*ps.taken("skT", g // 2, n))
                eng.wait_ge(*ps.taken("query", g, n))
                products(("sc", g, n), [[(head(qhT, 4 * (n % 2) + c), head(skT, 4 * n + c))] for c in range(4)])

            def x2(t):
                eng.wait_ge(x_ready, norms.index(("ffn", 0, t)) + 1)
                x_transposed(("x2T", t), t)
                for n in range(2):
                    eng.wait_ge(*ps.taken("x2T", t, n))

            def kv_slice(t, f, n):
                w = weights_here("kvq", t, f, n)
                products(("kvq", t, f, n), [[(xTb(k, t), w[:, k, :]) for k in range(KB)]], SLICE)

            def turned(t, f, n):
                eng.wait_ge(roped, (t * 2 + f) * 6 + kq_turn(n) + 1)
                transposes(("kqT", t, f, n), [head(kq_slot(n), i) for i in range(HALF)])

            def score(t, f, h):
                ps.free(eng, "score", t, f, h)
                if h == 0:
                    for m in (0, 1, 2, 6, 7, 8):
                        eng.wait_ge(*ps.taken("kqT", t, f, m))
                    for m in range(3, 6):
                        eng.wait_ge(*ps.taken("kvq", t, f, m))
                for grp in range(GROUPS):
                    for kt in range(t + 1):
                        col = 2 * SLICE + (grp * (t + 1) + kt) * P
                        ins = eng.matmul(banks[:, col:col + P], lhsT=head(qT, grp * HALF + h),
                                         rhs=k_heads(t, kt, f, grp, h, 1), start=True, stop=True)
                ins.then_inc(ps.sem_full("score", t, f, h), 1)

            def pturn(t, f, h):
                ps.free(eng, "pT", t, f, h)
                eng.wait_ge(p_done, (t * 2 + f) * HALF + h + 1)
                for i in range(GROUPS * (t + 1)):
                    ins = eng.transpose(banks[:, 4 * SLICE + i * P:4 * SLICE + (i + 1) * P], head(prob, i), ident)
                ins.then_inc(ps.sem_full("pT", t, f, h), 1)

            def weigh(t, f, h):
                eng.wait_ge(*ps.taken("pT", t, f, h))
                products(("pv", t, f, h), [[(head(probT, i), v_heads(t, i % (t + 1), f, i // (t + 1), h, 1))
                                            for i in range(GROUPS * (t + 1))]])

            def heads(t, f):
                eng.wait_ge(*ps.taken("pv", t, f, HALF - 1))
                transposes(("aoT", t, f), [head(oh, h) for h in range(HALF)])

            def step(kind, a, b):
                if kind == "inputs":
                    inputs()
                elif kind == "smalls":
                    smalls()
                elif kind == "decays":
                    decays()
                elif kind == "qkv":
                    qkv(a)
                elif kind == "z":
                    z(a)
                elif kind == "keys":
                    keys(a, b)
                elif kind == "grams":
                    grams(a, b)
                elif kind == "betas":
                    betas(a, b)
                elif kind == "flipped":
                    inverse_transposed(a, b)
                elif kind == "targets":
                    targets(a, b)
                elif kind == "masked":
                    masked(a, b)
                elif kind == "doubled":
                    doubled(a, b)
                elif kind == "values":
                    values(a)
                elif kind == "carried":
                    carried(a)
                elif kind == "summed":
                    summed(a, b)
                elif kind == "gated":
                    gated(a, b)
                elif kind == "begun":
                    half_mixed(a, b, 0)
                    if a + b:
                        half_mixed(a, b, 1)
                elif kind == "finished":
                    half_mixed(a, b, 1)
                elif kind == "subkeys":
                    subkeys(a)
                elif kind == "mixed":
                    mixed(a, b)
                elif kind == "scores":
                    scores(a, b)
                elif kind == "x2":
                    x2(a)
                elif kind == "slice":
                    kv_slice(a, *b)
                elif kind == "turned":
                    turned(a, *b)
                elif kind == "score":
                    score(a, *b)
                elif kind == "pturn":
                    pturn(a, *b)
                elif kind == "weigh":
                    weigh(a, *b)
                elif kind == "heads":
                    heads(a, b)

            def add_rows(g, h, j, slots, first=False, last=False):
                head = HEADS * g + h
                if first and g:
                    eng.wait_ge(sums_taken, g)
                for i, slot in enumerate(PE_SLOTS):
                    if slot not in slots:
                        continue
                    eng.wait_ge(diag_ready, PE_N * (2 * head + j) + i + 1)
                    eng.wait_ge(landed[slot], 16 * (4 * head + 2 + j + 1))
                    for c in range(2):
                        ins = eng.matmul(banks[:, c * SLICE:(c + 1) * SLICE], lhsT=diag[:, i * P:(i + 1) * P],
                                         rhs=ring[:, slot * D + c * SLICE:slot * D + (c + 1) * SLICE],
                                         start=first and i == 0, stop=last and i == PE_N - 1)
                    ins.then_inc(pe_used, 1)

            for st in opening_steps():
                step(*st)
            for n in (1, 3):
                eng.wait_ge(*ps.taken("z", n))
            for g in range(4):
                placed = gather_steps(g)
                alone = blocks_alone(g, placed)
                for i in range(2 * alone):
                    ahead = 0
                    while ahead < len(placed[i]) and placed[i][ahead][0] in AHEAD:
                        step(*placed[i][ahead])
                        ahead += 1
                    b = i // 2
                    if b % 4 >= 2:
                        add_rows(g, b // 4, b % 4 - 2, HALVES[i % 2], first=i == 4, last=i == 2 * BLOCKS - 1)
                    for st in placed[i][ahead:]:
                        step(*st)
                if alone < BLOCKS:
                    with eng.Fori(alone // 4, HEADS - 1) as h:
                        for j in range(2):
                            add_rows(g, h, j, range(RING))
                    for j in range(2):
                        add_rows(g, HEADS - 1, j, range(RING), last=j == 1)

        @block.scalar
        def _(eng):
            did = Steps(eng, act)
            rs_n = [0]

            def copy_out(key, out, in_=None, func=ACT.Copy):
                eng.wait_ge(*ps.full(*key))
                eng.activation(out, ps.bank(*key) if in_ is None else in_, func).then_inc(ps.sem_taken(*key), 1)

            def x_out(key, t):
                for n in range(2):
                    out = xT[:, :].rearrange("p (k n) -> p k n", k=KB)[:, 4 * n:4 * n + 4, t * P:(t + 1) * P]
                    copy_out(key + (n,), out, heads4(ps.bank(*key, n)))

            def rsqrt_start(n):
                rs_n[0] += 1
                eng.wait_ge(rs_asked, rs_n[0])
                did(eng.activation(rs_y[:, 0:n], rs_in[:, 0:n], ACT.Ln))
                did.wait()
                eng.activation(rs_y[:, 0:n], rs_y[:, 0:n], ACT.Exp, scale=-0.5).then_inc(rs_said, 1)

            def keys(t, f):
                copy_out(("kt", t, f), half(MT, f), func=ACT.Square)
                copy_out(("qt", t, f), half(AT, f), func=ACT.Square)
                eng.wait_ge(dec_in, 2 * t + f + 1)
                eng.activation(half(dec, f), half(dec, f), ACT.Exp).then_inc(dec_out, 1)

            def scaled(t, f):
                rsqrt_start(8)

            def summed(t, f):
                if t:
                    eng.wait_ge(od_sum, f + 1)
                else:
                    eng.wait_ge(*ps.taken("o", t, f))
                eng.activation(half(Ybuf, f), half(od, f), ACT.Square).then_inc(sq_o, 1)

            def gated(t, f):
                if f == 0:
                    rsqrt_start(HEADS)
                copy_out(("oT", t, f), half(oT, f))
                if f and not t:
                    for i in range(2):
                        copy_out(("S", t, i), half(S1, i))

            def mixed(layer, t):
                x_out(("x1T", layer, t), t)

            def inverse_out(t, s):
                for f in range(2):
                    copy_out(("T", t, s, f), half(Tm, f))

            def silu(n):
                eng.wait_ge(sil_in, n + 1)
                first = qkv_blocks(n)[0]
                pair = qkvT[:, first * SEQ:(first + 2) * SEQ]
                eng.activation(pair, pair, ACT.Silu).then_inc(sil_out, 1)

            def qkv(n):
                if n == 0:
                    eng.wait_ge(zero_ok, 1)
                if n >= 2:
                    eng.wait_ge(sil_in, n - 1)
                copy_out(("qkv", n), conv_rows(n)[:, :, CONV - 1:],
                         ps.bank("qkv", n).rearrange("p (b k) -> p b k", b=2))
                if n:
                    silu(n - 1)

            def z(n):
                if n == 0:
                    silu(11)
                s, t = n // 2, n % 2
                copy_out(("z", n), zs[:, t * D + s * SLICE:t * D + (s + 1) * SLICE], func=ACT.Silu)

            def scores(g, n):
                at = (n % 2) * SLICE
                copy_out(("query", g, n), qhT[:, at:at + SLICE])
                if g:
                    eng.wait_ge(idx_ready, HEADS * (g - 1) + 2 * n + 2)
                copy_out(("sc", g, n), sc[:, n * SLICE:(n + 1) * SLICE])

            def gates(g, n):
                first, count = chosen(n)
                eng.wait_ge(gx_in, HEADS * g + first + count)
                at = (g % 2) * P + first * TOPK
                eng.activation(gate[:, at:at + count * TOPK], best[:, first * TOPK:(first + count) * TOPK],
                               ACT.Exp).then_inc(gx_out, count)

            def kv_slice(t, f, n):
                key = ("kvq", t, f, n)
                if n // 3 == 1:
                    copy_out(key, v_heads(t, t, f, n - 3, 0, HALF))
                else:
                    turn = kq_turn(n)
                    if turn >= 2:
                        before = turn - 2
                        eng.wait_ge(*ps.full("kqT", t, f, before if before < 3 else before + 3))
                    copy_out(key, kq_slot(n))

            def turned(t, f, n):
                out = k_heads(t, t, f, n, 0, HALF) if n < 3 else qT[:, (n - 6) * HALF * P:(n - 5) * HALF * P]
                copy_out(("kqT", t, f, n), out)

            def soft(t, f, h):
                n = (t * 2 + f) * HALF + h
                wide = GROUPS * (t + 1) * P
                eng.wait_ge(nmx, n + 1)
                m = mx_of(n)
                eng.activation(prob[:, 0:wide], prob[:, 0:wide], ACT.Exp, bias=m[:, 1:2], scale=SCALE,
                               accum_out=m[:, 2:3]).then_inc(p_done, 1)

            def pturn(t, f, h):
                n = (t * 2 + f) * HALF + h
                wide = GROUPS * (t + 1) * P
                if n:
                    eng.wait_ge(*ps.full("pv", *((t, f, h - 1) if h else ((t, f - 1, HALF - 1) if f
                                                                         else (t - 1, 1, HALF - 1)))))
                copy_out(("pT", t, f, h), probT[:, 0:wide], banks[:, 4 * SLICE:4 * SLICE + wide])

            def step(kind, a, b):
                if kind in SPLIT:
                    return
                kind = kind.removeprefix("after_")
                if kind == "keys":
                    keys(a, b)
                elif kind == "scaled":
                    scaled(a, b)
                elif kind == "betas":
                    copy_out(("kbT", a, b), half(kbT, b))
                elif kind == "targets":
                    copy_out(("vn", a, b), half(vn, b))
                elif kind == "summed":
                    summed(a, b)
                elif kind == "gated":
                    gated(a, b)
                elif kind == "subkeys":
                    for i in range(4):
                        copy_out(("skT", a // 2, i), skT[:, 4 * i * P:(4 * i + 4) * P])
                elif kind == "normed":
                    rsqrt_start(1)
                elif kind == "mixed":
                    mixed(a, b)
                elif kind == "flipped":
                    inverse_out(a, b)
                elif kind == "inputs":
                    inputs()
                elif kind == "smalls":
                    smalls()
                elif kind == "decays":
                    decays()
                elif kind == "qkv":
                    qkv(a)
                elif kind == "z":
                    z(a)
                elif kind == "scores":
                    scores(a, b)
                elif kind == "gates":
                    gates(a, b)
                elif kind == "x2":
                    x_out(("x2T", a), a)
                elif kind == "slice":
                    kv_slice(a, *b)
                elif kind == "turned":
                    turned(a, *b)
                elif kind == "soft":
                    soft(a, *b)
                elif kind == "pturn":
                    pturn(a, *b)
                elif kind == "heads":
                    copy_out(("aoT", a, b), half(oaT, b))

            def rows(g, h, b):
                head = HEADS * g + h
                if b < 2:
                    eng.wait_ge(ring_used, vector_rows(head, b + 1))
                    eng.activation(gel[:, b * RING:(b + 1) * RING], dots[:, b * RING:(b + 1) * RING],
                                   ACT.Gelu).then_inc(gelu_done, 1)
                    return
                eng.wait_ge(wts_ready, 2 * head + b - 1)
                for i, slot in enumerate(PE_SLOTS):
                    eng.wait_ge(pe_used, tensor_rows(head, b - 3) + i + 1)
                    c = (b - 2) * RING + slot
                    eng.activation(diag[:, i * P:(i + 1) * P], ident, ACT.Copy, scale=wts[:, c:c + 1])\
                       .then_inc(diag_ready, 1)

            def inputs():
                for t in range(TILES):
                    x_out(("x0T", t), t)

            def smalls():
                copy_out(("convw",), cw[:, :], ps.bank("convw")[:, 0:24 * CONV])
                eng.wait_ge(sm_in, 1)
                did(eng.activation(gtmp[:, 16:32], gtmp[:, 16:32], ACT.Exp))
                eng.activation(gtmp[:, 32:48], gtmp[:, 32:48], ACT.Exp, scale=-1.0)
                eng.activation(alog[:, :], alog[:, :], ACT.Exp)
                did.wait()
                eng.activation(gtmp[:, 16:32], gtmp[:, 16:32], ACT.Ln, bias=1.0).then_inc(sm_out, 1)

            def decays():
                eng.wait_ge(*ps.taken("gcum"))
                eng.activation(egc[:, :], gcum[:, :], ACT.Exp).then_inc(sm_out, 1)

            for st in opening_steps():
                step(*st)
            for g in range(4):
                placed = gather_steps(g)
                alone = blocks_alone(g, placed)
                for b in range(alone):
                    if b % 4 >= 2:
                        rows(g, b // 4, b % 4)
                    for st in placed[2 * b]:
                        step(*st)
                    if b % 4 < 2:
                        rows(g, b // 4, b % 4)
                    for st in placed[2 * b + 1]:
                        step(*st)
                if alone < BLOCKS:
                    with eng.Fori(alone // 4, HEADS) as h:
                        for b in range(4):
                            rows(g, h, b)
                rsqrt_start(1)

        @block.vector
        def _(eng):
            did = Steps(eng, vec)
            rs_n = [0]
            norm_n = [0]

            def tt(out, a, b, op):
                return eng.tensor_tensor(out, a, b, op)

            def rsqrt(source, n, out, scale, eps):
                rs_n[0] += 1
                eng.tensor_scalar(rs_in[:, 0:n], source, scale, eps, ALU.mult, ALU.add).then_inc(rs_asked, 1)
                eng.wait_ge(rs_said, rs_n[0])
                did(tt(rs_t[:, 0:n], rs_y[:, 0:n], rs_y[:, 0:n], ALU.mult))
                did.wait()
                did(tt(rs_t[:, 0:n], rs_t[:, 0:n], rs_in[:, 0:n], ALU.mult))
                did.wait()
                did(eng.tensor_scalar(rs_t[:, 0:n], rs_t[:, 0:n], -0.5, 1.5, ALU.mult, ALU.add))
                did.wait()
                did(tt(out, rs_y[:, 0:n], rs_t[:, 0:n], ALU.mult))
                did.wait()

            def keys(t, f):
                cols = slice(t * HEADS + f * HALF, t * HEADS + (f + 1) * HALF)
                eng.wait_ge(*ps.full("gB", t, f))
                tt(heads4(half(dec, f)), heads4(ps.bank("gB", t, f)), spread(gcum[:, cols]),
                   ALU.subtract).then_inc(ps.sem_taken("gB", t, f), 1)
                eng.wait_ge(*ps.taken("gB", t, f))
                tt(heads4(half(dec, f)), heads4(half(dec, f)), negmask.unsqueeze(1).to_broadcast([P, HALF, P]),
                   ALU.add).then_inc(dec_in, 1)

            def values(t):
                for f in range(2):
                    cols = slice(t * HEADS + f * HALF, t * HEADS + (f + 1) * HALF)
                    eng.wait_ge(*ps.full("vt", t, f))
                    tt(heads4(half(vb, f)), heads4(ps.bank("vt", t, f)), spread(beta[:, cols]),
                       ALU.mult).then_inc(ps.sem_taken("vt", t, f), 1)
                for n in (t, 2 + t):
                    eng.wait_ge(*ps.taken("z", n))
                z3 = zs[:, t * D:(t + 1) * D].rearrange("p (h d) -> p h d", h=HEADS)
                did(tt(z3, z3, normw[:, :].unsqueeze(1).to_broadcast([P, HEADS, P]), ALU.mult))

            def scaled(t, f):
                cols = slice(t * HEADS + f * HALF, t * HEADS + (f + 1) * HALF)
                hs = slice(f * HALF, (f + 1) * HALF)
                eng.wait_ge(*ps.taken("qt", t, f))
                r = rqk[:, 8 * f:8 * f + 8]
                did(eng.tensor_reduce(ss[:, 8 * f:8 * f + HALF], heads4(half(AT, f)), AX_X, ALU.add))
                did(eng.tensor_reduce(ss[:, 8 * f + HALF:8 * f + 8], heads4(half(MT, f)), AX_X, ALU.add))
                did.wait()
                rsqrt(ss[:, 8 * f:8 * f + 8], 8, r, 1.0, NORM_EPS)
                rq, rk = r[:, 0:HALF], r[:, HALF:8]
                did(tt(coef[:, hs], rk, beta[:, cols], ALU.mult))
                did(eng.tensor_scalar(c_query[:, hs], rq, SCALE, None, ALU.mult))
                eng.wait_ge(dec_out, 2 * t + f + 1)
                did(tt(heads4(half(dec, f)), heads4(half(dec, f)), spread(rk), ALU.mult))
                did.wait()
                if t:
                    did(tt(c_state[:, hs], coef[:, hs], egc[:, cols], ALU.mult))
                    did(tt(c_carry[:, hs], c_query[:, hs], egc[:, cols], ALU.mult))
                ins = tt(heads4(half(kb, f)), heads4(ps.bank("kt", t, f)), spread(coef[:, hs]), ALU.mult)
                if not t:
                    ins = tt(heads4(half(kS, f)), heads4(ps.bank("kt", t, f)),
                             heads4(half(dec, f))[:, :, P - 1:P].to_broadcast([P, HALF, P]), ALU.mult)
                ins.then_inc(ps.sem_taken("kt", t, f), 1)

            def grams(t, f):
                for key, out in (("A", AT), ("M", MT)):
                    eng.wait_ge(*ps.full(key, t, f))
                    tt(half(out, f), ps.bank(key, t, f), half(dec, f), ALU.mult)\
                        .then_inc(ps.sem_taken(key, t, f), 1)

            def started(t):
                first = consts[:, C_LVL:C_LVL + P].unsqueeze(1).to_broadcast([P, HALF, P])
                for f in range(2):
                    eng.wait_ge(*ps.taken("M", t, f))
                    did(tt(heads4(half(TT, f)), heads4(half(MT, f)), first, ALU.mult))
                did.wait()
                for f in range(2):
                    tt(heads4(half(TT, f)), heads4(half(TT, f)), ident.unsqueeze(1).to_broadcast([P, HALF, P]),
                       ALU.add).then_inc(tt_ready, 1)

            def masked(t, s):
                level = consts[:, C_LVL + s * P:C_LVL + (s + 1) * P]
                for f in range(2):
                    eng.wait_ge(*ps.full("Y", t, s, f))
                    tt(heads4(half(Ybuf, f)), heads4(ps.bank("Y", t, s, f)),
                       level.unsqueeze(1).to_broadcast([P, HALF, P]), ALU.mult)\
                        .then_inc(ps.sem_taken("Y", t, s, f), 1)

            def doubled(t, s):
                for f in range(2):
                    eng.wait_ge(*ps.full("ZT", t, s, f))
                    tt(half(TT, f), half(TT, f), ps.bank("ZT", t, s, f), ALU.add)\
                        .then_inc(ps.sem_taken("ZT", t, s, f), 1)

            def carried(t):
                for f in range(2):
                    hs = slice(f * HALF, (f + 1) * HALF)
                    eng.wait_ge(*ps.full("kS", t, f))
                    tt(heads4(half(Ybuf, f)), heads4(ps.bank("kS", t, f)), spread(c_state[:, hs]), ALU.mult)\
                        .then_inc(ps.sem_taken("kS", t, f), 1)
                    eng.wait_ge(*ps.taken("kS", t, f))
                    tt(half(vb, f), half(vb, f), half(Ybuf, f), ALU.subtract).then_inc(vb_ready, 1)
                    eng.wait_ge(*ps.full("qS", t, f))
                    tt(heads4(half(MT, f)), heads4(ps.bank("qS", t, f)), spread(c_carry[:, hs]), ALU.mult)\
                        .then_inc(ps.sem_taken("qS", t, f), 1)

            def summed(t, f):
                hs = slice(f * HALF, (f + 1) * HALF)
                eng.wait_ge(*ps.full("o", t, f))
                tt(heads4(half(od, f)), heads4(ps.bank("o", t, f)), spread(c_query[:, hs]), ALU.mult)\
                    .then_inc(ps.sem_taken("o", t, f), 1)
                if t:
                    eng.wait_ge(*ps.taken("o", t, f))
                    eng.wait_ge(*ps.taken("qS", t, f))
                    tt(half(od, f), half(od, f), half(MT, f), ALU.add).then_inc(od_sum, 1)

            def gated(t, f):
                if f == 0:
                    for i in range(2):
                        eng.wait_ge(sq_o, 2 * t + i + 1)
                        did(eng.tensor_reduce(ss[:, HALF * i:HALF * (i + 1)], heads4(half(Ybuf, i)), AX_X, ALU.add))
                    did.wait()
                    rsqrt(ss[:, 0:HEADS], HEADS, rqk[:, 0:HEADS], 1.0 / P, NORM_EPS)
                did(tt(heads4(half(od, f)), heads4(half(od, f)), spread(rqk[:, f * HALF:(f + 1) * HALF]), ALU.mult))
                did.wait()
                tt(half(od, f), half(od, f), half(zs[:, t * D:(t + 1) * D], f), ALU.mult).then_inc(od_ready, 1)

            def layer_norm(t):
                xt = xtile(t)
                i = norm_n[0]
                norm_n[0] += 1
                for s in range(2):
                    did(eng.bn_stats(bn[:, 6 * s:6 * s + 6], xt[:, s * SLICE:(s + 1) * SLICE]))
                did.wait()
                did(eng.bn_aggr(mv[:, :], bn[:, :].rearrange("p (s c) -> p s c", s=2)))
                did.wait()
                rsqrt(mv[:, 1:2], 1, rs_t[:, 8:9], 1.0, LN_EPS)
                did(eng.tensor_scalar(xt, xt, mv[:, 0:1], rs_t[:, 8:9], ALU.subtract, ALU.mult))
                did.wait()
                eng.wait_ge(gb_land, 32 * (i + 1))
                did(tt(xt, xt, gb[:, 0:D], ALU.mult))
                did.wait()
                tt(xt, xt, gb[:, D:2 * D], ALU.add).then_inc(x_ready, 1)

            def normed(layer, t):
                for s in range(2):
                    eng.wait_ge(*ps.full("mix", layer, t, s))
                    xs = xtile(t)[:, s * SLICE:(s + 1) * SLICE]
                    eng.scalar_tensor_tensor(xs, xs, ALPHA, ps.bank("mix", layer, t, s), ALU.mult, ALU.add)\
                        .then_inc(ps.sem_taken("mix", layer, t, s), 1)
                for s in range(2):
                    eng.wait_ge(*ps.taken("mix", layer, t, s))
                layer_norm(t)

            def top16(rows):
                for row, v, _ in rows:
                    did(eng.max(v[:, 0:8], row))
                did.wait()
                for row, v, p in rows:
                    did(eng.max_index(p[:, 0:8], v[:, 0:8], row))
                did.wait()
                for row, v, _ in rows:
                    did(eng.match_replace(row, v[:, 0:8], row, -3.0e38))
                did.wait()
                for row, v, _ in rows:
                    did(eng.max(v[:, 8:16], row))
                did.wait()
                for row, v, p in rows:
                    did(eng.max_index(p[:, 8:16], v[:, 8:16], row))
                did.wait()

            def top(g, n):
                first, count = chosen(n)
                eng.wait_ge(*ps.taken("sc", g, first // 2))
                top16([(sc[:, i * P:(i + 1) * P], topv[:, i * TOPK:(i + 1) * TOPK], topi[:, i * TOPK:(i + 1) * TOPK])
                       for i in range(2 * first, 2 * (first + count))])

            def best_of(g, n):
                first, count = chosen(n)
                mine = slice(2 * first * TOPK, 2 * (first + count) * TOPK)
                did(eng.tensor_copy(topf[:, mine], topi[:, mine]))
                tv = topv[:, mine].rearrange("p (h c k) -> p h c k", h=count, c=2)
                four = [P, count, TOPK, TOPK]
                wide = TOPK * TOPK
                did(tt(cand[:, 0:count * wide].rearrange("p (h i j) -> p h i j", h=count, i=TOPK),
                       tv[:, :, 0, :].unsqueeze(3).to_broadcast(four),
                       tv[:, :, 1, :].unsqueeze(2).to_broadcast(four), ALU.add))
                did.wait()
                top16([(cand[:, i * wide:(i + 1) * wide], best[:, (first + i) * TOPK:(first + i + 1) * TOPK],
                        pos[:, (first + i) * TOPK:(first + i + 1) * TOPK]) for i in range(count)])

            def gates(g, n):
                first, count = chosen(n)
                k = count * TOPK
                mine = slice(first * TOPK, first * TOPK + k)
                hs, hs2 = slice(first, first + count), slice(HEADS + first, HEADS + first + count)
                at = (g % 2) * P + first * TOPK
                gt = gate[:, at:at + k].rearrange("p (h k) -> p h k", h=count)
                b3 = best[:, mine].rearrange("p (h k) -> p h k", h=count)
                did(eng.tensor_copy(gden[:, hs].unsqueeze(2), b3[:, :, 0:1]))
                did(eng.tensor_scalar(posc[:, 0:k], pos[:, mine], 4, None, ALU.logical_shift_right))
                did(eng.tensor_scalar(posc[:, k:2 * k], pos[:, mine], 15, None, ALU.bitwise_and))
                did.wait()
                tt(b3, b3, spread(gden[:, hs], TOPK), ALU.subtract).then_inc(gx_in, count)
                did(eng.tensor_copy(posf[:, 0:2 * k], posc[:, 0:2 * k]))
                eng.wait_ge(gx_out, HEADS * g + first + count)
                did(eng.tensor_reduce(gden[:, hs], gt, AX_X, ALU.add))
                did.wait()
                did(eng.reciprocal(gden[:, hs2], gden[:, hs]))
                did.wait()
                did(tt(gt, gt, spread(gden[:, hs2], TOPK), ALU.mult))
                did.wait()

            def experts(g, n):
                first, count = chosen(n)
                k = count * TOPK
                hot4 = hot[:, 0:k * TOPK].rearrange("p (h k i) -> p h k i", h=count, k=TOPK)
                four = [P, count, TOPK, TOPK]
                for c in range(2):
                    place = posf[:, c * k:(c + 1) * k].rearrange("p (h k) -> p h k", h=count)
                    names = topf[:, 2 * first * TOPK:2 * (first + count) * TOPK]\
                        .rearrange("p (h c k) -> p h c k", h=count, c=2)[:, :, c, :]
                    did(tt(hot4, place.unsqueeze(3).to_broadcast(four),
                           iota16.unsqueeze(1).unsqueeze(1).to_broadcast(four), ALU.is_equal))
                    did.wait()
                    did(tt(hot4, hot4, names.unsqueeze(2).to_broadcast(four), ALU.mult))
                    did.wait()
                    did(eng.tensor_reduce(expert[:, c * k:(c + 1) * k]
                                          .rearrange("p (h k) -> p h k", h=count), hot4, AX_X, ALU.add))
                    did.wait()
                at = (g % 2) * P + first * TOPK
                eng.scalar_tensor_tensor(idx[:, at:at + k], expert[:, 0:k], float(P), expert[:, k:2 * k],
                                         ALU.mult, ALU.add).then_inc(idx_ready, count)

            def rotated(t, f, n):
                eng.wait_ge(*ps.taken("kvq", t, f, n))
                if t or f or n:
                    eng.wait_ge(roped, (t * 2 + f) * 6 + kq_turn(n))
                rot = heads4(kq_slot(n))[:, :, 0:32]
                halves = rot.rearrange("p h (a c) -> p h a c", a=2)
                four = [P, HALF, 2, 16]
                table = [consts[:, C_ROPE + (t * 2 + i) * 16:C_ROPE + (t * 2 + i + 1) * 16]
                         .unsqueeze(1).unsqueeze(1).to_broadcast(four) for i in range(2)]
                cos_part = rope[:, 0:P].rearrange("p (h a c) -> p h a c", h=HALF, a=2)
                sin_part = rope[:, P:2 * P].rearrange("p (h a c) -> p h a c", h=HALF, a=2)
                did(tt(cos_part, halves, table[0], ALU.mult))
                did(tt(sin_part, halves, table[1], ALU.mult))
                did.wait()
                did(tt(halves[:, :, 0, :], cos_part[:, :, 0, :], sin_part[:, :, 1, :], ALU.subtract))
                tt(halves[:, :, 1, :], cos_part[:, :, 1, :], sin_part[:, :, 0, :], ALU.add).then_inc(roped, 1)

            def soft(t, f, h):
                n = (t * 2 + f) * HALF + h
                wide = (t + 1) * P
                m = mx_of(n)
                if n:
                    before = (t, f, h - 1) if h else ((t, f - 1, HALF - 1) if f else (t - 1, 1, HALF - 1))
                    eng.wait_ge(*ps.full("pT", *before))
                eng.wait_ge(*ps.full("score", t, f, h))
                scored = banks[:, 2 * SLICE:2 * SLICE + GROUPS * wide].rearrange("p (g k) -> p g k", g=GROUPS)
                masked3 = prob[:, 0:GROUPS * wide].rearrange("p (g k) -> p g k", g=GROUPS)
                eng.tensor_tensor_reduce(masked3, scored, attmask[:, :, SEQ - wide:], 1.0, 2.0 * NEG,
                                         ALU.add, ALU.max, m[:, 0:1]).then_inc(ps.sem_taken("score", t, f, h), 1)
                eng.wait_ge(*ps.taken("score", t, f, h))
                eng.tensor_scalar(m[:, 1:2], m[:, 0:1], -SCALE, None, ALU.mult).then_inc(nmx, 1)

            def head_out(t, f, h):
                n = (t * 2 + f) * HALF + h
                m = mx_of(n)
                eng.wait_ge(p_done, n + 1)
                did(eng.reciprocal(m[:, 3:4], m[:, 2:3]))
                did.wait()
                if h == 0 and (t or f):
                    eng.wait_ge(*ps.full("aoT", *((t, 0) if f else (t - 1, 1))))
                eng.wait_ge(*ps.full("pv", t, f, h))
                eng.tensor_scalar(oh[:, h * P:(h + 1) * P], ps.bank("pv", t, f, h)[:, 0:P], m[:, 3:4], None,
                                  ALU.mult).then_inc(ps.sem_taken("pv", t, f, h), 1)

            def step(kind, a, b):
                if kind in SPLIT:
                    return
                kind = kind.removeprefix("after_")
                if kind == "keys":
                    keys(a, b)
                elif kind == "scaled":
                    scaled(a, b)
                elif kind == "grams":
                    grams(a, b)
                elif kind == "masked":
                    masked(a, b)
                elif kind == "doubled":
                    doubled(a, b)
                elif kind == "carried":
                    carried(a)
                elif kind == "summed":
                    summed(a, b)
                elif kind == "gated":
                    gated(a, b)
                elif kind == "normed":
                    normed(a, b)
                elif kind == "started":
                    started(a)
                elif kind == "values":
                    values(a)
                elif kind == "smalls":
                    smalls()
                elif kind == "decays":
                    decays()
                elif kind == "qkv":
                    convolve(a)
                elif kind == "top":
                    top(a, b)
                elif kind == "best":
                    best_of(a, b)
                elif kind == "gates":
                    gates(a, b)
                elif kind == "experts":
                    experts(a, b)
                elif kind == "rotated":
                    rotated(a, *b)
                elif kind == "soft":
                    soft(a, *b)
                elif kind == "out":
                    head_out(a, *b)

            def row(slot):
                return ring[:, slot * D:(slot + 1) * D]

            def dot_rows(g, h, j, slots):
                for s in slots:
                    eng.wait_ge(landed[s], 16 * (4 * (HEADS * g + h) + j + 1))
                    c = j * RING + s
                    eng.tensor_tensor_reduce(row(s), row(s), xtile(g % 2), 1.0, 0.0, ALU.mult, ALU.add,
                                             dots[:, c:c + 1]).then_inc(ring_used, 1)

            def weigh_rows(g, h, j):
                head = HEADS * g + h
                turn = 2 * head + j + 1
                cols = slice(j * RING, (j + 1) * RING)
                eng.wait_ge(gelu_done, turn)
                if not (isinstance(h, int) and head == 0):
                    eng.wait_ge(diag_ready, PE_N * (turn - 2))
                gates_of = (g % 2) * P + h * TOPK + j * RING
                tt(wts[:, cols], gel[:, cols], gate[:, bass.ds(gates_of, RING)], ALU.mult).then_inc(wts_ready, 1)
                eng.wait_ge(wts_ready, turn)

            def add_rows(g, h, j, slots, first=False):
                head = HEADS * g + h
                for i, s in enumerate(VE_SLOTS):
                    if s not in slots:
                        continue
                    eng.wait_ge(landed[s], 16 * (4 * head + 2 + j + 1))
                    eng.wait_ge(ring_used, vector_rows(head, 2 + j) + i - 1)
                    a = acc[:, (i % 2) * D:(i % 2 + 1) * D]
                    c = j * RING + s
                    if first and i == 1:
                        ins = eng.tensor_scalar(a, row(s), wts[:, c:c + 1], None, ALU.mult)
                    else:
                        ins = eng.scalar_tensor_tensor(a, row(s), wts[:, c:c + 1], a, ALU.mult, ALU.add)
                    ins.then_inc(ring_used, 1)

            for n in range(2):
                did(eng.memset(conv_rows(n)[:, :, 0:CONV - 1], 0.0))
            did.wait()
            eng.memset(gden[:, :], 0.0).then_inc(zero_ok, 1)
            eng.wait_ge(zero_ok, 1)
            eng.memset(gden[:, :], 0.0).then_inc(ring_used, VE_N)
            eng.wait_ge(ring_used, VE_N)
            eng.memset(gden[:, :], 0.0).then_inc(pe_used, PE_N)

            def convolve(n):
                eng.wait_ge(*ps.taken("qkv", n))
                if n == 0:
                    eng.wait_ge(*ps.taken("convw"))
                for j in range(CONV - 1, -1, -1):
                    for b, blk in enumerate(qkv_blocks(n)):
                        out = qkvT[:, blk * SEQ:(blk + 1) * SEQ]
                        src = conv_rows(n)[:, b, j:j + SEQ]
                        w = cw[:, j * 24 + blk:j * 24 + blk + 1]
                        if j == CONV - 1:
                            did(eng.tensor_scalar(out, src, w, None, ALU.mult))
                        else:
                            ins = eng.scalar_tensor_tensor(out, src, w, out, ALU.mult, ALU.add)
                            if j == 0 and b == 1:
                                ins.then_inc(sil_in, 1)
                            else:
                                did(ins)
                    if j:
                        did.wait()

            def smalls():
                eng.wait_ge(*ps.full("ab"))
                eng.tensor_copy(ab[:, :], ps.bank("ab")[:, 0:TILES * 16]).then_inc(ps.sem_taken("ab"), 1)
                eng.wait_ge(*ps.taken("ab"))
                ab3 = ab[:, :].rearrange("p (t c) -> p t c", t=TILES)
                small = [gtmp[:, 16 * i:16 * i + 16] for i in range(3)]
                u3 = small[0].rearrange("p (t h) -> p t h", t=TILES)
                did(tt(u3, ab3[:, :, 0:HEADS], dtb[:, :].unsqueeze(1).to_broadcast([P, TILES, HEADS]), ALU.add))
                did(eng.tensor_copy(small[2].rearrange("p (t h) -> p t h", t=TILES), ab3[:, :, HEADS:16]))
                did.wait()
                did(eng.tensor_scalar(small[1], small[0], -1.0, None, ALU.mult))
                did.wait()
                tt(small[1], small[0], small[1], ALU.min).then_inc(sm_in, 1)
                did(eng.tensor_scalar(small[0], small[0], 0.0, None, ALU.max))
                did.wait()
                eng.wait_ge(sm_out, 1)
                did(tt(small[0], small[0], small[1], ALU.add))
                did(eng.tensor_scalar(small[2], small[2], 1.0, None, ALU.add))
                did.wait()
                did(eng.scalar_tensor_tensor(u3, u3, -1.0, alog[:, :].unsqueeze(1).to_broadcast([P, TILES, HEADS]),
                                             ALU.mult, ALU.mult))
                did(eng.reciprocal(beta[:, :], small[2]))
                did.wait()
                eng.tensor_copy(glog[:, :], small[0]).then_inc(g_ready, 1)

            def decays():
                eng.wait_ge(*ps.full("gcum"))
                eng.tensor_copy(gcum[:, :], ps.bank("gcum")[:, 0:TILES * HEADS]).then_inc(ps.sem_taken("gcum"), 1)
                eng.wait_ge(*ps.taken("gcum"))
                eng.wait_ge(sm_out, 2)

            for st in opening_steps():
                step(*st)
            for g in range(4):
                xt = xtile(g % 2)
                did(eng.tensor_scalar(acc[:, 0:D], xt, ALPHA, None, ALU.mult))
                did.wait()
                placed = gather_steps(g)
                alone = blocks_alone(g, placed)
                for i in range(2 * alone):
                    h, b = divmod(i // 2, 4)
                    if b < 2:
                        dot_rows(g, h, b, HALVES[i % 2])
                    else:
                        if i % 2 == 0:
                            weigh_rows(g, h, b - 2)
                        add_rows(g, h, b - 2, HALVES[i % 2], first=i == 4)
                    for st in placed[i]:
                        step(*st)
                if alone < BLOCKS:
                    with eng.Fori(alone // 4, HEADS) as h:
                        for j in range(2):
                            dot_rows(g, h, j, range(RING))
                        for j in range(2):
                            weigh_rows(g, h, j)
                            add_rows(g, h, j, range(RING))
                eng.wait_ge(ring_used, vector_rows(HEADS * (g + 1), 0))
                did(tt(acc[:, 0:D], acc[:, 0:D], acc[:, D:2 * D], ALU.add))
                did.wait()
                eng.wait_ge(pe_used, tensor_rows(HEADS * (g + 1), 0))
                tt(xt, acc[:, 0:D], banks[:, 0:D], ALU.add).then_inc(sums_taken, 1)
                eng.wait_ge(sums_taken, g + 1)
                layer_norm(g % 2)


def constants():
    import numpy as np

    c = np.zeros((P, C_ALL), np.float32)
    i, j = np.arange(P)[:, None], np.arange(P)[None, :]
    c[:, C_ID:C_ID + P] = i == j
    c[:, C_TRI:C_TRI + P] = i <= j
    c[:, C_NEG:C_NEG + P] = np.where(j >= i, 0.0, NEG)
    for s in range(LEVELS):
        w = 1 << s
        low_left = (i // (2 * w) == j // (2 * w)) & (i % (2 * w) >= w) & (j % (2 * w) < w)
        if s == 0:
            low_left = low_left.T
        c[:, C_LVL + s * P:C_LVL + (s + 1) * P] = -1.0 * low_left
    rel = P + i - np.arange(SEQ)[None, :]
    for g, (window, dilation) in enumerate(((128, 1), (512, 4), (2048, 16))):
        ok = (rel >= 0) & (rel % dilation == 0) & (rel <= window)
        c[:, C_ATT + g * SEQ:C_ATT + (g + 1) * SEQ] = np.where(ok, 0.0, NEG)
    inv = np.float32(500000.0) ** (-np.arange(16, dtype=np.float32) * np.float32(2.0) / np.float32(32))
    for t in range(TILES):
        ang = (np.arange(P, dtype=np.float32) + t * P)[:, None] * inv.astype(np.float32)[None, :]
        c[:, C_ROPE + 32 * t:C_ROPE + 32 * t + 16] = np.cos(ang)
        c[:, C_ROPE + 32 * t + 16:C_ROPE + 32 * t + 32] = np.sin(ang)
    c[:, C_IOTA:C_IOTA + 16] = np.arange(16)[None, :]
    return c


def kernel(**inputs):
    import numpy as np
    import concourse.bacc as bacc
    from concourse.bass_utils import run_bass_kernel_spmd

    nc = bacc.Bacc("TRN2", target_bir_lowering=False, num_devices=1)
    shapes = {
        "x": (SEQ, D), "dn_w_in": (D, 4 * D + 16), "dn_conv": (CONV, 3 * D), "dn_a_log": (1, HEADS),
        "dn_dt_bias": (1, HEADS), "dn_norm_w": (1, P), "dn_w_out": (D, D), "shared_w_kv": (D, 6 * D),
        "attn_w_q": (D, 3 * D), "attn_w_out": (D, D), "peer_w_query": (2, D, 2 * D),
        "peer_sub_keys": (2, 16, P, P), "peer_u": (2 * P * P, D), "peer_v": (2 * P * P, D),
        "ln_mix_g": (2, D), "ln_mix_b": (2, D), "ln_ffn_g": (2, D), "ln_ffn_b": (2, D),
    }
    arrays, aps = {}, {}
    for name, shape in shapes.items():
        a = np.ascontiguousarray(inputs[name]).reshape(shape)
        parts = {name: a}
        if name in ("peer_u", "peer_v"):
            parts = {f"{name}_{i}": a[i * P * P:(i + 1) * P * P] for i in range(2)}
        for key, value in parts.items():
            arrays[key] = value
            aps[key] = nc.dram_tensor(key, value.shape, mybir.dt.from_np(value.dtype), kind="ExternalInput").ap()
    arrays["constants"] = constants()
    const_ap = nc.dram_tensor("constants", (P, C_ALL), F32, kind="ExternalInput").ap()
    out = nc.dram_tensor("out", (SEQ, D), F32, kind="ExternalOutput").ap()
    sub_keys = [aps["peer_sub_keys"][i].rearrange("s k d -> k s d") for i in range(2)]
    yoco_deltanet_dilated_peer(
        nc, aps["x"], aps["dn_w_in"], aps["dn_conv"], aps["dn_a_log"], aps["dn_dt_bias"], aps["dn_norm_w"],
        aps["dn_w_out"], aps["shared_w_kv"], aps["attn_w_q"], aps["attn_w_out"],
        [aps["peer_w_query"][i] for i in range(2)], sub_keys,
        [aps[f"peer_u_{i}"][:, :] for i in range(2)], [aps[f"peer_v_{i}"][:, :] for i in range(2)],
        aps["ln_mix_g"], aps["ln_mix_b"], aps["ln_ffn_g"], aps["ln_ffn_b"], const_ap, out)
    r = run_bass_kernel_spmd(nc, [arrays], core_ids=[0])
    return r.results[0]["out"].reshape(1, SEQ, D)
```
